# Optimizing a Trainium2 kernel written in Bass

```python
import math
import jax, jax.numpy as jnp
from jax import lax
import numpy as np

D_MODEL = 1024
BATCH = 1
SEQ = 512
DEPTH = 2

N_MIXERS = 3
POOL_WINDOWS = (2, 4, 8, 16)
POOL_GROUPS = len(POOL_WINDOWS)
POOL_CH = D_MODEL // POOL_GROUPS
HEAD_DIM = 64
N_Q_HEADS = D_MODEL // HEAD_DIM
N_KV_HEADS = 4
GQA_GROUP = N_Q_HEADS // N_KV_HEADS
WINDOW = 128
ATTN_BLOCK = WINDOW
ROPE_THETA = 10000.0
QKV_WIDTH = (N_Q_HEADS + 2 * N_KV_HEADS) * HEAD_DIM
CONV_WIDTH = 3
N_EXPERTS = 64
TOP_K = 8
N_EXPERT_GROUPS = 8
TOPK_GROUPS = 4
D_EXPERT = 256
D_SHARED = 256
ROUTED_SCALE = 2.5
MOE_BLOCK = 128
LN_EPS = 1e-5
DEEPNORM_ALPHA = (2 * DEPTH) ** 0.25
DEEPNORM_BETA = (8 * DEPTH) ** -0.25

kernel_name = "hybrid_pool_swa_conv_moe_deepnorm"

def _layer_norm(x, g, b):
    xf = x.astype(jnp.float32)
    mu = xf.mean(-1, keepdims=True)
    var = jnp.square(xf - mu).mean(-1, keepdims=True)
    y = (xf - mu) * lax.rsqrt(var + LN_EPS) * g.astype(jnp.float32) + b.astype(jnp.float32)
    return y.astype(x.dtype)

def _rope_tables(seq):
    pos = jnp.arange(seq, dtype=jnp.float32)
    inv_freq = ROPE_THETA ** (-jnp.arange(0, HEAD_DIM, 2, dtype=jnp.float32) / HEAD_DIM)
    ang = pos[:, None] * inv_freq[None, :]
    return jnp.cos(ang), jnp.sin(ang)

def _apply_rope(t, cos, sin):
    tf = t.astype(jnp.float32)
    t1, t2 = jnp.split(tf, 2, axis=-1)
    c = cos[None, :, None, :]
    s = sin[None, :, None, :]
    return jnp.concatenate([t1 * c - t2 * s, t2 * c + t1 * s], axis=-1).astype(t.dtype)

def _pool_mixer(x, w_grp, scale):
    bsz, seq, d = x.shape
    xg = x.astype(jnp.float32).reshape(bsz, seq, POOL_GROUPS, POOL_CH)
    csum = jnp.cumsum(xg, axis=1)
    pos = jnp.arange(seq)
    outs = []
    for g, w in enumerate(POOL_WINDOWS):
        cg = csum[:, :, g]
        shifted = jnp.pad(cg, ((0, 0), (w, 0), (0, 0)))[:, :seq]
        cnt = jnp.minimum(pos + 1, w).astype(jnp.float32)[None, :, None]
        outs.append((cg - shifted) / cnt - xg[:, :, g])
    pooled = jnp.stack(outs, axis=2).astype(x.dtype)
    y = jnp.einsum('bsgc,gcd->bsgd', pooled, w_grp).reshape(bsz, seq, d)
    return y * scale

def _swa_attention(x, wqkv, bqkv, sinks, wo, bo, cos, sin):
    bsz, seq, d = x.shape
    nb = seq // ATTN_BLOCK
    qkv = x @ wqkv + bqkv
    q, k, v = jnp.split(qkv, [N_Q_HEADS * HEAD_DIM, (N_Q_HEADS + N_KV_HEADS) * HEAD_DIM], axis=-1)
    q = _apply_rope(q.reshape(bsz, seq, N_Q_HEADS, HEAD_DIM), cos, sin) * (HEAD_DIM ** -0.5)
    k = _apply_rope(k.reshape(bsz, seq, N_KV_HEADS, HEAD_DIM), cos, sin)
    v = v.reshape(bsz, seq, N_KV_HEADS, HEAD_DIM)
    qb = q.reshape(bsz, nb, ATTN_BLOCK, N_KV_HEADS, GQA_GROUP, HEAD_DIM)
    kb = k.reshape(bsz, nb, ATTN_BLOCK, N_KV_HEADS, HEAD_DIM)
    vb = v.reshape(bsz, nb, ATTN_BLOCK, N_KV_HEADS, HEAD_DIM)
    kk = jnp.concatenate([jnp.concatenate([jnp.zeros_like(kb[:, :1]), kb[:, :-1]], axis=1), kb], axis=2)
    vv = jnp.concatenate([jnp.concatenate([jnp.zeros_like(vb[:, :1]), vb[:, :-1]], axis=1), vb], axis=2)
    s = jnp.einsum('bnqhgd,bnkhd->bnhgqk', qb, kk, preferred_element_type=jnp.float32)
    qi = jnp.arange(ATTN_BLOCK)[:, None]
    ki = jnp.arange(2 * ATTN_BLOCK)[None, :]
    band = (ki > qi) & (ki <= qi + ATTN_BLOCK)
    exists = (jnp.arange(nb)[:, None, None] > 0) | (ki >= ATTN_BLOCK)[None]
    valid = band[None] & exists
    s = jnp.where(valid[None, :, None, None], s, -jnp.inf)
    sink = sinks.astype(jnp.float32).reshape(N_KV_HEADS, GQA_GROUP)[None, None, :, :, None, None]
    m = jnp.maximum(s.max(-1, keepdims=True), sink)
    p = jnp.exp(s - m)
    p = p / (p.sum(-1, keepdims=True) + jnp.exp(sink - m))
    o = jnp.einsum('bnhgqk,bnkhd->bnqhgd', p.astype(vv.dtype), vv)
    o = o.reshape(bsz, seq, N_Q_HEADS * HEAD_DIM)
    return o @ wo + bo

def _gated_conv(x, w_in, conv_w, w_out):
    bsz, seq, d = x.shape
    proj = x @ w_in
    gb, gc, h = jnp.split(proj, 3, axis=-1)
    u = gc * h
    conv = lax.conv_general_dilated(u, conv_w[:, None, :], window_strides=(1,),
                                    padding=[(CONV_WIDTH - 1, 0)],
                                    dimension_numbers=('NWC', 'WIO', 'NWC'),
                                    feature_group_count=d)
    return (gb * conv) @ w_out

def _moe(x2, w_router, b_router, w1, w3, w2, ws1, ws3, ws2):
    t = x2.shape[0]
    scores = jax.nn.sigmoid(x2.astype(jnp.float32) @ w_router.astype(jnp.float32))
    sel = scores + b_router.astype(jnp.float32)
    grp = sel.reshape(t, N_EXPERT_GROUPS, N_EXPERTS // N_EXPERT_GROUPS)
    grp_score = lax.top_k(grp, 2)[0].sum(-1)
    grp_idx = lax.top_k(grp_score, TOPK_GROUPS)[1]
    grp_mask = (grp_idx[..., None] == jnp.arange(N_EXPERT_GROUPS)).any(1)
    exp_mask = jnp.repeat(grp_mask, N_EXPERTS // N_EXPERT_GROUPS, axis=1)
    exp_idx = lax.top_k(jnp.where(exp_mask, sel, -jnp.inf), TOP_K)[1]
    gate = jnp.take_along_axis(scores, exp_idx, axis=1)
    gate = gate / gate.sum(-1, keepdims=True) * ROUTED_SCALE

    n_assign = t * TOP_K
    flat_e = exp_idx.reshape(n_assign)
    flat_t = jnp.repeat(jnp.arange(t), TOP_K)
    flat_g = gate.reshape(n_assign).astype(x2.dtype)
    order = jnp.argsort(flat_e)
    se = flat_e[order]
    counts = jnp.bincount(flat_e, length=N_EXPERTS)
    padded = (counts + MOE_BLOCK - 1) // MOE_BLOCK * MOE_BLOCK
    start = jnp.cumsum(counts) - counts
    pend = jnp.cumsum(padded)
    pstart = pend - padded
    dest = pstart[se] + jnp.arange(n_assign) - start[se]
    n_blocks = (n_assign + N_EXPERTS * (MOE_BLOCK - 1) + MOE_BLOCK - 1) // MOE_BLOCK
    n_rows = n_blocks * MOE_BLOCK
    row_t = jnp.zeros((n_rows,), jnp.int32).at[dest].set(flat_t[order].astype(jnp.int32))
    row_g = jnp.zeros((n_rows,), x2.dtype).at[dest].set(flat_g[order])
    block_e = jnp.clip(jnp.searchsorted(pend, jnp.arange(n_blocks) * MOE_BLOCK, side='right'),
                       0, N_EXPERTS - 1)

    def expert_block(args):
        e, toks, gs = args
        xb = x2[toks]
        hb = jax.nn.silu(xb @ w1[e]) * (xb @ w3[e])
        return (hb @ w2[e]) * gs[:, None]

    yb = lax.map(expert_block, (block_e, row_t.reshape(n_blocks, MOE_BLOCK),
                                row_g.reshape(n_blocks, MOE_BLOCK)))
    routed = jax.ops.segment_sum(yb.reshape(n_rows, -1), row_t, num_segments=t)
    shared = (jax.nn.silu(x2 @ ws1) * (x2 @ ws3)) @ ws2
    return routed + shared

def setup_inputs(seed: int = 0) -> dict:
    key = jax.random.key(seed)
    ks = jax.random.split(key, 24)
    n_pool = len(range(0, DEPTH, N_MIXERS))
    n_attn = len(range(1, DEPTH, N_MIXERS))
    n_conv = len(range(2, DEPTH, N_MIXERS))
    f32 = jnp.float32

    def nrm(k, shape, scale):
        return jax.random.normal(k, shape, f32) * scale

    d = D_MODEL
    return {
        "x": nrm(ks[0], (BATCH, SEQ, d), 1.0),
        "ln_gain": 1.0 + nrm(ks[1], (DEPTH, 2, d), 0.02),
        "ln_bias": nrm(ks[2], (DEPTH, 2, d), 0.02),
        "pool_w": nrm(ks[3], (n_pool, POOL_GROUPS, POOL_CH, POOL_CH), POOL_CH ** -0.5 * DEEPNORM_BETA),
        "pool_scale": 1.0 + nrm(ks[4], (n_pool, d), 0.02),
        "attn_wqkv": nrm(ks[5], (n_attn, d, QKV_WIDTH), d ** -0.5),
        "attn_bqkv": nrm(ks[6], (n_attn, QKV_WIDTH), 0.02),
        "attn_sinks": nrm(ks[7], (n_attn, N_Q_HEADS), 1.0),
        "attn_wo": nrm(ks[8], (n_attn, N_Q_HEADS * HEAD_DIM, d), (N_Q_HEADS * HEAD_DIM) ** -0.5 * DEEPNORM_BETA),
        "attn_bo": nrm(ks[9], (n_attn, d), 0.02),
        "conv_w_in": nrm(ks[10], (n_conv, d, 3 * d), d ** -0.5),
        "conv_w": nrm(ks[11], (n_conv, CONV_WIDTH, d), CONV_WIDTH ** -0.5),
        "conv_w_out": nrm(ks[12], (n_conv, d, d), d ** -0.5 * DEEPNORM_BETA),
        "router_w": nrm(ks[13], (DEPTH, d, N_EXPERTS), d ** -0.5),
        "router_bias": nrm(ks[14], (DEPTH, N_EXPERTS), 0.01),
        "expert_w1": nrm(ks[15], (DEPTH, N_EXPERTS, d, D_EXPERT), d ** -0.5),
        "expert_w3": nrm(ks[16], (DEPTH, N_EXPERTS, d, D_EXPERT), d ** -0.5),
        "expert_w2": nrm(ks[17], (DEPTH, N_EXPERTS, D_EXPERT, d), D_EXPERT ** -0.5 * DEEPNORM_BETA),
        "shared_w1": nrm(ks[18], (DEPTH, d, D_SHARED), d ** -0.5),
        "shared_w3": nrm(ks[19], (DEPTH, d, D_SHARED), d ** -0.5),
        "shared_w2": nrm(ks[20], (DEPTH, D_SHARED, d), D_SHARED ** -0.5 * DEEPNORM_BETA),
    }

def reference(x, ln_gain, ln_bias, pool_w, pool_scale, attn_wqkv, attn_bqkv, attn_sinks,
              attn_wo, attn_bo, conv_w_in, conv_w, conv_w_out, router_w, router_bias,
              expert_w1, expert_w3, expert_w2, shared_w1, shared_w3, shared_w2):
    bsz, seq, d = x.shape
    cos, sin = _rope_tables(seq)
    for i in range(DEPTH):
        kind = i % N_MIXERS
        j = i // N_MIXERS
        if kind == 0:
            mix = _pool_mixer(x, pool_w[j], pool_scale[j])
        elif kind == 1:
            mix = _swa_attention(x, attn_wqkv[j], attn_bqkv[j], attn_sinks[j],
                                 attn_wo[j], attn_bo[j], cos, sin)
        else:
            mix = _gated_conv(x, conv_w_in[j], conv_w[j], conv_w_out[j])
        x = _layer_norm(DEEPNORM_ALPHA * x + mix, ln_gain[i, 0], ln_bias[i, 0])
        ff = _moe(x.reshape(bsz * seq, d), router_w[i], router_bias[i], expert_w1[i],
                  expert_w3[i], expert_w2[i], shared_w1[i], shared_w3[i], shared_w2[i])
        x = _layer_norm(DEEPNORM_ALPHA * x + ff.reshape(bsz, seq, d), ln_gain[i, 1], ln_bias[i, 1])
    return x


_drawn_inputs = setup_inputs


def setup_inputs(seed=0):
    import zlib

    import numpy as np

    out = dict(_drawn_inputs(seed))
    spreads = {}
    factors = {'attn_bqkv': 2.911, 'attn_sinks': 8.0}
    for name, (base, spread) in spreads.items():
        noise = np.random.default_rng([zlib.crc32(name.encode()), seed]).standard_normal(out[name].shape)
        drawn = base * np.exp(spread * noise) if base else spread * noise
        out[name] = __import__('jax').numpy.asarray(drawn.astype(out[name].dtype))
    for name, factor in factors.items():
        out[name] = (out[name] * factor).astype(out[name].dtype)
    return out
```

```python
import math
from contextlib import ExitStack

import numpy as np

import concourse.bass as bass
from concourse import mybir

F32 = mybir.dt.float32
F32R = mybir.dt.float32r
BF16 = mybir.dt.bfloat16
I32 = mybir.dt.int32
U32 = mybir.dt.uint32
ALU = mybir.AluOpType
ACT = mybir.ActivationFunctionType
AX = mybir.AxisListType

P = 128
SEQ = 512
D = 1024
TILES = SEQ // P
CHUNKS = D // P
LAYERS = 2
WINDOWS = (2, 4, 8, 16)
GROUP_CH = D // len(WINDOWS)
HEAD = 64
HEADS = D // HEAD
KV_HEADS = 4
PER_KV = HEADS // KV_HEADS
KV = KV_HEADS * HEAD
QKV = D + 2 * KV
EXPERTS = 64
TOP_K = 8
EXPERT_GROUPS = 8
PER_GROUP = EXPERTS // EXPERT_GROUPS
TOP_GROUPS = 4
FF = 256
FC = FF // P
ROUTED_SCALE = 2.5
EPS = 1e-5
ALPHA = (2 * LAYERS) ** 0.25
CAP = 96
ROUNDS = -(-SEQ // CAP)
FAR = -4096.0
LOW = -1.0e30
TAKEN = -3.0e38
FILLER = -2.0e38

UNIT = CHUNKS * FF
SLOTS = 6
PIECES = 2
PIECE = UNIT // PIECES
TAB = 6
BANK = 512


class Block:

    def __init__(self, q, r, expert=None):
        self.q, self.r, self.expert = q + r // 4, r % 4, expert

    def after(self, k):
        return Block(self.q, self.r + k, self.expert + k)

    def times(self, k, plus=0):
        return 4 * k * self.q + (k * self.r + plus)


def shape_constants():
    t = np.arange(P)
    pool = np.zeros((P, len(WINDOWS), 3, P), np.float32)
    for g, w in enumerate(WINDOWS):
        for kind in range(3):
            first = 0 if kind == 0 else P
            dst = first + t[None, :]
            src = t[:, None] + (first if kind < 2 else 0)
            inside = (src <= dst) & (src > dst - w)
            m = np.where(inside, 1.0 / np.minimum(dst + 1, w), 0.0)
            if kind < 2:
                m = m - (src == dst)
            pool[:, g, kind, :] = m
    slots = np.broadcast_to(np.arange(CAP, dtype=np.float32)[None, :], (P, CAP))
    dummy = np.stack([-(SEQ + t), SEQ + t], 1).astype(np.float32)
    inv = (10000.0 ** (-np.arange(0, HEAD, 2, dtype=np.float32) / np.float32(HEAD))).astype(np.float32)
    ang = (np.arange(SEQ, dtype=np.float32)[:, None] * inv[None, :]).astype(np.float32)
    rope = np.stack([np.cos(ang), np.sin(ang)], 1).astype(np.float32)
    rope = rope.reshape(TILES, P, 2, HEAD // 2).transpose(1, 0, 2, 3)
    ki = np.arange(2 * P)[None, :]
    band = np.where((ki > t[:, None]) & (ki <= t[:, None] + P), 0.0, LOW).astype(np.float32)
    return {
        "ident": np.eye(P, dtype=np.float32),
        "pool_band": pool,
        "slots": np.ascontiguousarray(slots),
        "dummy": dummy,
        "rope": np.ascontiguousarray(rope),
        "band": band,
    }


def build(nc, i, c, out):
    ctx = ExitStack()

    def sb(name, shape, dt=F32):
        return ctx.enter_context(nc.sbuf_tensor(name, shape, dt))

    def sem(name):
        return ctx.enter_context(nc.semaphore(name))

    raw = sb("raw", [P, SLOTS * UNIT])
    split = sb("split", [P, 2 * SLOTS * UNIT], F32R)
    xT = sb("xT", [P, 2, 2, CHUNKS, P], F32R)
    xn = sb("xn", [P, TILES, D])
    par = sb("par", [P, 3, D])
    rw = sb("rw", [P, 2, CHUNKS, EXPERTS], F32R)
    hT = sb("hT", [P, 2, FC, P], F32R)
    ident = sb("ident", [P, P])
    work = sb("work", [P, 3232])
    psum = ctx.enter_context(nc.psum_tensor("psum", [P, 8, BANK], F32))
    rows = nc.dram_tensor("rows", [SEQ, D], F32).ap()
    sums = [nc.dram_tensor(f"sums{l}", [SEQ + CAP, D], F32).ap() for l in range(LAYERS)]

    parf = par[:].rearrange("p a d -> p (a d)")

    def at(t, start, *dims, dt=F32):
        n = 1
        for d in dims:
            n *= d
        words = n * (2 if dt == BF16 else 4) // 4
        v = t[:, start:start + words]
        if dt != F32:
            v = v.bitcast(dt)
        if len(dims) == 1:
            return v
        names = "abcd"[:len(dims)]
        return v.rearrange(f"p ({' '.join(names)}) -> p {' '.join(names)}", **dict(zip(names, dims)))

    h_sb = at(work, 0, FC, P)
    oh = at(work, 256, 2, TILES, CAP, dt=BF16)
    tab = at(work, 640, TILES, EXPERTS, TAB, dt=BF16)
    ranks = at(work, 1408, TILES, EXPERTS)
    slots = at(work, 1664, CAP)
    order = at(work, 1760, 2, P, dt=BF16)
    xp = at(work, 1888, D)
    rw_raw = at(work, 0, CHUNKS, EXPERTS)
    k_nat = at(work, 0, TILES, KV)
    v_nat = at(work, 1024, TILES, KV)
    score = [at(work, 2048, PER_KV, 2 * P), at(raw, 7168, PER_KV, 2 * P)]
    router_bias = at(work, 3072, EXPERTS)
    negsink = at(work, 3136, HEADS)
    dummy = at(work, 3152, 2)
    stats = at(work, 3154, 2, 6)
    mean_var = at(work, 3166, 2)
    power = at(work, 3168, 3)
    slot_row = at(work, 3171, 1)
    index = work[:, 3172:3176].bitcast(I32)
    gate = at(work, 3176, 4)
    index_out = work[:, 3180:3184].bitcast(I32)
    most = at(work, 3184, 1)
    most_int = work[:, 3185:3186].bitcast(I32)
    top = at(work, 3188, PER_KV)
    negtop = at(work, 3192, 2, PER_KV)
    sink_arg = at(work, 3200, 2, PER_KV)
    total = at(work, 3208, 2, PER_KV)
    sink_exp = at(work, 3216, 2, PER_KV)
    inverse = at(work, 3224, 2, PER_KV)
    prob = at(parf, 2048, TILES, EXPERTS)
    sel = at(parf, 2304, TILES, EXPERTS)
    rest = at(parf, 2560, TILES, EXPERTS)
    chosen = at(parf, 2816, TILES, EXPERTS, dt=BF16)
    gsum = at(parf, 2944, TILES)
    group_top = at(work, 256, TILES, EXPERT_GROUPS, 8)
    gext = at(work, 512, TILES, EXPERT_GROUPS + 4)
    gtop = at(work, 560, TILES, 8)
    etop = at(work, 592, TILES, 8)
    xg = [xn[:, b, :] for b in range(2)]
    yo = [xn[:, 2 + b, :] for b in range(2)]
    pool_band = at(raw, 8192, len(WINDOWS), 3, P)
    pool_w = at(raw, 9728, len(WINDOWS), 2, GROUP_CH)
    pool_tmp = at(raw, 11776, BANK)
    pooled = at(work, 1888, CHUNKS, P)
    wqkv_raw = at(raw, 0, CHUNKS, QKV)
    wqkv = split[:, :].rearrange("p (s c n) -> p s c n", s=2, c=CHUNKS)
    wo_raw = at(raw, 0, 3, D)
    wo = split[:, 0:2 * CHUNKS * D].rearrange("p (s c n) -> p s c n", s=2, c=CHUNKS)
    band = at(raw, 3072, 2 * P)
    kT = at(raw, 4096, KV_HEADS, 2, P)
    qT = [at(raw, 5120 + 512 * b, PER_KV, P) for b in range(2)]
    pT = at(raw, 6144, 2, PER_KV, P)
    q_nat = at(raw, 8192, TILES, D)
    bqkv = at(parf, 0, QKV)
    rope = at(parf, QKV, TILES, 2, HEAD // 2)
    bo = par[:, 2, :]

    def raw_slot(slot):
        return raw[:, slot * UNIT:(slot + 1) * UNIT]

    def split_slot(slot):
        return split[:, 2 * slot * UNIT:2 * (slot + 1) * UNIT].rearrange("p (s n) -> p s n", s=2)

    ps_xT = psum[:, 0:2, :]
    ps_h = psum[:, 2, :]
    ps_hT = psum[:, 3, :]
    ps_list = psum[:, 4, :]
    ps_y = psum[:, 5:7, :]
    ps_log = psum[:, 7, :]

    def xT_ps(m):
        return ps_xT[:, :, 0:4 * m].rearrange("p b (c t) -> p b c t", c=4)

    s_const = sem("s_const")
    s_x = [sem(f"s_x{t}") for t in range(TILES)]
    s_pool_w = sem("s_pool_w")
    s_par = sem("s_par")
    s_dve = sem("s_dve")
    s_power = sem("s_power")
    s_pool_waited = sem("s_pool_waited")
    s_pooled = sem("s_pooled")
    s_pooled_sb = sem("s_pooled_sb")
    s_mix = sem("s_mix")
    s_mix_used = sem("s_mix_used")
    s_var = sem("s_var")
    s_vareps = sem("s_vareps")
    s_rstd = sem("s_rstd")
    s_norm = sem("s_norm")
    s_rw_in = sem("s_rw_in")
    s_rw_head = sem("s_rw_head")
    s_rw_tail = sem("s_rw_tail")
    s_moe_const = sem("s_moe_const")
    per_layer = ("xp", "rows_out", "logits", "prob", "order", "chosen", "ranked", "most", "tabled",
                 "head", "tail", "xTready", "xhead", "xtail", "m1", "silu", "hidden", "hTready", "hhead",
                 "htail", "m2", "yout", "oh", "listed", "slotrow", "index", "idxcopy", "slots", "round_over",
                 "pe_idle", "dve_idle")
    S = [{n: sem(f"s_{n}{l}") for n in per_layer} for l in range(LAYERS)]
    s_w = [[sem(f"s_w{l}_{k}") for k in range(SLOTS)] for l in range(LAYERS)]
    s_xg = [[sem(f"s_xg{l}_{b}") for b in range(2)] for l in range(LAYERS)]
    s_scat = [[sem(f"s_scat{l}_{b}") for b in range(2)] for l in range(LAYERS)]
    s_acc_out = [sem(f"s_acc_out{l}") for l in range(LAYERS)]
    s_acc_in = [[sem(f"s_acc_in{l}_{t}") for t in range(TILES)] for l in range(LAYERS)]
    s_out = sem("s_out")
    s_wqkv = [sem(f"s_wqkv{k}") for k in range(CHUNKS)]
    s_qhead = sem("s_qhead")
    s_qtail = sem("s_qtail")
    s_axT = sem("s_axT")
    s_axhead = sem("s_axhead")
    s_axtail = sem("s_axtail")
    s_qkv = sem("s_qkv")
    s_qkv_used = sem("s_qkv_used")
    s_roped = sem("s_roped")
    s_wo_in = [sem(f"s_wo_in{k}") for k in range(3)]
    s_wohead = sem("s_wohead")
    s_wotail = sem("s_wotail")
    s_qkT = sem("s_qkT")
    s_qkT_sb = sem("s_qkT_sb")
    s_score = sem("s_score")
    s_masked = sem("s_masked")
    s_negtop = sem("s_negtop")
    s_exp = sem("s_exp")
    s_inv = sem("s_inv")
    s_pT = sem("s_pT")
    s_pT_cur = sem("s_pT_cur")
    s_pT_prev = sem("s_pT_prev")
    s_pv = sem("s_pv")
    s_o = sem("s_o")
    s_wo = sem("s_wo")
    s_wo_used = sem("s_wo_used")
    s_band = sem("s_band")

    UNITS = TILES * KV_HEADS
    HALVES = (0, 1)
    PASSES = ((0, 0), (0, 1), (1, 0))

    def prev_count(n):
        return max(0, n - KV_HEADS)

    def run_steps(eng, rnd, body):
        base = EXPERTS // 4 * rnd + 1

        def peeled(s):
            body(Block(base, s, s), lambda k: 0 <= s + k < EXPERTS)

        for s in range(-3, 5):
            peeled(s)
        with eng.Fori(0, 14) as q:
            for r in range(4):
                body(Block(base + 1 + q, 1 + r, 4 * q + (5 + r)), lambda k: True)
        for s in range(61, 66):
            peeled(s)

    def run_rounds(eng, l, one_round):
        one_round(0)
        eng.wait_ge(S[l]["most"], 1)
        most_tokens = eng.value_load(most_int[0:1, 0:1], min_val=0, max_val=SEQ)
        with eng.Fori(1, ROUNDS) as rnd:
            with eng.If(most_tokens > rnd * CAP):
                one_round(rnd)
            eng.nop()

    def weight_unit(b, u):
        k = 3 * (b.r + 1) + u
        return k % SLOTS, 2 * (b.q - 1) + k // SLOTS + 1

    block = ctx.enter_context(nc.Block())

    @block.sync
    def _(sp):
        def load_par(vectors):
            for dst, src in vectors:
                sp.dma_start(dst, src).then_inc(s_par, 16)

        def bc(v):
            return v.partition_broadcast(P)

        def expert_matrix(l, n, u, slot):
            if u < 2:
                w = i["expert_w1" if u == 0 else "expert_w3"]
            else:
                w = i["expert_w2"]
            src = w[l].rearrange("e (p a) f -> p e (a f)", p=P)[:, bass.ds(n, 1), :]
            return sp.dma_start(raw_slot(slot).rearrange("p (e n) -> p e n", e=1), src)

        def shared_matrix(l, u):
            w = i[("shared_w1", "shared_w3", "shared_w2")[u]][l]
            sp.dma_start(raw_slot(u), w.rearrange("(p a) f -> p (a f)", p=P)).then_inc(s_w[l][u], 16)

        def moe_consts(l):
            sp.dma_start(slots, c["slots"]).then_inc(s_moe_const, 16)
            sp.dma_start(router_bias, bc(i["router_bias"][l])).then_inc(s_moe_const, 16)

        def experts(l):
            def one(b, u, e, wait):
                slot, _ = weight_unit(b, u)
                if wait:
                    sp.wait_ge(S[l]["tail"], b.times(3 * PIECES, PIECES * (u - 14)))
                expert_matrix(l, e, u, slot).then_inc(s_w[l][slot], 16)

            def one_round(rnd):
                base = 16 * rnd + 1
                if isinstance(rnd, int):
                    first = 4
                    for n in range(1, first):
                        for u in range(3):
                            one(Block(1, n), u, n, True)
                    with sp.Fori(1, EXPERTS // 4) as q:
                        for r in range(4):
                            for u in range(3):
                                one(Block(base + q, r), u, 4 * q + r, True)
                else:
                    with sp.Fori(0, EXPERTS // 4) as q:
                        for r in range(4):
                            for u in range(3):
                                one(Block(base + q, r), u, 4 * q + r, True)

            run_rounds(sp, l, one_round)

        for t in range(TILES):
            sp.dma_start(xn[:, t, :], i["x"][0, t * P:(t + 1) * P, :]).then_inc(s_x[t], 16)
            if t == 0:
                sp.dma_start(pool_band, c["pool_band"]).then_inc(s_pool_w, 16)
                sp.dma_start(pool_w, i["pool_w"][0].rearrange("g (k p) n -> p g k n", p=P)).then_inc(s_pool_w, 16)
                load_par([(par[:, 2, :], bc(i["pool_scale"][0])), (par[:, 0, :], bc(i["ln_gain"][0, 0])),
                          (par[:, 1, :], bc(i["ln_bias"][0, 0]))])
                sp.dma_start(ident[:], c["ident"]).then_inc(s_const, 16)
                sp.dma_start(dummy, c["dummy"]).then_inc(s_const, 16)
        sp.dma_start(rw_raw, i["router_w"][0].rearrange("(p a) e -> p a e", p=P)).then_inc(s_rw_in, 16)
        moe_consts(0)
        for u in range(3):
            shared_matrix(0, u)
        expert_matrix(0, 0, 0, 3).then_inc(s_w[0][3], 16)
        sp.wait_ge(s_norm, 1 * TILES)
        for u in (1, 2):
            expert_matrix(0, 0, u, 3 + u).then_inc(s_w[0][3 + u], 16)
        load_par([(par[:, 0, :], bc(i["ln_gain"][0, 1])), (par[:, 1, :], bc(i["ln_bias"][0, 1]))])
        experts(0)

        sp.wait_ge(S[0]["dve_idle"], 1)
        for k in range(CHUNKS):
            sp.dma_start(wqkv_raw[:, k, :], i["attn_wqkv"][0, k * P:(k + 1) * P, :]).then_inc(s_wqkv[k], 16)
        sp.wait_ge(s_norm, 2 * TILES)
        load_par([(bqkv, bc(i["attn_bqkv"][0])), (rope, c["rope"]), (bo, bc(i["attn_bo"][0])),
                  (negsink, bc(i["attn_sinks"][0]))])
        sp.wait_ge(s_qtail, CHUNKS)
        sp.dma_start(band, c["band"]).then_inc(s_band, 16)
        for k in range(CHUNKS):
            if k >= 3:
                sp.wait_ge(s_wotail, k - 2)
            sp.dma_start(wo_raw[:, k % 3, :], i["attn_wo"][0, k * P:(k + 1) * P, :]).then_inc(s_wo_in[k % 3], 16)
            if k == 2:
                sp.wait_ge(s_roped, TILES)
                load_par([(par[:, 0, :], bc(i["ln_gain"][1, 0])), (par[:, 1, :], bc(i["ln_bias"][1, 0]))])
        sp.wait_ge(s_o, UNITS)
        sp.wait_ge(s_pv, UNITS)
        for u in range(3):
            shared_matrix(1, u)
        sp.dma_start(rw_raw, i["router_w"][1].rearrange("(p a) e -> p a e", p=P)).then_inc(s_rw_in, 16)
        moe_consts(1)
        expert_matrix(1, 0, 0, 3).then_inc(s_w[1][3], 16)
        sp.wait_ge(s_axT, 2 * TILES)
        for u in (1, 2):
            expert_matrix(1, 0, u, 3 + u).then_inc(s_w[1][3 + u], 16)
        sp.wait_ge(s_norm, 3 * TILES)
        load_par([(par[:, 0, :], bc(i["ln_gain"][1, 1])), (par[:, 1, :], bc(i["ln_bias"][1, 1]))])
        experts(1)
        for t in range(TILES):
            sp.wait_ge(s_norm, 3 * TILES + t + 1)
            sp.dma_start(out[0, t * P:(t + 1) * P, :], xn[:, t, :]).then_inc(s_out, 16)
        sp.wait_ge(s_out, 16 * TILES)

    @block.gpsimd
    def _(pool):
        pool.memset(power[:, 0:1], -0.5).then_inc(s_power, 1)
        pool.wait_ge(s_power, 1)

        def hold_waits():
            pool.sem_inc(s_pool_waited, 1)

        def rstd(n):
            pool.wait_ge(s_var, n + 1)
            pool.tensor_scalar(power[:, 1:2], mean_var[:, 1:2], EPS, None, ALU.add).then_inc(s_vareps, 1)
            pool.wait_ge(s_vareps, n + 1)
            pool.tensor_tensor(power[:, 2:3], power[:, 1:2], power[:, 0:1], ALU.pow).then_inc(s_rstd, 1)

        def rows_and_sums(l):
            for t in range(TILES):
                rstd(2 * l * TILES + t)
            for t in range(TILES):
                store_rows(l, t)

        def store_rows(l, t):
            pool.wait_ge(S[l]["xp"], t + 1)
            pool.dma_start(rows[t * P:(t + 1) * P, :], xp).then_inc(S[l]["rows_out"], 16)

        def order_matrices(l):
            if l:
                pool.wait_ge(s_o, UNITS)
            pool.memset(order, 1.0).then_inc(S[l]["order"], 1)
            pool.wait_ge(S[l]["order"], 1)
            pool.affine_select(out=order[:, 0, :], in_=order[:, 0, :], compare_op=ALU.is_gt, fill=0.0, base=0,
                               pattern=[[1, P]], channel_multiplier=-1).then_inc(S[l]["order"], 1)

        def store_sums(l):
            for t in range(TILES):
                pool.wait_ge(S[l]["yout"], t + 1)
                pool.dma_start(sums[l][t * P:(t + 1) * P, :], xn[:, t, :]).then_inc(s_acc_out[l], 16)
                if t == 0:
                    pool.dma_start(sums[l][SEQ:SEQ + CAP, :], xn[0:CAP, 0, :]).then_inc(s_acc_out[l], 16)
            pool.wait_ge(S[l]["rows_out"], 16 * TILES)
            pool.wait_ge(s_acc_out[l], 16 * (TILES + 1))

        def experts(l):
            s = S[l]

            def body(b, valid):
                if valid(2):
                    n = b.after(2)
                    pool.wait_ge(s["index"], n.times(1, 1 - 4))
                    pool.wait_ge(s["xTready"], n.times(1, -1))
                    hold_waits()
                    pool.indirect_dma_start(
                        xg[n.r % 2][0:CAP, :], None, rows[:, :],
                        bass.IndirectOffsetOnAxis(ap=index[0:CAP, n.r:n.r + 1].bitcast(U32), axis=0),
                        bounds_check=SEQ - 1, oob_is_err=False).then_inc(s_xg[l][n.r % 2], 16)
                if valid(0):
                    pool.wait_ge(s["index"], b.times(1, 1 - 4))
                    hold_waits()
                    pool.tensor_copy(index_out[0:CAP, b.r:b.r + 1], index[0:CAP, b.r:b.r + 1]).then_inc(s["idxcopy"], 1)
                if valid(-2):
                    n = b.after(-2)
                    pool.wait_ge(s["yout"], n.times(1, 1))
                    pool.wait_ge(s["idxcopy"], n.times(1, 1 - 4))
                    if not (isinstance(n.q, int) and n.q == 1 and n.r == 0):
                        before = n.after(-1)
                        pool.wait_ge(s_scat[l][before.r % 2], 16 * (2 * (before.q - 1) + before.r // 2 + 1))
                    hold_waits()
                    pool.indirect_dma_start(
                        sums[l][:, :], bass.IndirectOffsetOnAxis(ap=index_out[0:CAP, n.r:n.r + 1].bitcast(U32), axis=0),
                        yo[n.r % 2][0:CAP, :], None, compute_op=ALU.add).then_inc(s_scat[l][n.r % 2], 16)

            def one_round(rnd):
                run_steps(pool, rnd, body)
                for b in range(2):
                    pool.wait_ge(s_scat[l][b], 16 * (EXPERTS // 2) * (rnd + 1))
                hold_waits()

            run_rounds(pool, l, one_round)
            pool.wait_ge(s["pe_idle"], 1)
            for t in range(TILES):
                pool.dma_start(xn[:, t, :], sums[l][t * P:(t + 1) * P, :]).then_inc(s_acc_in[l][t], 16)

        for l in range(LAYERS):
            rows_and_sums(l)
            order_matrices(l)
            store_sums(l)
            experts(l)
            for t in range(TILES):
                rstd((2 * l + 1) * TILES + t)

    @block.scalar
    def _(act):
        def matrix_head(l, slot, landed, piece):
            if piece == 0:
                act.wait_ge(s_w[l][slot], 16 * landed)
            cols = slice(piece * PIECE, (piece + 1) * PIECE)
            act.activation(split_slot(slot)[:, 0, cols], raw_slot(slot)[:, cols], ACT.Copy).then_inc(S[l]["head"], 1)

        def rows_head(s, b, m, waits):
            for sm, v in waits:
                act.wait_ge(sm, v)
            act.activation(xT[:, b % 2, 0, :, 0:m].rearrange("p (b c) t -> p b c t", b=2), xT_ps(m), ACT.Copy).then_inc(s, 1)

        def silu(l, b, m):
            act.wait_ge(S[l]["m1"], b.times(1, 1))
            if not (isinstance(b.q, int) and b.times(1) == 0):
                act.wait_ge(S[l]["hTready"], b.times(1))
            act.activation(h_sb[0:m], ps_h[0:m, 0:FF].rearrange("p (a j) -> p j a", j=FC), ACT.Silu).then_inc(S[l]["silu"], 1)

        def hidden_head(l, b, m):
            act.wait_ge(S[l]["hTready"], b.times(1, 1))
            if not (isinstance(b.q, int) and b.times(1) == 0):
                act.wait_ge(S[l]["m2"], b.times(1))
            act.activation(hT[:, 0, :, 0:m], ps_hT[:, 0:FC * m].rearrange("p (j t) -> p j t", j=FC),
                           ACT.Copy).then_inc(S[l]["hhead"], 1)

        def dense(l):
            s = S[l]
            for t in range(TILES):
                act.wait_ge(s_norm, 2 * l * TILES + t + 1)
                if t:
                    act.wait_ge(s["xTready"], t)
                    act.wait_ge(s["rows_out"], 16 * t)
                elif l == 0:
                    act.wait_ge(s_mix, TILES)
                act.activation(xp.rearrange("p (c a) -> p c a", c=CHUNKS),
                               xn[:, t, :].rearrange("p (a c) -> p c a", c=CHUNKS), ACT.Copy).then_inc(s["xp"], 1)
                act.wait_ge(s["xTready"], t + 1)
                rows_head(s["xhead"], t, P, [(s["m1"], t - 1)] if t >= 2 else [])
                silu(l, Block(0, t), P)
                hidden_head(l, Block(0, t), P)
            act.wait_ge(s["logits"], TILES)
            act.activation(prob, ps_log[:, 0:TILES * EXPERTS].rearrange("p (t e) -> p t e", t=TILES),
                           ACT.Sigmoid).then_inc(s["prob"], 1)

        def experts(l):
            s = S[l]

            def body(b, valid):
                if valid(-2):
                    n = b.after(-2)
                    act.wait_ge(s["m2"], n.times(1, 1))
                    if not (isinstance(n.q, int) and n.q == 1 and n.r < 2):
                        old = n.after(-2)
                        act.wait_ge(s_scat[l][n.r % 2], 16 * (2 * (old.q - 1) + old.r // 2 + 1))
                    act.activation(yo[n.r % 2][0:CAP].rearrange("p (b n) -> p b n", b=2), ps_y[0:CAP], ACT.Copy,
                                   scale=gate[0:CAP, n.r:n.r + 1]).then_inc(s["yout"], 1)
                if valid(-1):
                    hidden_head(l, b.after(-1), CAP)
                if valid(1):
                    n = b.after(1)
                    rows_head(s["xhead"], n.r, CAP, [(s["xTready"], n.times(1, 1)), (s["m1"], n.times(1, -1))])
                if valid(0):
                    slot, landed = weight_unit(b, 2)
                    if not first_of_all(b):
                        act.wait_ge(s["m2"], b.times(1, -1))
                    for piece in range(PIECES):
                        matrix_head(l, slot, landed, piece)
                if valid(1):
                    n = b.after(1)
                    if not first_of_all(n):
                        act.wait_ge(s["m1"], n.times(1, -1))
                    slot, landed = weight_unit(n, 0)
                    for piece in range(PIECES):
                        matrix_head(l, slot, landed, piece)
                    slot, landed = weight_unit(n, 1)
                    matrix_head(l, slot, landed, 0)
                if valid(0):
                    silu(l, b, CAP)
                if valid(1):
                    matrix_head(l, slot, landed, 1)

            run_rounds(act, l, lambda rnd: run_steps(act, rnd, body))

        def first_of_all(b):
            return isinstance(b.q, int) and b.times(1) == 4

        def shared_heads(l):
            for u in range(3):
                for piece in range(PIECES):
                    matrix_head(l, u, 1, piece)

        def router_head(l):
            act.wait_ge(s_rw_in, 16 * (l + 1))
            act.activation(rw[:, 0], rw_raw, ACT.Copy).then_inc(s_rw_head, 1)

        shared_heads(0)
        router_head(0)
        for t in range(TILES):
            act.wait_ge(s_pooled, t + 1)
            if t:
                act.wait_ge(s_mix, t)
            act.activation(pooled.rearrange("p (b c) t -> p b (c t)", b=2), ps_xT, ACT.Copy).then_inc(s_pooled_sb, 1)
        dense(0)
        experts(0)

        act.wait_ge(S[0]["pe_idle"], 1)
        for k in range(CHUNKS):
            act.wait_ge(s_wqkv[k], 16)
            act.activation(wqkv[:, 0, k, :], wqkv_raw[:, k, :], ACT.Copy).then_inc(s_qhead, 1)
        for t in range(TILES):
            waits = [(s_axT, t + 1)]
            if t >= 2:
                waits.append((s_qkv, t - 1))
            rows_head(s_axhead, t, P, waits)

        def wo_head(k):
            act.wait_ge(s_wo_in[k % 3], 16 * (k // 3 + 1))
            act.activation(wo[:, 0, k, :], wo_raw[:, k % 3, :], ACT.Copy).then_inc(s_wohead, 1)

        act.wait_ge(s_qkv, TILES)

        def attention_unit(u):
            n, g = divmod(u, KV_HEADS)
            keys = slice(0 if n else P, 2 * P)
            act.wait_ge(s_qkT, u + 1)
            if u >= 2:
                act.wait_ge(s_score, u - 1)
            act.activation(qT[u % 2][0:HEAD], ps_hT[0:HEAD, :].rearrange("p (h t) -> p h t", h=PER_KV), ACT.Copy)
            act.activation(kT[0:HEAD, g, n % 2, :], ps_y[0:HEAD, 0, 0:P], ACT.Copy).then_inc(s_qkT_sb, 1)
            act.wait_ge(s_negtop, u + 1)
            for h in range(PER_KV):
                act.activation(score[u % 2][:, h, keys], score[u % 2][:, h, keys], ACT.Exp,
                               bias=negtop[:, u % 2, h:h + 1], accum_out=total[:, u % 2, h:h + 1])
            act.activation(sink_exp[:, u % 2, :], sink_arg[:, u % 2, :], ACT.Exp).then_inc(s_exp, 1)

        def weights_out(u):
            act.wait_ge(s_pT, u + 1)
            if u:
                act.wait_ge(s_pv, u)
            act.activation(pT[:, 1], ps_h.rearrange("p (h t) -> p h t", h=PER_KV), ACT.Copy).then_inc(s_pT_cur, 1)

        for u in range(UNITS + 1):
            if u < UNITS:
                attention_unit(u)
            if u:
                weights_out(u - 1)
                if u % KV_HEADS == 0:
                    n = u // KV_HEADS - 1
                    waits = [(s_axT, TILES + n + 1)]
                    if n >= 2:
                        waits.append((s_wo, n - 1))
                    rows_head(s_axhead, n, P, waits)
            if u < 4:
                wo_head(2 * u)
                wo_head(2 * u + 1)
        act.wait_ge(s_wo, TILES)
        shared_heads(1)
        router_head(1)
        dense(1)
        experts(1)

    @block.vector
    def _(dve):
        links = [0]

        def link(ins):
            links[0] += 1
            ins.then_inc(s_dve, 1)
            dve.wait_ge(s_dve, links[0])

        norms = [0]

        def layer_norm(t):
            x = xn[:, t, :]
            for h in HALVES:
                last = dve.bn_stats(stats[:, h, :], x[:, h * BANK:(h + 1) * BANK])
            link(last)
            dve.bn_aggr(mean_var, stats).then_inc(s_var, 1)
            norms[0] += 1
            dve.wait_ge(s_rstd, norms[0])
            link(dve.tensor_scalar(x, x, mean_var[:, 0:1], power[:, 2:3], ALU.subtract, ALU.mult))
            link(dve.tensor_tensor(x, x, par[:, 0, :], ALU.mult))
            dve.tensor_tensor(x, x, par[:, 1, :], ALU.add).then_inc(s_norm, 1)

        def matrix_tail(l, slot, piece, count):
            dve.wait_ge(S[l]["head"], count)
            cols = slice(piece * PIECE, (piece + 1) * PIECE)
            w = split_slot(slot)
            dve.tensor_tensor(w[:, 1, cols], raw_slot(slot)[:, cols], w[:, 0, cols].bitcast(F32),
                              ALU.subtract).then_inc(S[l]["tail"], 1)

        def unit_count(b, u, piece):
            return b.times(3 * PIECES, PIECES * (u - 12 + 3) + piece + 1)

        def rows_tail(head, n, tail, b, m):
            dve.wait_ge(head, n)
            dst = xT[:, b % 2, 1, :, 0:m].rearrange("p (b c) t -> p b c t", b=2)
            hd = xT[:, b % 2, 0, :, 0:m].rearrange("p (b c) t -> p b c t", b=2).bitcast(F32)
            for h in HALVES:
                last = dve.tensor_tensor(dst[:, h], xT_ps(m)[:, h], hd[:, h], ALU.subtract)
            last.then_inc(tail, 1)

        def hidden(l, b, m):
            dve.wait_ge(S[l]["silu"], b.times(1, 1))
            dve.tensor_tensor(h_sb[0:m], h_sb[0:m], ps_h[0:m, FF:2 * FF].rearrange("p (a j) -> p j a", j=FC),
                              ALU.mult).then_inc(S[l]["hidden"], 1)

        def hidden_tail(l, b, m):
            dve.wait_ge(S[l]["hhead"], b.times(1, 1))
            dve.tensor_tensor(hT[:, 1, :, 0:m], ps_hT[:, 0:FC * m].rearrange("p (j t) -> p j t", j=FC),
                              hT[:, 0, :, 0:m].bitcast(F32), ALU.subtract).then_inc(S[l]["htail"], 1)

        def router_tail(l):
            dve.wait_ge(s_rw_head, l + 1)
            dve.tensor_tensor(rw[:, 1], rw_raw, rw[:, 0].bitcast(F32), ALU.subtract).then_inc(s_rw_tail, 1)

        def shared_tile(l, t):
            dve.wait_ge(S[l]["m2"], t + 1)
            dve.wait_ge(S[l]["xp"], t + 1)
            x = xn[:, t, :].rearrange("p (b n) -> p b n", b=2)
            for h in HALVES:
                last = dve.scalar_tensor_tensor(out=x[:, h], in0=x[:, h], scalar=ALPHA, in1=ps_y[:, h],
                                                op0=ALU.mult, op1=ALU.add)
            last.then_inc(S[l]["yout"], 1)

        def route(l):
            s = S[l]
            dve.wait_ge(s["prob"], 1)
            dve.wait_ge(s_moe_const, 32 * (l + 1))
            link(dve.tensor_tensor(sel, prob, router_bias.unsqueeze(1).to_broadcast([P, TILES, EXPERTS]), ALU.add))
            for t in range(TILES):
                for g in range(EXPERT_GROUPS):
                    last = dve.max(group_top[:, t, g, :], sel[:, t, g * PER_GROUP:(g + 1) * PER_GROUP])
            dve.memset(gext[:, :, EXPERT_GROUPS:], FILLER)
            link(last)
            link(dve.tensor_tensor(gext[:, :, 0:EXPERT_GROUPS], group_top[:, :, :, 0], group_top[:, :, :, 1], ALU.add))
            for t in range(TILES):
                last = dve.max(gtop[:, t, :], gext[:, t, :])
            link(last)
            link(dve.memset(gtop[:, :, TOP_GROUPS:], FILLER))
            for t in range(TILES):
                last = dve.match_replace(gext[:, t, :], gtop[:, t, :], gext[:, t, :], TAKEN)
            link(last)
            groups = gext[:, :, 0:EXPERT_GROUPS]
            link(dve.tensor_scalar(groups, groups, TAKEN, None, ALU.is_equal))
            wide = groups.unsqueeze(3).to_broadcast([P, TILES, EXPERT_GROUPS, PER_GROUP])
            sel4 = sel.rearrange("p t (g k) -> p t g k", k=PER_GROUP)
            rest4 = rest.rearrange("p t (g k) -> p t g k", k=PER_GROUP)
            link(dve.tensor_tensor(sel4, sel4, wide, ALU.mult))
            link(dve.tensor_scalar(rest4, wide, -LOW, LOW, ALU.mult, ALU.add))
            link(dve.tensor_tensor(sel, sel, rest, ALU.add))
            for t in range(TILES):
                last = dve.max(etop[:, t, :], sel[:, t, :])
            link(last)
            for t in range(TILES):
                last = dve.match_replace(rest[:, t, :], etop[:, t, :], sel[:, t, :], TAKEN)
            link(last)
            link(dve.tensor_scalar(rest, rest, TAKEN, None, ALU.is_equal))
            dve.tensor_copy(chosen, rest).then_inc(s["chosen"], 1)
            link(dve.tensor_tensor(prob, prob, rest, ALU.mult))
            link(dve.tensor_reduce(gsum, prob, AX.X, ALU.add))
            link(dve.reciprocal(gsum, gsum))
            link(dve.tensor_tensor(prob, prob, gsum.unsqueeze(2).to_broadcast([P, TILES, EXPERTS]), ALU.mult))
            link(dve.tensor_scalar(prob, prob, ROUTED_SCALE, None, ALU.mult))
            for k in range(3):
                link(dve.tensor_copy(tab[:, :, :, 3 + k], prob))
                if k < 2:
                    link(dve.tensor_tensor(prob, prob, tab[:, :, :, 3 + k], ALU.subtract))
            dve.wait_ge(s["ranked"], 1)
            link(dve.tensor_tensor(ranks, ps_list[:, 0:256].rearrange("p (t e) -> p t e", t=TILES), rest, ALU.mult))
            link(dve.tensor_scalar(rest, rest, -FAR, FAR, ALU.mult, ALU.add))
            dve.tensor_reduce(most, ps_list[:, 256:256 + EXPERTS], AX.X, ALU.max)
            link(dve.tensor_tensor(ranks, ranks, rest, ALU.add))
            dve.tensor_copy(most_int, most).then_inc(s["most"], 1)

        def experts(l):
            s = S[l]

            def body(b, valid):
                if valid(-1):
                    hidden_tail(l, b.after(-1), CAP)
                if valid(3):
                    n = b.after(3)
                    if not (isinstance(n.q, int) and n.q == 1 and n.r < 2):
                        dve.wait_ge(s["listed"], n.times(1, -1 - 4))
                    dve.tensor_tensor(oh[:, n.r % 2],
                                      ranks[:, :, bass.ds(n.expert, 1)].to_broadcast([P, TILES, CAP]),
                                      slots.unsqueeze(1).to_broadcast([P, TILES, CAP]),
                                      ALU.is_equal).then_inc(s["oh"], 1)
                if valid(2):
                    n = b.after(2)
                    dve.wait_ge(s["listed"], n.times(1, 1 - 4))
                    first = isinstance(n.q, int) and n.q == 1
                    if not first:
                        dve.wait_ge(s["yout"], n.times(1, -3))
                        dve.wait_ge(s["idxcopy"], n.times(1, -3 - 4))
                    dve.tensor_scalar(slot_row[0:CAP], ps_list[0:CAP, 2:3], dummy[0:CAP, 0:1], dummy[0:CAP, 1:2],
                                      ALU.mult, ALU.add).then_inc(s["slotrow"], 1)
                    dve.tensor_reduce(gate[0:CAP, n.r:n.r + 1], ps_list[0:CAP, 3:6], AX.X, ALU.add)
                    dve.wait_ge(s["slotrow"], n.times(1, 1 - 4))
                    dve.tensor_scalar(index[0:CAP, n.r:n.r + 1], slot_row[0:CAP], ps_list[0:CAP, 0:1],
                                      ps_list[0:CAP, 1:2], ALU.add, ALU.add).then_inc(s["index"], 1)
                if valid(1):
                    n = b.after(1)
                    rows_tail(s["xhead"], n.times(1, 1), s["xtail"], n.r, CAP)
                if valid(0):
                    slot, _ = weight_unit(b, 2)
                    for piece in range(PIECES):
                        matrix_tail(l, slot, piece, unit_count(b, 2, piece))
                if valid(1):
                    slot, _ = weight_unit(n, 0)
                    for piece in range(PIECES):
                        matrix_tail(l, slot, piece, unit_count(n, 0, piece))
                    slot, _ = weight_unit(n, 1)
                    matrix_tail(l, slot, 0, unit_count(n, 1, 0))
                if valid(0):
                    hidden(l, b, CAP)
                if valid(1):
                    matrix_tail(l, slot, 1, unit_count(n, 1, 1))

            def one_round(rnd):
                if not isinstance(rnd, int):
                    dve.tensor_scalar(slots, slots, float(CAP), None, ALU.add).then_inc(s["slots"], 1)
                    dve.wait_ge(s["slots"], rnd)
                run_steps(dve, rnd, body)
                dve.wait_ge(s["tail"], 3 * PIECES * (EXPERTS * (rnd + 1) + 1))
                dve.sem_inc(s["round_over"], 1)

            run_rounds(dve, l, one_round)
            dve.sem_inc(s["dve_idle"], 1)

        def shared_tails(l):
            for u in range(3):
                for piece in range(PIECES):
                    matrix_tail(l, u, piece, PIECES * u + piece + 1)

        def pool_tile(t):
            dve.wait_ge(s_mix, t + 1)
            dve.wait_ge(s_par, 16 * 3)
            dve.wait_ge(s_pooled, min(t + 2, TILES))
            for h in HALVES:
                cols = slice(h * BANK, (h + 1) * BANK)
                link(dve.tensor_tensor(pool_tmp, ps_y[:, h, :], par[:, 2, cols], ALU.mult))
                link(dve.scalar_tensor_tensor(out=xn[:, t, cols], in0=xn[:, t, cols], scalar=ALPHA, in1=pool_tmp,
                                              op0=ALU.mult, op1=ALU.add))
            dve.sem_inc(s_mix_used, 1)
            layer_norm(t)

        def last_norm(l):
            dve.wait_ge(s_par, 16 * (5 if l == 0 else 13))
            for t in range(TILES):
                dve.wait_ge(s_acc_in[l][t], 16)
                layer_norm(t)

        shared_tails(0)
        for t in range(TILES):
            dve.wait_ge(s_x[t], 16)
        dve.wait_ge(s_const, 32)
        router_tail(0)
        for t in range(TILES):
            pool_tile(t)

        def dense_tiles(l):
            token_table(l)
            for t in range(TILES):
                rows_tail(S[l]["xhead"], t + 1, S[l]["xtail"], t, P)
                hidden(l, Block(0, t), P)
                hidden_tail(l, Block(0, t), P)
                shared_tile(l, t)

        def token_table(l):
            number = dummy[:, 1:2]
            for t in range(TILES):
                dve.memset(tab[:, t, :, 1], float(t * P))
            dve.memset(tab[:, :, :, 2], 1.0)
            dve.memset(tab[:, :, :, 0], 1.0)
            link(dve.tensor_scalar(most, number, -float(SEQ), None, ALU.add))
            link(dve.tensor_scalar(tab[:, :, :, 0], tab[:, :, :, 0], most, None, ALU.mult))

        dense_tiles(0)
        route(0)
        experts(0)

        def wqkv_tail(k):
            dve.wait_ge(s_qhead, k + 1)
            dve.tensor_tensor(wqkv[:, 1, k, :], wqkv_raw[:, k, :], wqkv[:, 0, k, :].bitcast(F32),
                              ALU.subtract).then_inc(s_qtail, 1)

        dve.wait_ge(s_par, 16 * 5)
        for t in range(TILES):
            dve.wait_ge(s_acc_in[0][t], 16)
            layer_norm(t)
            wqkv_tail(2 * t)
            wqkv_tail(2 * t + 1)

        def rotate(x, t, heads, tmp):
            v = x.rearrange("p (h s j) -> p h s j", s=2, j=HEAD // 2)
            tm = tmp.rearrange("p (s h j) -> p s h j", s=2, h=heads)
            cos = rope[:, t, 0, :].unsqueeze(1).to_broadcast([P, heads, HEAD // 2])
            sin = rope[:, t, 1, :].unsqueeze(1).to_broadcast([P, heads, HEAD // 2])
            for k in HALVES:
                last = dve.tensor_tensor(tm[:, k], v[:, :, k, :], sin, ALU.mult)
            link(last)
            for k in HALVES:
                last = dve.tensor_tensor(v[:, :, k, :], v[:, :, k, :], cos, ALU.mult)
            link(last)
            dve.tensor_tensor(v[:, :, 0, :], v[:, :, 0, :], tm[:, 1], ALU.subtract)
            link(dve.tensor_tensor(v[:, :, 1, :], v[:, :, 1, :], tm[:, 0], ALU.add))

        dve.wait_ge(s_par, 16 * 9)
        dve.tensor_scalar(negsink, negsink, -1.0, None, ALU.mult)
        for t in range(TILES):
            rows_tail(s_axhead, t + 1, s_axtail, t, P)
            dve.wait_ge(s_qkv, t + 1)
            for h in HALVES:
                cols = slice(h * BANK, (h + 1) * BANK)
                dve.tensor_tensor(q_nat[:, t, cols], ps_y[:, h, :], bqkv[:, cols], ALU.add)
            dve.tensor_tensor(k_nat[:, t, :], ps_log[:, 0:KV], bqkv[:, D:D + KV], ALU.add)
            dve.tensor_tensor(v_nat[:, t, :], ps_log[:, KV:2 * KV], bqkv[:, D + KV:QKV], ALU.add).then_inc(s_qkv_used, 1)
            dve.wait_ge(s_qkv_used, t + 1)
            tmp = score[0].rearrange("p a b -> p (a b)")
            rotate(q_nat[:, t, :], t, HEADS, tmp)
            rotate(k_nat[:, t, :], t, KV_HEADS, tmp[:, 0:KV])
            dve.sem_inc(s_roped, 1)

        def wo_tail(k):
            dve.wait_ge(s_wohead, k + 1)
            dve.tensor_tensor(wo[:, 1, k, :], wo_raw[:, k % 3, :], wo[:, 0, k, :].bitcast(F32),
                              ALU.subtract).then_inc(s_wotail, 1)

        def softmax(u):
            n, g = divmod(u, KV_HEADS)
            keys = slice(0 if n else P, 2 * P)
            width = 2 * P if n else P
            dve.wait_ge(s_score, u + 1)
            if u >= 2:
                dve.wait_ge(s_pT, u - 1)
            sc = ps_xT.rearrange("p b (h k) -> p (b h) k", h=2)
            mask = band[:, keys].unsqueeze(1).to_broadcast([P, PER_KV, width])
            buf = score[u % 2][:, :, keys]
            dve.scalar_tensor_tensor(out=buf, in0=sc[:, :, keys], scalar=HEAD ** -0.5, in1=mask,
                                     op0=ALU.mult, op1=ALU.add).then_inc(s_masked, 1)
            dve.wait_ge(s_masked, u + 1)
            link(dve.tensor_reduce(top, buf, AX.X, ALU.max))
            sink = negsink[:, g * PER_KV:(g + 1) * PER_KV]
            link(dve.scalar_tensor_tensor(out=negtop[:, u % 2], in0=top, scalar=-1.0, in1=sink,
                                          op0=ALU.mult, op1=ALU.min))
            dve.tensor_tensor(sink_arg[:, u % 2], negtop[:, u % 2], sink, ALU.subtract).then_inc(s_negtop, 1)

        def previous_out(u):
            if u // KV_HEADS:
                dve.wait_ge(s_pT, u + 1)
                dve.wait_ge(s_pv, u)
                dve.tensor_copy(pT[:, 0], ps_log.rearrange("p (h t) -> p h t", h=PER_KV)).then_inc(s_pT_prev, 1)

        def divide(u):
            n, g = divmod(u, KV_HEADS)
            dve.wait_ge(s_exp, u + 1)
            link(dve.tensor_tensor(total[:, u % 2], total[:, u % 2], sink_exp[:, u % 2], ALU.add))
            link(dve.reciprocal(inverse[:, u % 2], total[:, u % 2]))
            dve.wait_ge(s_pv, u + 1)
            dve.tensor_tensor(q_nat[:, n, g * 256:(g + 1) * 256].rearrange("p (h j) -> p h j", h=PER_KV),
                              ps_list[:, 0:256].rearrange("p (h j) -> p h j", h=PER_KV),
                              inverse[:, u % 2].unsqueeze(2).to_broadcast([P, PER_KV, HEAD]),
                              ALU.mult).then_inc(s_o, 1)

        def attention_tile(n):
            rows_tail(s_axhead, TILES + n + 1, s_axtail, n, P)
            dve.wait_ge(s_wo, n + 1)
            x = xn[:, n, :].rearrange("p (b n) -> p b n", b=2)
            for h in HALVES:
                last = dve.scalar_tensor_tensor(out=x[:, h], in0=x[:, h], scalar=ALPHA, in1=ps_y[:, h],
                                                op0=ALU.mult, op1=ALU.add)
            last.then_inc(s_wo_used, 1)
            dve.wait_ge(s_wo_used, n + 1)
            link(dve.tensor_tensor(xn[:, n, :], xn[:, n, :], bo, ALU.add))
            layer_norm(n)

        dve.wait_ge(s_band, 16)
        for u in range(UNITS + 1):
            if u < UNITS:
                softmax(u)
            if u:
                previous_out(u - 1)
                divide(u - 1)
                if u % KV_HEADS == 0:
                    if u == KV_HEADS:
                        dve.wait_ge(s_par, 16 * 11)
                    attention_tile(u // KV_HEADS - 1)
            if u < 4:
                wo_tail(2 * u)
                wo_tail(2 * u + 1)
        shared_tails(1)
        router_tail(1)
        dense_tiles(1)
        route(1)
        experts(1)
        last_norm(1)

    @block.tensor
    def _(pe):
        def product(out_ap, stationary, moving, first, last):
            for k, (a, b) in enumerate(PASSES):
                mm = pe.matmul(out_ap, stationary(a), moving(b), start=first and k == 0,
                               stop=last and k == len(PASSES) - 1)
            return mm

        def transpose_rows(src, m):
            for k in range(CHUNKS):
                mm = pe.transpose(xT_ps(m)[:, k // 4, k % 4, :], src[0:m, k * P:(k + 1) * P], ident[0:m, 0:m])
            return mm

        def first_product(b, m, w1_slot):
            w = split[:, 2 * w1_slot * UNIT:2 * (w1_slot + 2) * UNIT].rearrange(
                "p (m s c n) -> p s c m n", m=2, s=2, c=CHUNKS)
            for k in range(CHUNKS):
                mm = product(ps_h[0:m].rearrange("p (m n) -> p m n", m=2), lambda a: xT[:, b % 2, a, k, 0:m],
                             lambda a: w[:, a, k], k == 0, k == CHUNKS - 1)
            return mm

        def transpose_hidden(m):
            for j in range(FC):
                mm = pe.transpose(ps_hT[:, j * m:(j + 1) * m], h_sb[0:m, j, :], ident[0:m, 0:m])
            return mm

        def second_product(m, slot):
            w = split_slot(slot).rearrange("p s (j n) -> p s j n", j=FC)
            for h in HALVES:
                for j in range(FC):
                    mm = product(ps_y[0:m, h, :], lambda a: hT[:, a, j, 0:m],
                                 lambda a: w[:, a, j, h * BANK:(h + 1) * BANK], j == 0, j == FC - 1)
            return mm

        def dense(l):
            s = S[l]

            def finish(t):
                pe.wait_ge(s["htail"], t + 1)
                pe.wait_ge(s["tail"], 3 * PIECES)
                if t:
                    pe.wait_ge(s["yout"], t)
                second_product(P, 2).then_inc(s["m2"], 1)

            for t in range(TILES):
                pe.wait_ge(s["xp"], t + 1)
                if t:
                    pe.wait_ge(s["xtail"], t)
                transpose_rows(xp, P).then_inc(s["xTready"], 1)
                pe.wait_ge(s["xtail"], t + 1)
                pe.wait_ge(s_rw_tail, l + 1)
                for k in range(CHUNKS):
                    mm = product(ps_log[:, t * EXPERTS:(t + 1) * EXPERTS], lambda a: xT[:, t % 2, a, k, :],
                                 lambda a: rw[:, a, k, :], k == 0, k == CHUNKS - 1)
                mm.then_inc(s["logits"], 1)
                pe.wait_ge(s["tail"], 2 * PIECES)
                first_product(t, P, 0).then_inc(s["m1"], 1)
                pe.wait_ge(s["hidden"], t + 1)
                transpose_hidden(P).then_inc(s["hTready"], 1)
                finish(t)

        def rank(l):
            s = S[l]
            pe.wait_ge(s_moe_const, 32 * (l + 1))
            pe.wait_ge(s["order"], 2)
            pe.wait_ge(s["chosen"], 1)
            for t in range(TILES):
                for k in range(t + 1):
                    pe.matmul(ps_list[:, t * EXPERTS:(t + 1) * EXPERTS], order[:, 0 if k == t else 1, :],
                              chosen[:, k, :], start=(k == 0), stop=(k == t))
            for k in range(TILES):
                mm = pe.matmul(ps_list[:, 256:256 + EXPERTS], order[:, 1, :], chosen[:, k, :],
                               start=(k == 0), stop=(k == TILES - 1))
            mm.then_inc(s["ranked"], 1)

        def experts(l):
            s = S[l]

            def body(b, valid):
                if valid(-1):
                    n = b.after(-1)
                    pe.wait_ge(s["hidden"], n.times(1, 1))
                    pe.wait_ge(s["htail"], n.times(1))
                    transpose_hidden(CAP).then_inc(s["hTready"], 1)
                if valid(1):
                    n = b.after(1)
                    pe.wait_ge(s_xg[l][n.r % 2], 16 * (2 * (n.q - 1) + n.r // 2 + 1))
                    pe.wait_ge(s["xtail"], n.times(1))
                    transpose_rows(xg[n.r % 2], CAP).then_inc(s["xTready"], 1)
                if valid(2):
                    n = b.after(2)
                    pe.wait_ge(s["oh"], n.times(1, 1 - 4))
                    if not (isinstance(n.q, int) and n.q == 1 and n.r == 0):
                        pe.wait_ge(s["index"], n.times(1, -4))
                    for t in range(TILES):
                        mm = pe.matmul(ps_list[0:CAP, 0:TAB], oh[:, n.r % 2, t, :],
                                       tab[:, t, bass.ds(n.expert, 1), :].rearrange("p e k -> p (e k)"),
                                       start=(t == 0), stop=(t == TILES - 1))
                    mm.then_inc(s["listed"], 1)
                if valid(0):
                    pe.wait_ge(s["xtail"], b.times(1, 1))
                    pe.wait_ge(s["tail"], b.times(3 * PIECES, PIECES * (-12 + 3 + 2)))
                    slot, _ = weight_unit(b, 0)
                    first_product(b.r, CAP, slot).then_inc(s["m1"], 1)
                if valid(-1):
                    n = b.after(-1)
                    pe.wait_ge(s["htail"], n.times(1, 1))
                    pe.wait_ge(s["tail"], n.times(3 * PIECES, PIECES * (-12 + 3 + 3)))
                    pe.wait_ge(s["yout"], n.times(1))
                    slot, _ = weight_unit(n, 2)
                    second_product(CAP, slot).then_inc(s["m2"], 1)

            def one_round(rnd):
                run_steps(pe, rnd, body)
                pe.wait_ge(s["m2"], EXPERTS * (rnd + 1) + 4)

            run_rounds(pe, l, one_round)
            pe.sem_inc(s["pe_idle"], 1)

        pe.wait_ge(s_const, 32)
        pe.wait_ge(s_pool_w, 32)

        def pool_rows(t):
            pe.wait_ge(s_x[t], 16)
            if t:
                pe.wait_ge(s_pooled_sb, t)
            for k in range(CHUNKS):
                g = k * P // GROUP_CH
                dst = ps_xT[:, k // 4, (k % 4) * P:(k % 4 + 1) * P]
                mm = pe.matmul(dst, xn[:, t, k * P:(k + 1) * P], pool_band[:, g, min(t, 1), :],
                               start=True, stop=(t == 0))
                if t:
                    mm = pe.matmul(dst, xn[:, t - 1, k * P:(k + 1) * P], pool_band[:, g, 2, :],
                                   start=False, stop=True)
            mm.then_inc(s_pooled, 1)

        def mix(t):
            pe.wait_ge(s_pooled_sb, t + 1)
            if t:
                pe.wait_ge(s_mix_used, t)
            for g in range(len(WINDOWS)):
                dst = ps_y[:, g // 2, (g % 2) * GROUP_CH:(g % 2 + 1) * GROUP_CH]
                for k in range(2):
                    mm = pe.matmul(dst, pooled[:, 2 * g + k, :], pool_w[:, g, k, :], start=(k == 0), stop=(k == 1))
            mm.then_inc(s_mix, 1)

        for t in range(TILES + 1):
            if t < TILES:
                pool_rows(t)
            if t:
                mix(t - 1)
        dense(0)
        rank(0)
        experts(0)

        for t in range(TILES + 1):
            if t < TILES:
                pe.wait_ge(s_norm, 2 * TILES - TILES + t + 1)
                if t:
                    pe.wait_ge(s_axtail, t)
                transpose_rows(xn[:, t, :], P).then_inc(s_axT, 1)
            if t:
                n = t - 1
                pe.wait_ge(s_axtail, n + 1)
                pe.wait_ge(s_qtail, CHUNKS)
                if n:
                    pe.wait_ge(s_qkv_used, n)
                for b in range(3):
                    dst = ps_y[:, b, :] if b < 2 else ps_log
                    for k in range(CHUNKS):
                        mm = product(dst, lambda a: xT[:, n % 2, a, k, :],
                                     lambda a: wqkv[:, a, k, b * BANK:(b + 1) * BANK], k == 0, k == CHUNKS - 1)
                mm.then_inc(s_qkv, 1)

        def scores(u):
            n, g = divmod(u, KV_HEADS)
            pe.wait_ge(s_roped, TILES)
            if u:
                pe.wait_ge(s_qkT_sb, u)
            if u > KV_HEADS:
                pe.wait_ge(s_wo_used, (u - 1) // KV_HEADS)
            for h in range(PER_KV):
                pe.transpose(ps_hT[0:HEAD, h * P:(h + 1) * P],
                             q_nat[:, n, (g * PER_KV + h) * HEAD:(g * PER_KV + h + 1) * HEAD], ident[:, :])
            pe.transpose(ps_y[0:HEAD, 0, 0:P], k_nat[:, n, g * HEAD:(g + 1) * HEAD], ident[:, :]).then_inc(s_qkT, 1)
            pe.wait_ge(s_qkT_sb, u + 1)
            if u:
                pe.wait_ge(s_masked, u)
            for h in range(PER_KV):
                for b in ((1, 0) if n else (1,)):
                    dst = ps_xT[:, h // 2, (h % 2) * 2 * P + b * P:(h % 2) * 2 * P + (b + 1) * P]
                    mm = pe.matmul(dst, qT[u % 2][0:HEAD, h, :], kT[0:HEAD, g, (n - 1 + b) % 2, :], start=True, stop=True)
            mm.then_inc(s_score, 1)

        def values(u):
            n, g = divmod(u, KV_HEADS)
            pe.wait_ge(s_exp, u + 1)
            if u:
                pe.wait_ge(s_pT_cur, u)
                if prev_count(u):
                    pe.wait_ge(s_pT_prev, prev_count(u))
            for b in ((1, 0) if n else (1,)):
                for h in range(PER_KV):
                    dst = (ps_h if b else ps_log)[:, h * P:(h + 1) * P]
                    mm = pe.transpose(dst, score[u % 2][:, h, b * P:(b + 1) * P], ident[:, :])
            mm.then_inc(s_pT, 1)
            pe.wait_ge(s_pT_cur, u + 1)
            if n:
                pe.wait_ge(s_pT_prev, prev_count(u + 1))
            if u:
                pe.wait_ge(s_o, u)
            for h in range(PER_KV):
                blocks = (1, 0) if n else (1,)
                for b in blocks:
                    mm = pe.matmul(ps_list[:, h * HEAD:(h + 1) * HEAD], pT[:, b, h, :],
                                   v_nat[:, n - 1 + b, g * HEAD:(g + 1) * HEAD],
                                   start=(b == 1), stop=(b == blocks[-1]))
            mm.then_inc(s_pv, 1)

        def project(n):
            pe.wait_ge(s_o, KV_HEADS * (n + 1))
            pe.wait_ge(s_masked, min(KV_HEADS * (n + 1) + 1, UNITS))
            transpose_rows(q_nat[:, n, :], P).then_inc(s_axT, 1)
            pe.wait_ge(s_axtail, TILES + n + 1)
            pe.wait_ge(s_wotail, CHUNKS)
            if n:
                pe.wait_ge(s_wo_used, n)
            for b in HALVES:
                for k in range(CHUNKS):
                    mm = product(ps_y[:, b, :], lambda a: xT[:, n % 2, a, k, :],
                                 lambda a: wo[:, a, k, b * BANK:(b + 1) * BANK], k == 0, k == CHUNKS - 1)
            mm.then_inc(s_wo, 1)

        for u in range(UNITS + 1):
            if u < UNITS:
                if u and u % KV_HEADS == 1 and u > 1:
                    pe.wait_ge(s_axtail, TILES + u // KV_HEADS)
                scores(u)
            if u:
                values(u - 1)
                if u % KV_HEADS == 0:
                    project(u // KV_HEADS - 1)
        dense(1)
        rank(1)
        experts(1)

    ctx.close()


def kernel(**inputs):
    import concourse.bacc as bacc
    from concourse.bass_utils import run_bass_kernel_spmd

    names = ("x", "ln_gain", "ln_bias", "pool_w", "pool_scale", "attn_wqkv", "attn_bqkv", "attn_sinks", "attn_wo",
             "attn_bo", "router_w", "router_bias", "expert_w1", "expert_w3", "expert_w2", "shared_w1", "shared_w3",
             "shared_w2")
    nc = bacc.Bacc("TRN2", target_bir_lowering=False, num_devices=1)
    arrays, ins, consts = {}, {}, {}
    for name in names:
        a = np.ascontiguousarray(inputs[name])
        arrays[f"in_{name}"] = a
        ins[name] = nc.dram_tensor(f"in_{name}", a.shape, mybir.dt.from_np(a.dtype), kind="ExternalInput").ap()
    for name, a in shape_constants().items():
        a = np.ascontiguousarray(a)
        arrays[f"const_{name}"] = a
        consts[name] = nc.dram_tensor(f"const_{name}", a.shape, mybir.dt.from_np(a.dtype), kind="ExternalInput").ap()
    out = nc.dram_tensor("out", (1, SEQ, D), F32, kind="ExternalOutput").ap()
    build(nc, ins, consts, out)
    r = run_bass_kernel_spmd(nc, [arrays], core_ids=[0])
    return r.results[0]["out"]
```

```python
import math
from contextlib import ExitStack

import numpy as np

import concourse.bass as bass
from concourse import mybir

F32 = mybir.dt.float32
F32R = mybir.dt.float32r
BF16 = mybir.dt.bfloat16
I32 = mybir.dt.int32
U32 = mybir.dt.uint32
ALU = mybir.AluOpType
ACT = mybir.ActivationFunctionType
AX = mybir.AxisListType

P = 128
SEQ = 512
D = 1024
TILES = SEQ // P
CHUNKS = D // P
LAYERS = 2
WINDOWS = (2, 4, 8, 16)
GROUP_CH = D // len(WINDOWS)
HEAD = 64
HEADS = D // HEAD
KV_HEADS = 4
PER_KV = HEADS // KV_HEADS
KV = KV_HEADS * HEAD
QKV = D + 2 * KV
EXPERTS = 64
TOP_K = 8
EXPERT_GROUPS = 8
PER_GROUP = EXPERTS // EXPERT_GROUPS
TOP_GROUPS = 4
FF = 256
FC = FF // P
ROUTED_SCALE = 2.5
EPS = 1e-5
ALPHA = (2 * LAYERS) ** 0.25
CAP = 96
ROUNDS = -(-SEQ // CAP)
FAR = -4096.0
LOW = -1.0e30
TAKEN = -3.0e38
FILLER = -2.0e38

UNIT = CHUNKS * FF
SLOTS = 6
PIECES = 2
PIECE = UNIT // PIECES
TAB = 6
BANK = 512


class Block:

    def __init__(self, q, r, expert=None):
        self.q, self.r, self.expert = q + r // 4, r % 4, expert

    def after(self, k):
        return Block(self.q, self.r + k, self.expert + k)

    def times(self, k, plus=0):
        return 4 * k * self.q + (k * self.r + plus)


def shape_constants():
    t = np.arange(P)
    pool = np.zeros((P, len(WINDOWS), 3, P), np.float32)
    for g, w in enumerate(WINDOWS):
        for kind in range(3):
            first = 0 if kind == 0 else P
            dst = first + t[None, :]
            src = t[:, None] + (first if kind < 2 else 0)
            inside = (src <= dst) & (src > dst - w)
            m = np.where(inside, 1.0 / np.minimum(dst + 1, w), 0.0)
            if kind < 2:
                m = m - (src == dst)
            pool[:, g, kind, :] = m
    slots = np.broadcast_to(np.arange(CAP, dtype=np.float32)[None, :], (P, CAP))
    dummy = np.stack([-(SEQ + t), SEQ + t], 1).astype(np.float32)
    inv = (10000.0 ** (-np.arange(0, HEAD, 2, dtype=np.float32) / np.float32(HEAD))).astype(np.float32)
    ang = (np.arange(SEQ, dtype=np.float32)[:, None] * inv[None, :]).astype(np.float32)
    rope = np.stack([np.cos(ang), np.sin(ang)], 1).astype(np.float32)
    rope = rope.reshape(TILES, P, 2, HEAD // 2).transpose(1, 0, 2, 3)
    ki = np.arange(2 * P)[None, :]
    band = np.where((ki > t[:, None]) & (ki <= t[:, None] + P), 0.0, LOW).astype(np.float32)
    return {
        "ident": np.eye(P, dtype=np.float32),
        "pool_band": pool,
        "slots": np.ascontiguousarray(slots),
        "dummy": dummy,
        "rope": np.ascontiguousarray(rope),
        "band": band,
    }


def build(nc, i, c, out):
    ctx = ExitStack()

    def sb(name, shape, dt=F32):
        return ctx.enter_context(nc.sbuf_tensor(name, shape, dt))

    def sem(name):
        return ctx.enter_context(nc.semaphore(name))

    raw = sb("raw", [P, SLOTS * UNIT])
    split = sb("split", [P, 2 * SLOTS * UNIT], F32R)
    xT = sb("xT", [P, 2, 2, CHUNKS, P], F32R)
    xn = sb("xn", [P, TILES, D])
    par = sb("par", [P, 3, D])
    rw = sb("rw", [P, 2, CHUNKS, EXPERTS], F32R)
    hT = sb("hT", [P, 2, FC, P], F32R)
    ident = sb("ident", [P, P])
    work = sb("work", [P, 3360])
    psum = ctx.enter_context(nc.psum_tensor("psum", [P, 8, BANK], F32))
    rows = nc.dram_tensor("rows", [SEQ, D], F32).ap()
    sums = [nc.dram_tensor(f"sums{l}", [SEQ + CAP, D], F32).ap() for l in range(LAYERS)]

    parf = par[:].rearrange("p a d -> p (a d)")

    def at(t, start, *dims, dt=F32):
        n = 1
        for d in dims:
            n *= d
        words = n * (2 if dt == BF16 else 4) // 4
        v = t[:, start:start + words]
        if dt != F32:
            v = v.bitcast(dt)
        if len(dims) == 1:
            return v
        names = "abcd"[:len(dims)]
        return v.rearrange(f"p ({' '.join(names)}) -> p {' '.join(names)}", **dict(zip(names, dims)))

    h_sb = at(work, 0, FC, P)
    oh = at(work, 256, 2, TILES, CAP, dt=BF16)
    tab = at(work, 640, TILES, EXPERTS, TAB, dt=BF16)
    ranks = at(work, 1408, TILES, EXPERTS)
    slots = at(work, 1664, CAP)
    order = at(work, 1760, 2, P, dt=BF16)
    xp = at(work, 1888, D)
    rw_raw = at(work, 0, CHUNKS, EXPERTS)
    k_nat = at(work, 0, TILES, KV)
    v_nat = at(work, 1024, TILES, KV)
    score = [at(work, 2048, PER_KV, 2 * P), at(raw, 7168, PER_KV, 2 * P)]
    router_bias = at(work, 3072, EXPERTS)
    negsink = at(work, 3136, HEADS)
    dummy = at(work, 3152, 2)
    stats = at(work, 3154, 2, 6)
    mean_var = at(work, 3166, 2)
    power = at(work, 3168, 3)
    slot_row = at(work, 3171, 1)
    index = work[:, 3172:3176].bitcast(I32)
    gate = at(work, 3176, 4)
    index_out = work[:, 3180:3184].bitcast(I32)
    most = at(work, 3184, 1)
    most_int = work[:, 3185:3186].bitcast(I32)
    top = at(work, 3188, PER_KV)
    negtop = at(work, 3192, 2, PER_KV)
    sink_arg = at(work, 3200, 2, PER_KV)
    total = at(work, 3208, 2, PER_KV)
    sink_exp = at(work, 3216, 2, PER_KV)
    inverse = at(work, 3224, 2, PER_KV)
    band = at(work, 3232, 2 * P, dt=BF16)
    prob = at(parf, 2048, TILES, EXPERTS)
    sel = at(parf, 2304, TILES, EXPERTS)
    rest = at(parf, 2560, TILES, EXPERTS)
    chosen = at(parf, 2816, TILES, EXPERTS, dt=BF16)
    gsum = at(parf, 2944, TILES)
    group_top = at(work, 256, TILES, EXPERT_GROUPS, 8)
    gext = at(work, 512, TILES, EXPERT_GROUPS + 4)
    gtop = at(work, 560, TILES, 8)
    etop = at(work, 592, TILES, 8)
    xg = [xn[:, b, :] for b in range(2)]
    yo = [xn[:, 2 + b, :] for b in range(2)]
    pool_band = at(raw, 8192, len(WINDOWS), 3, P)
    pool_w = at(raw, 9728, len(WINDOWS), 2, GROUP_CH)
    pooled = at(work, 1888, CHUNKS, P)
    wqkv_raw = at(raw, 0, CHUNKS, QKV)
    wqkv = split[:, :].rearrange("p (s c n) -> p s c n", s=2, c=CHUNKS)
    wo_raw = at(raw, 0, 3, D)
    wo = split[:, 4 * UNIT:4 * UNIT + 2 * CHUNKS * D].rearrange("p (s c n) -> p s c n", s=2, c=CHUNKS)
    band_raw = at(raw, 3072, 2 * P)
    kT = at(raw, 4096, KV_HEADS, 2, P)
    qT = [at(raw, 5120 + 512 * b, PER_KV, P) for b in range(2)]
    pT = at(raw, 6144, 2, PER_KV, P)
    q_nat = at(raw, 8192, TILES, D)
    bqkv = at(parf, 0, QKV)
    rope = at(parf, QKV, TILES, 2, HEAD // 2)
    bo = par[:, 2, :]

    def raw_slot(slot):
        return raw[:, slot * UNIT:(slot + 1) * UNIT]

    def split_slot(slot):
        return split[:, 2 * slot * UNIT:2 * (slot + 1) * UNIT].rearrange("p (s n) -> p s n", s=2)

    ps_xT = psum[:, 0:2, :]
    ps_h = psum[:, 2, :]
    ps_hT = psum[:, 3, :]
    ps_list = psum[:, 4, :]
    ps_y = psum[:, 5:7, :]
    ps_log = psum[:, 7, :]
    ps_kT = psum[0:HEAD, 4, 256:256 + P]

    def in_chunks(banks, m=P):
        return banks[:, :, 0:4 * m].rearrange("p b (c t) -> p b c t", c=4)

    def qkv_ps(t):
        return psum[:, 5:8, :] if t % 2 == 0 else psum[:, 2:5, :]

    s_const = sem("s_const")
    s_x = [sem(f"s_x{t}") for t in range(TILES)]
    s_pool_band = sem("s_pool_band")
    s_pool_w = sem("s_pool_w")
    s_pool_scale = sem("s_pool_scale")
    s_pool_scaled = sem("s_pool_scaled")
    s_par = sem("s_par")
    s_dve = sem("s_dve")
    s_power = sem("s_power")
    s_pool_waited = sem("s_pool_waited")
    s_pooled = sem("s_pooled")
    s_pooled_sb = sem("s_pooled_sb")
    s_mix = sem("s_mix")
    s_mix_used = sem("s_mix_used")
    s_var = sem("s_var")
    s_vareps = sem("s_vareps")
    s_rstd = sem("s_rstd")
    s_norm = sem("s_norm")
    s_rw_in = sem("s_rw_in")
    s_rw_head = sem("s_rw_head")
    s_rw_tail = sem("s_rw_tail")
    s_moe_const = sem("s_moe_const")
    per_layer = ("xp", "rows_out", "logits", "prob", "order", "chosen", "ranked", "most", "tabled",
                 "head", "tail", "xTready", "xhead", "xtail", "m1", "silu", "hidden", "hTready", "hhead",
                 "htail", "m2", "yout", "oh", "listed", "slotrow", "index", "idxcopy", "slots", "round_over",
                 "pe_idle", "loads_over")
    S = [{n: sem(f"s_{n}{l}") for n in per_layer} for l in range(LAYERS)]
    s_w = [[sem(f"s_w{l}_{k}") for k in range(SLOTS)] for l in range(LAYERS)]
    s_xg = [[sem(f"s_xg{l}_{b}") for b in range(2)] for l in range(LAYERS)]
    s_scat = [[sem(f"s_scat{l}_{b}") for b in range(2)] for l in range(LAYERS)]
    s_acc_out = [sem(f"s_acc_out{l}") for l in range(LAYERS)]
    s_acc_in = [[sem(f"s_acc_in{l}_{t}") for t in range(TILES)] for l in range(LAYERS)]
    s_out = sem("s_out")
    s_wqkv = [sem(f"s_wqkv{k}") for k in range(CHUNKS)]
    s_qhead = sem("s_qhead")
    s_qtail = sem("s_qtail")
    s_axT = sem("s_axT")
    s_axhead = sem("s_axhead")
    s_axtail = sem("s_axtail")
    s_qkv = sem("s_qkv")
    s_qkv_used = sem("s_qkv_used")
    s_roped = sem("s_roped")
    s_wo_in = [sem(f"s_wo_in{k}") for k in range(3)]
    s_wohead = sem("s_wohead")
    s_wotail = sem("s_wotail")
    s_qkT = sem("s_qkT")
    s_qkT_sb = sem("s_qkT_sb")
    s_score = sem("s_score")
    s_masked = sem("s_masked")
    s_negtop = sem("s_negtop")
    s_exp = sem("s_exp")
    s_inv = sem("s_inv")
    s_pT = sem("s_pT")
    s_pT_cur = sem("s_pT_cur")
    s_pT_prev = sem("s_pT_prev")
    s_pv = sem("s_pv")
    s_o = sem("s_o")
    s_wo = sem("s_wo")
    s_wo_used = sem("s_wo_used")
    s_band = sem("s_band")
    s_band_copied = sem("s_band_copied")

    UNITS = TILES * KV_HEADS
    HALVES = (0, 1)
    PASSES = ((0, 0), (0, 1), (1, 0))

    def projected(i):
        return (i - 6) // KV_HEADS if i >= 6 and i % KV_HEADS == 2 else None

    def prev_count(n):
        return max(0, n - KV_HEADS)

    def run_steps(eng, rnd, body):
        base = EXPERTS // 4 * rnd + 1

        def peeled(s):
            body(Block(base, s, s), lambda k: 0 <= s + k < EXPERTS)

        for s in range(-3, 5):
            peeled(s)
        with eng.Fori(0, 14) as q:
            for r in range(4):
                body(Block(base + 1 + q, 1 + r, 4 * q + (5 + r)), lambda k: True)
        for s in range(61, 66):
            peeled(s)

    def run_rounds(eng, l, one_round):
        one_round(0)
        eng.wait_ge(S[l]["most"], 1)
        most_tokens = eng.value_load(most_int[0:1, 0:1], min_val=0, max_val=SEQ)
        with eng.Fori(1, ROUNDS) as rnd:
            with eng.If(most_tokens > rnd * CAP):
                one_round(rnd)
            eng.nop()

    def first_of_all(b):
        return isinstance(b.q, int) and b.times(1) == 4

    def split_early(b):
        return isinstance(b.q, int) and b.times(1) in (4, 5)

    def weight_unit(b, u):
        k = 3 * (b.r + 1) + u
        return k % SLOTS, 2 * (b.q - 1) + k // SLOTS + 1

    block = ctx.enter_context(nc.Block())

    @block.sync
    def _(sp):
        def load_par(vectors):
            for dst, src in vectors:
                sp.dma_start(dst, src).then_inc(s_par, 16)

        def bc(v):
            return v.partition_broadcast(P)

        def expert_matrix(l, n, u, slot):
            if u < 2:
                w = i["expert_w1" if u == 0 else "expert_w3"]
            else:
                w = i["expert_w2"]
            src = w[l].rearrange("e (p a) f -> p e (a f)", p=P)[:, bass.ds(n, 1), :]
            return sp.dma_start(raw_slot(slot).rearrange("p (e n) -> p e n", e=1), src)

        def shared_matrix(l, u):
            w = i[("shared_w1", "shared_w3", "shared_w2")[u]][l]
            sp.dma_start(raw_slot(u), w.rearrange("(p a) f -> p (a f)", p=P)).then_inc(s_w[l][u], 16)

        def moe_consts(l):
            sp.dma_start(slots, c["slots"]).then_inc(s_moe_const, 16)
            sp.dma_start(router_bias, bc(i["router_bias"][l])).then_inc(s_moe_const, 16)

        def experts(l):
            def one(b, u, e, wait):
                slot, _ = weight_unit(b, u)
                if wait:
                    sp.wait_ge(S[l]["tail"], b.times(3 * PIECES, PIECES * (u - 14)))
                expert_matrix(l, e, u, slot).then_inc(s_w[l][slot], 16)

            def one_round(rnd):
                base = 16 * rnd + 1
                if isinstance(rnd, int):
                    first = 4
                    for n in range(1, first):
                        for u in range(3):
                            one(Block(1, n), u, n, True)
                    with sp.Fori(1, EXPERTS // 4) as q:
                        for r in range(4):
                            for u in range(3):
                                one(Block(base + q, r), u, 4 * q + r, True)
                else:
                    with sp.Fori(0, EXPERTS // 4) as q:
                        for r in range(4):
                            for u in range(3):
                                one(Block(base + q, r), u, 4 * q + r, True)
                sp.wait_ge(S[l]["tail"], 3 * PIECES * (EXPERTS * (rnd + 1) + 1))
                sp.sem_inc(S[l]["loads_over"], 1)

            run_rounds(sp, l, one_round)

        def load_x(t):
            sp.dma_start(xn[:, t, :], i["x"][0, t * P:(t + 1) * P, :]).then_inc(s_x[t], 16)

        load_x(0)
        sp.dma_start(pool_band, c["pool_band"]).then_inc(s_pool_band, 16)
        sp.dma_start(pool_w, i["pool_w"][0].rearrange("g (k p) n -> p g k n", p=P)).then_inc(s_pool_w, 16)
        sp.dma_start(par[:, 2, :], bc(i["pool_scale"][0])).then_inc(s_pool_scale, 16)
        load_x(1)
        load_par([(par[:, 0, :], bc(i["ln_gain"][0, 0])), (par[:, 1, :], bc(i["ln_bias"][0, 0]))])
        load_x(2)
        sp.dma_start(ident[:], c["ident"]).then_inc(s_const, 16)
        sp.dma_start(dummy, c["dummy"]).then_inc(s_const, 16)
        load_x(3)
        sp.dma_start(rw_raw, i["router_w"][0].rearrange("(p a) e -> p a e", p=P)).then_inc(s_rw_in, 16)
        moe_consts(0)
        for u in range(3):
            shared_matrix(0, u)
        expert_matrix(0, 0, 0, 3).then_inc(s_w[0][3], 16)
        sp.wait_ge(s_norm, 1 * TILES)
        for u in (1, 2):
            expert_matrix(0, 0, u, 3 + u).then_inc(s_w[0][3 + u], 16)
        load_par([(par[:, 0, :], bc(i["ln_gain"][0, 1])), (par[:, 1, :], bc(i["ln_bias"][0, 1]))])
        experts(0)

        for k in range(CHUNKS):
            if k == CHUNKS // 2:
                for t in range(TILES):
                    sp.wait_ge(s_acc_in[0][t], 16)
            sp.dma_start(wqkv_raw[:, k, :], i["attn_wqkv"][0, k * P:(k + 1) * P, :]).then_inc(s_wqkv[k], 16)
        sp.wait_ge(s_norm, 2 * TILES)
        load_par([(bqkv, bc(i["attn_bqkv"][0])), (rope, c["rope"]), (bo, bc(i["attn_bo"][0])),
                  (negsink, bc(i["attn_sinks"][0]))])
        sp.wait_ge(s_qtail, CHUNKS)
        sp.dma_start(band_raw, c["band"]).then_inc(s_band, 16)
        for k in range(CHUNKS):
            if k >= 3:
                sp.wait_ge(s_wotail, k - 2)
            sp.dma_start(wo_raw[:, k % 3, :], i["attn_wo"][0, k * P:(k + 1) * P, :]).then_inc(s_wo_in[k % 3], 16)
        sp.wait_ge(s_roped, TILES)
        load_par([(par[:, 0, :], bc(i["ln_gain"][1, 0])), (par[:, 1, :], bc(i["ln_bias"][1, 0]))])
        sp.wait_ge(s_wotail, CHUNKS)
        sp.wait_ge(s_band_copied, 1)
        for u in range(2):
            shared_matrix(1, u)
        sp.wait_ge(s_o, UNITS)
        sp.wait_ge(s_pv, UNITS)
        shared_matrix(1, 2)
        sp.dma_start(rw_raw, i["router_w"][1].rearrange("(p a) e -> p a e", p=P)).then_inc(s_rw_in, 16)
        moe_consts(1)
        expert_matrix(1, 0, 0, 3).then_inc(s_w[1][3], 16)
        sp.wait_ge(s_axT, 2 * TILES)
        for u in (1, 2):
            expert_matrix(1, 0, u, 3 + u).then_inc(s_w[1][3 + u], 16)
        sp.wait_ge(s_norm, 3 * TILES)
        load_par([(par[:, 0, :], bc(i["ln_gain"][1, 1])), (par[:, 1, :], bc(i["ln_bias"][1, 1]))])
        experts(1)
        for t in range(TILES):
            sp.wait_ge(s_norm, 3 * TILES + t + 1)
            sp.dma_start(out[0, t * P:(t + 1) * P, :], xn[:, t, :]).then_inc(s_out, 16)
        sp.wait_ge(s_out, 16 * TILES)

    @block.gpsimd
    def _(pool):
        pool.memset(power[:, 0:1], -0.5).then_inc(s_power, 1)
        pool.wait_ge(s_power, 1)

        def hold_waits():
            pool.sem_inc(s_pool_waited, 1)

        def rstd(n):
            pool.wait_ge(s_var, n + 1)
            pool.tensor_scalar(power[:, 1:2], mean_var[:, 1:2], EPS, None, ALU.add).then_inc(s_vareps, 1)
            pool.wait_ge(s_vareps, n + 1)
            pool.tensor_tensor(power[:, 2:3], power[:, 1:2], power[:, 0:1], ALU.pow).then_inc(s_rstd, 1)

        def rows_and_sums(l):
            for t in range(TILES):
                rstd(2 * l * TILES + t)
            for t in range(TILES):
                store_rows(l, t)

        def store_rows(l, t):
            pool.wait_ge(S[l]["xp"], t + 1)
            pool.dma_start(rows[t * P:(t + 1) * P, :], xp).then_inc(S[l]["rows_out"], 16)

        def order_matrices(l):
            if l:
                pool.wait_ge(s_o, UNITS)
            pool.memset(order, 1.0).then_inc(S[l]["order"], 1)
            pool.wait_ge(S[l]["order"], 1)
            pool.affine_select(out=order[:, 0, :], in_=order[:, 0, :], compare_op=ALU.is_gt, fill=0.0, base=0,
                               pattern=[[1, P]], channel_multiplier=-1).then_inc(S[l]["order"], 1)

        def store_sums(l):
            for t in range(TILES):
                pool.wait_ge(S[l]["yout"], t + 1)
                pool.dma_start(sums[l][t * P:(t + 1) * P, :], xn[:, t, :]).then_inc(s_acc_out[l], 16)
                if t == 0:
                    pool.dma_start(sums[l][SEQ:SEQ + CAP, :], xn[0:CAP, 0, :]).then_inc(s_acc_out[l], 16)
            pool.wait_ge(S[l]["rows_out"], 16 * TILES)
            pool.wait_ge(s_acc_out[l], 16 * (TILES + 1))

        def experts(l):
            s = S[l]

            def body(b, valid):
                if valid(2):
                    n = b.after(2)
                    pool.wait_ge(s["index"], n.times(1, 1 - 4))
                    pool.wait_ge(s["xTready"], n.times(1, -1))
                    hold_waits()
                    pool.indirect_dma_start(
                        xg[n.r % 2][0:CAP, :], None, rows[:, :],
                        bass.IndirectOffsetOnAxis(ap=index[0:CAP, n.r:n.r + 1].bitcast(U32), axis=0),
                        bounds_check=SEQ - 1, oob_is_err=False).then_inc(s_xg[l][n.r % 2], 16)
                if valid(0):
                    pool.wait_ge(s["index"], b.times(1, 1 - 4))
                    hold_waits()
                    pool.tensor_copy(index_out[0:CAP, b.r:b.r + 1], index[0:CAP, b.r:b.r + 1]).then_inc(s["idxcopy"], 1)
                if valid(-2):
                    n = b.after(-2)
                    pool.wait_ge(s["yout"], n.times(1, 1))
                    pool.wait_ge(s["idxcopy"], n.times(1, 1 - 4))
                    if not (isinstance(n.q, int) and n.q == 1 and n.r == 0):
                        before = n.after(-1)
                        pool.wait_ge(s_scat[l][before.r % 2], 16 * (2 * (before.q - 1) + before.r // 2 + 1))
                    hold_waits()
                    pool.indirect_dma_start(
                        sums[l][:, :], bass.IndirectOffsetOnAxis(ap=index_out[0:CAP, n.r:n.r + 1].bitcast(U32), axis=0),
                        yo[n.r % 2][0:CAP, :], None, compute_op=ALU.add).then_inc(s_scat[l][n.r % 2], 16)

            def one_round(rnd):
                run_steps(pool, rnd, body)
                for b in range(2):
                    pool.wait_ge(s_scat[l][b], 16 * (EXPERTS // 2) * (rnd + 1))
                hold_waits()

            run_rounds(pool, l, one_round)
            pool.wait_ge(s["pe_idle"], 1)
            for t in range(TILES):
                pool.dma_start(xn[:, t, :], sums[l][t * P:(t + 1) * P, :]).then_inc(s_acc_in[l][t], 16)

        for l in range(LAYERS):
            rows_and_sums(l)
            order_matrices(l)
            store_sums(l)
            experts(l)
            for t in range(TILES):
                rstd((2 * l + 1) * TILES + t)

    @block.scalar
    def _(act):
        def matrix_head(l, slot, landed, piece):
            if piece == 0:
                act.wait_ge(s_w[l][slot], 16 * landed)
            cols = slice(piece * PIECE, (piece + 1) * PIECE)
            act.activation(split_slot(slot)[:, 0, cols], raw_slot(slot)[:, cols], ACT.Copy).then_inc(S[l]["head"], 1)

        def rows_head(s, b, m, waits, banks=ps_xT):
            for sm, v in waits:
                act.wait_ge(sm, v)
            act.activation(xT[:, b % 2, 0, :, 0:m].rearrange("p (b c) t -> p b c t", b=2), in_chunks(banks, m),
                           ACT.Copy).then_inc(s, 1)

        def silu(l, b, m):
            act.wait_ge(S[l]["m1"], b.times(1, 1))
            if not (isinstance(b.q, int) and b.times(1) == 0):
                act.wait_ge(S[l]["hTready"], b.times(1))
            act.activation(h_sb[0:m], ps_h[0:m, 0:FF].rearrange("p (a j) -> p j a", j=FC), ACT.Silu).then_inc(S[l]["silu"], 1)

        def hidden_head(l, b, m):
            act.wait_ge(S[l]["hTready"], b.times(1, 1))
            if not (isinstance(b.q, int) and b.times(1) == 0):
                act.wait_ge(S[l]["m2"], b.times(1))
            act.activation(hT[:, 0, :, 0:m], ps_hT[:, 0:FC * m].rearrange("p (j t) -> p j t", j=FC),
                           ACT.Copy).then_inc(S[l]["hhead"], 1)

        def dense(l):
            s = S[l]

            def ordered_rows(t):
                act.wait_ge(s_norm, 2 * l * TILES + t + 1)
                if t:
                    act.wait_ge(s["xTready"], t)
                    act.wait_ge(s["rows_out"], 16 * t)
                elif l == 0:
                    act.wait_ge(s_mix, TILES)
                act.activation(xp.rearrange("p (c a) -> p c a", c=CHUNKS),
                               xn[:, t, :].rearrange("p (a c) -> p c a", c=CHUNKS), ACT.Copy).then_inc(s["xp"], 1)

            def head(t):
                act.wait_ge(s["xTready"], t + 1)
                rows_head(s["xhead"], t, P, [(s["logits"], t - 1)] if t >= 2 else [])

            if l:
                act.wait_ge(s_pv, UNITS)
                act.wait_ge(s_wo, TILES - 1)
            ordered_rows(0)
            head(0)
            if l:
                act.wait_ge(s_wo, TILES)
                for piece in range(PIECES):
                    matrix_head(1, 2, 1, piece)
                router_head(1)
            ordered_rows(1)
            act.wait_ge(s_rw_tail, l + 1)
            for t in range(TILES):
                silu(l, Block(0, t), P)
                hidden_head(l, Block(0, t), P)
                if t + 1 < TILES:
                    head(t + 1)
                if t + 2 < TILES:
                    ordered_rows(t + 2)
                if t < 3:
                    for piece in range(PIECES):
                        matrix_head(l, 3 + t, 1, piece)
            act.wait_ge(s["logits"], TILES)
            act.activation(prob, ps_log[:, 0:TILES * EXPERTS].rearrange("p (t e) -> p t e", t=TILES),
                           ACT.Sigmoid).then_inc(s["prob"], 1)

        def experts(l):
            s = S[l]

            def body(b, valid):
                if valid(-2):
                    n = b.after(-2)
                    act.wait_ge(s["m2"], n.times(1, 1))
                    if not (isinstance(n.q, int) and n.q == 1 and n.r < 2):
                        old = n.after(-2)
                        act.wait_ge(s_scat[l][n.r % 2], 16 * (2 * (old.q - 1) + old.r // 2 + 1))
                    act.activation(yo[n.r % 2][0:CAP].rearrange("p (b n) -> p b n", b=2), ps_y[0:CAP], ACT.Copy,
                                   scale=gate[0:CAP, n.r:n.r + 1]).then_inc(s["yout"], 1)
                if valid(-1):
                    hidden_head(l, b.after(-1), CAP)
                if valid(1):
                    n = b.after(1)
                    if first_of_all(n):
                        act.wait_ge(s["m2"], TILES)
                        for u in range(3):
                            for piece in range(PIECES):
                                matrix_head(l, *weight_unit(b.after(2), u), piece)
                    rows_head(s["xhead"], n.r, CAP, [(s["xTready"], n.times(1, 1)), (s["m1"], n.times(1, -1))])
                if valid(0) and not split_early(b):
                    slot, landed = weight_unit(b, 2)
                    act.wait_ge(s["m2"], b.times(1, -1))
                    for piece in range(PIECES):
                        matrix_head(l, slot, landed, piece)
                if valid(1) and not split_early(b.after(1)):
                    n = b.after(1)
                    act.wait_ge(s["m1"], n.times(1, -1))
                    slot, landed = weight_unit(n, 0)
                    for piece in range(PIECES):
                        matrix_head(l, slot, landed, piece)
                    slot, landed = weight_unit(n, 1)
                    matrix_head(l, slot, landed, 0)
                if valid(0):
                    silu(l, b, CAP)
                if valid(1) and not split_early(b.after(1)):
                    matrix_head(l, slot, landed, 1)

            run_rounds(act, l, lambda rnd: run_steps(act, rnd, body))

        def shared_heads(l):
            for u in range(3):
                for piece in range(PIECES):
                    matrix_head(l, u, 1, piece)

        def router_head(l):
            act.wait_ge(s_rw_in, 16 * (l + 1))
            act.activation(rw[:, 0], rw_raw, ACT.Copy).then_inc(s_rw_head, 1)

        for t in range(TILES):
            act.wait_ge(s_pooled, t + 1)
            if t:
                act.wait_ge(s_mix, t)
            act.activation(pooled.rearrange("p (b c) t -> p b (c t)", b=2), ps_xT, ACT.Copy).then_inc(s_pooled_sb, 1)
        router_head(0)
        shared_heads(0)
        dense(0)
        experts(0)

        act.wait_ge(S[0]["pe_idle"], 1)
        for k in range(CHUNKS):
            act.wait_ge(s_wqkv[k], 16)
            act.activation(wqkv[:, 0, k, :], wqkv_raw[:, k, :], ACT.Copy).then_inc(s_qhead, 1)
            if k == CHUNKS // 2 - 1:
                rows_head(s_axhead, 0, P, [(s_axT, 1)])
        for t in range(1, TILES):
            waits = [(s_axT, t + 1)]
            if t >= 2:
                waits.append((s_qkv, t - 1))
            rows_head(s_axhead, t, P, waits)

        def wo_head(k):
            act.wait_ge(s_wo_in[k % 3], 16 * (k // 3 + 1))
            act.activation(wo[:, 0, k, :], wo_raw[:, k % 3, :], ACT.Copy).then_inc(s_wohead, 1)

        act.wait_ge(s_qkv, TILES)

        def queries_out(u):
            n, g = divmod(u, KV_HEADS)
            act.wait_ge(s_qkT, u + 1)
            if u >= 2:
                act.wait_ge(s_score, u - 1)
            act.activation(qT[u % 2][0:HEAD], ps_hT[0:HEAD, :].rearrange("p (h t) -> p h t", h=PER_KV), ACT.Copy)
            act.activation(kT[0:HEAD, g, n % 2, :], ps_kT, ACT.Copy).then_inc(s_qkT_sb, 1)

        def exponentials(u):
            keys = slice(0 if u // KV_HEADS else P, 2 * P)
            act.wait_ge(s_negtop, u + 1)
            for h in range(PER_KV):
                act.activation(score[u % 2][:, h, keys], score[u % 2][:, h, keys], ACT.Exp,
                               bias=negtop[:, u % 2, h:h + 1], accum_out=total[:, u % 2, h:h + 1])
            act.activation(sink_exp[:, u % 2, :], sink_arg[:, u % 2, :], ACT.Exp).then_inc(s_exp, 1)

        def weights_out(u):
            act.wait_ge(s_pT, u + 1)
            if u:
                act.wait_ge(s_pv, u)
            act.activation(pT[:, 1], ps_h.rearrange("p (h t) -> p h t", h=PER_KV), ACT.Copy).then_inc(s_pT_cur, 1)

        for i in range(UNITS + 3):
            if projected(i) is not None:
                n = projected(i)
                waits = [(s_axT, TILES + n + 1)]
                if n >= 2:
                    waits.append((s_wo, n - 1))
                rows_head(s_axhead, n, P, waits, ps_y)
            if i < UNITS:
                queries_out(i)
            if 2 <= i < UNITS + 2:
                weights_out(i - 2)
            if 1 <= i < UNITS + 1:
                exponentials(i - 1)
            if i < 4:
                wo_head(2 * i)
                wo_head(2 * i + 1)
            if 9 <= i < 9 + 2 * PIECES:
                matrix_head(1, (i - 9) // PIECES, 1, (i - 9) % PIECES)
        dense(1)
        experts(1)

    @block.vector
    def _(dve):
        links = [0]

        def link(ins):
            links[0] += 1
            ins.then_inc(s_dve, 1)
            dve.wait_ge(s_dve, links[0])

        norms = [0]

        def layer_norm(t):
            norm_stats(t)
            norm_apply(t)

        def norm_stats(t):
            x = xn[:, t, :]
            for h in HALVES:
                last = dve.bn_stats(stats[:, h, :], x[:, h * BANK:(h + 1) * BANK])
            link(last)
            dve.bn_aggr(mean_var, stats).then_inc(s_var, 1)
            norms[0] += 1

        def norm_apply(t):
            x = xn[:, t, :]
            dve.wait_ge(s_var, norms[0])
            link(dve.scalar_tensor_tensor(out=x, in0=x, scalar=mean_var[:, 0:1], in1=par[:, 0, :],
                                          op0=ALU.subtract, op1=ALU.mult))
            dve.wait_ge(s_rstd, norms[0])
            dve.scalar_tensor_tensor(out=x, in0=x, scalar=power[:, 2:3], in1=par[:, 1, :],
                                     op0=ALU.mult, op1=ALU.add).then_inc(s_norm, 1)

        def matrix_tail(l, slot, piece, count):
            dve.wait_ge(S[l]["head"], count)
            cols = slice(piece * PIECE, (piece + 1) * PIECE)
            w = split_slot(slot)
            dve.tensor_tensor(w[:, 1, cols], raw_slot(slot)[:, cols], w[:, 0, cols].bitcast(F32),
                              ALU.subtract).then_inc(S[l]["tail"], 1)

        def unit_count(b, u, piece):
            return b.times(3 * PIECES, PIECES * (u - 12 + 3) + piece + 1)

        def rows_tail(head, n, tail, b, m, banks=ps_xT):
            dve.wait_ge(head, n)
            dst = xT[:, b % 2, 1, :, 0:m].rearrange("p (b c) t -> p b c t", b=2)
            hd = xT[:, b % 2, 0, :, 0:m].rearrange("p (b c) t -> p b c t", b=2).bitcast(F32)
            for h in HALVES:
                last = dve.tensor_tensor(dst[:, h], in_chunks(banks, m)[:, h], hd[:, h], ALU.subtract)
            last.then_inc(tail, 1)

        def hidden(l, b, m):
            dve.wait_ge(S[l]["silu"], b.times(1, 1))
            dve.tensor_tensor(h_sb[0:m], h_sb[0:m], ps_h[0:m, FF:2 * FF].rearrange("p (a j) -> p j a", j=FC),
                              ALU.mult).then_inc(S[l]["hidden"], 1)

        def hidden_tail(l, b, m):
            dve.wait_ge(S[l]["hhead"], b.times(1, 1))
            dve.tensor_tensor(hT[:, 1, :, 0:m], ps_hT[:, 0:FC * m].rearrange("p (j t) -> p j t", j=FC),
                              hT[:, 0, :, 0:m].bitcast(F32), ALU.subtract).then_inc(S[l]["htail"], 1)

        def router_tail(l):
            dve.wait_ge(s_rw_head, l + 1)
            dve.tensor_tensor(rw[:, 1], rw_raw, rw[:, 0].bitcast(F32), ALU.subtract).then_inc(s_rw_tail, 1)

        def shared_tile(l, t):
            dve.wait_ge(S[l]["m2"], t + 1)
            dve.wait_ge(S[l]["xp"], t + 1)
            x = xn[:, t, :].rearrange("p (b n) -> p b n", b=2)
            for h in HALVES:
                last = dve.scalar_tensor_tensor(out=x[:, h], in0=x[:, h], scalar=ALPHA, in1=ps_y[:, h],
                                                op0=ALU.mult, op1=ALU.add)
            last.then_inc(S[l]["yout"], 1)

        def route(l):
            s = S[l]
            dve.wait_ge(s["prob"], 1)
            dve.wait_ge(s_moe_const, 32 * (l + 1))
            link(dve.tensor_tensor(sel, prob, router_bias.unsqueeze(1).to_broadcast([P, TILES, EXPERTS]), ALU.add))
            for t in range(TILES):
                for g in range(EXPERT_GROUPS):
                    last = dve.max(group_top[:, t, g, :], sel[:, t, g * PER_GROUP:(g + 1) * PER_GROUP])
            dve.memset(gext[:, :, EXPERT_GROUPS:], FILLER)
            link(last)
            shared_tile(l, TILES - 1)
            link(dve.tensor_tensor(gext[:, :, 0:EXPERT_GROUPS], group_top[:, :, :, 0], group_top[:, :, :, 1], ALU.add))
            for t in range(TILES):
                last = dve.max(gtop[:, t, :], gext[:, t, :])
            link(last)
            link(dve.memset(gtop[:, :, TOP_GROUPS:], FILLER))
            for t in range(TILES):
                last = dve.match_replace(gext[:, t, :], gtop[:, t, :], gext[:, t, :], TAKEN)
            link(last)
            groups = gext[:, :, 0:EXPERT_GROUPS]
            link(dve.tensor_scalar(groups, groups, TAKEN, None, ALU.is_equal))
            wide = groups.unsqueeze(3).to_broadcast([P, TILES, EXPERT_GROUPS, PER_GROUP])
            sel4 = sel.rearrange("p t (g k) -> p t g k", k=PER_GROUP)
            rest4 = rest.rearrange("p t (g k) -> p t g k", k=PER_GROUP)
            link(dve.tensor_tensor(sel4, sel4, wide, ALU.mult))
            link(dve.tensor_scalar(rest4, wide, -LOW, LOW, ALU.mult, ALU.add))
            link(dve.tensor_tensor(sel, sel, rest, ALU.add))
            for t in range(TILES):
                last = dve.max(etop[:, t, :], sel[:, t, :])
            link(last)
            for t in range(TILES):
                last = dve.match_replace(rest[:, t, :], etop[:, t, :], sel[:, t, :], TAKEN)
            link(last)
            link(dve.tensor_scalar(rest, rest, TAKEN, None, ALU.is_equal))
            dve.tensor_copy(chosen, rest).then_inc(s["chosen"], 1)
            link(dve.tensor_tensor(prob, prob, rest, ALU.mult))
            link(dve.tensor_reduce(gsum, prob, AX.X, ALU.add))
            link(dve.reciprocal(gsum, gsum))
            link(dve.tensor_tensor(prob, prob, gsum.unsqueeze(2).to_broadcast([P, TILES, EXPERTS]), ALU.mult))
            link(dve.tensor_scalar(prob, prob, ROUTED_SCALE, None, ALU.mult))
            for k in range(3):
                link(dve.tensor_copy(tab[:, :, :, 3 + k], prob))
                if k < 2:
                    link(dve.tensor_tensor(prob, prob, tab[:, :, :, 3 + k], ALU.subtract))
            dve.wait_ge(s["ranked"], 1)
            link(dve.tensor_tensor(ranks, ps_list[:, 0:256].rearrange("p (t e) -> p t e", t=TILES), rest, ALU.mult))
            link(dve.tensor_scalar(rest, rest, -FAR, FAR, ALU.mult, ALU.add))
            dve.tensor_reduce(most, ps_list[:, 256:256 + EXPERTS], AX.X, ALU.max)
            link(dve.tensor_tensor(ranks, ranks, rest, ALU.add))
            dve.tensor_copy(most_int, most).then_inc(s["most"], 1)

        def experts(l):
            s = S[l]

            def body(b, valid):
                if valid(-1):
                    hidden_tail(l, b.after(-1), CAP)
                if valid(3):
                    n = b.after(3)
                    if not (isinstance(n.q, int) and n.q == 1 and n.r < 2):
                        dve.wait_ge(s["listed"], n.times(1, -1 - 4))
                    dve.tensor_tensor(oh[:, n.r % 2],
                                      ranks[:, :, bass.ds(n.expert, 1)].to_broadcast([P, TILES, CAP]),
                                      slots.unsqueeze(1).to_broadcast([P, TILES, CAP]),
                                      ALU.is_equal).then_inc(s["oh"], 1)
                if valid(2):
                    n = b.after(2)
                    dve.wait_ge(s["listed"], n.times(1, 1 - 4))
                    first = isinstance(n.q, int) and n.q == 1
                    if not first:
                        dve.wait_ge(s["yout"], n.times(1, -3))
                        dve.wait_ge(s["idxcopy"], n.times(1, -3 - 4))
                    dve.tensor_scalar(slot_row[0:CAP], ps_list[0:CAP, 2:3], dummy[0:CAP, 0:1], dummy[0:CAP, 1:2],
                                      ALU.mult, ALU.add).then_inc(s["slotrow"], 1)
                    dve.tensor_reduce(gate[0:CAP, n.r:n.r + 1], ps_list[0:CAP, 3:6], AX.X, ALU.add)
                    dve.wait_ge(s["slotrow"], n.times(1, 1 - 4))
                    dve.tensor_scalar(index[0:CAP, n.r:n.r + 1], slot_row[0:CAP], ps_list[0:CAP, 0:1],
                                      ps_list[0:CAP, 1:2], ALU.add, ALU.add).then_inc(s["index"], 1)
                if valid(1):
                    n = b.after(1)
                    if first_of_all(n):
                        for u in range(3):
                            for piece in range(PIECES):
                                matrix_tail(l, u, piece, unit_count(b.after(2), u, piece))
                    rows_tail(s["xhead"], n.times(1, 1), s["xtail"], n.r, CAP)
                if valid(0) and not split_early(b):
                    slot, _ = weight_unit(b, 2)
                    for piece in range(PIECES):
                        matrix_tail(l, slot, piece, unit_count(b, 2, piece))
                if valid(1) and not split_early(n):
                    slot, _ = weight_unit(n, 0)
                    for piece in range(PIECES):
                        matrix_tail(l, slot, piece, unit_count(n, 0, piece))
                    slot, _ = weight_unit(n, 1)
                    matrix_tail(l, slot, 0, unit_count(n, 1, 0))
                if valid(0):
                    hidden(l, b, CAP)
                if valid(1) and not split_early(n):
                    matrix_tail(l, slot, 1, unit_count(n, 1, 1))

            def one_round(rnd):
                if not isinstance(rnd, int):
                    dve.tensor_scalar(slots, slots, float(CAP), None, ALU.add).then_inc(s["slots"], 1)
                    dve.wait_ge(s["slots"], rnd)
                run_steps(dve, rnd, body)
                dve.wait_ge(s["tail"], 3 * PIECES * (EXPERTS * (rnd + 1) + 1))
                dve.sem_inc(s["round_over"], 1)

            run_rounds(dve, l, one_round)

        def shared_tails(l):
            for u in range(3):
                for piece in range(PIECES):
                    matrix_tail(l, u, piece, PIECES * u + piece + 1)

        def pool_tile(t):
            dve.wait_ge(s_mix, t + 1)
            dve.wait_ge(s_pooled, min(t + 2, TILES))
            x = xn[:, t, :].rearrange("p (b n) -> p b n", b=2)
            for h in HALVES:
                last = dve.scalar_tensor_tensor(out=x[:, h], in0=x[:, h], scalar=ALPHA, in1=ps_y[:, h],
                                                op0=ALU.mult, op1=ALU.add)
            last.then_inc(s_mix_used, 1)
            dve.wait_ge(s_mix_used, t + 1)
            if t == 0:
                dve.wait_ge(s_par, 16 * 2)
            layer_norm(t)

        def last_norm(l):
            dve.wait_ge(s_par, 16 * (4 if l == 0 else 12))
            for t in range(TILES):
                dve.wait_ge(s_acc_in[l][t], 16)
                layer_norm(t)

        dve.wait_ge(s_pool_w, 16)
        dve.wait_ge(s_pool_scale, 16)
        for k in range(2):
            last = dve.tensor_tensor(pool_w[:, :, k, :], pool_w[:, :, k, :],
                                     par[:, 2, :].rearrange("p (g n) -> p g n", g=len(WINDOWS)), ALU.mult)
        last.then_inc(s_pool_scaled, 1)
        for t in range(TILES):
            dve.wait_ge(s_x[t], 16)
            pool_tile(t)
        router_tail(0)
        shared_tails(0)
        dve.wait_ge(s_const, 32)

        def dense_tiles(l):
            for t in range(TILES):
                hidden(l, Block(0, t), P)
                hidden_tail(l, Block(0, t), P)
                if t + 1 < TILES:
                    rows_tail(S[l]["xhead"], t + 2, S[l]["xtail"], t + 1, P)
                    shared_tile(l, t)
                if t < 3:
                    for piece in range(PIECES):
                        matrix_tail(l, 3 + t, piece, unit_count(Block(1, 0), t, piece))

        def token_table(l):
            number = dummy[:, 1:2]
            for t in range(TILES):
                dve.memset(tab[:, t, :, 1], float(t * P))
            dve.memset(tab[:, :, :, 2], 1.0)
            dve.memset(tab[:, :, :, 0], 1.0)
            link(dve.tensor_scalar(most, number, -float(SEQ), None, ALU.add))
            link(dve.tensor_scalar(tab[:, :, :, 0], tab[:, :, :, 0], most, None, ALU.mult))

        token_table(0)
        rows_tail(S[0]["xhead"], 1, S[0]["xtail"], 0, P)
        dense_tiles(0)
        route(0)
        experts(0)

        def wqkv_tail(k):
            dve.wait_ge(s_qhead, k + 1)
            dve.tensor_tensor(wqkv[:, 1, k, :], wqkv_raw[:, k, :], wqkv[:, 0, k, :].bitcast(F32),
                              ALU.subtract).then_inc(s_qtail, 1)

        dve.wait_ge(s_par, 16 * 4)
        for t in range(TILES):
            dve.wait_ge(s_acc_in[0][t], 16)
            layer_norm(t)
            if t == 0:
                for k in range(CHUNKS // 2):
                    wqkv_tail(k)
                rows_tail(s_axhead, 1, s_axtail, 0, P)
                for k in range(CHUNKS // 2, CHUNKS):
                    wqkv_tail(k)
            elif t == 1:
                rows_tail(s_axhead, 2, s_axtail, 1, P)

        def rotate(x, t, heads, tmp):
            v = x.rearrange("p (h s j) -> p h s j", s=2, j=HEAD // 2)
            tm = tmp.rearrange("p (s h j) -> p s h j", s=2, h=heads)
            cos = rope[:, t, 0, :].unsqueeze(1).to_broadcast([P, heads, HEAD // 2])
            sin = rope[:, t, 1, :].unsqueeze(1).to_broadcast([P, heads, HEAD // 2])
            for k in HALVES:
                last = dve.tensor_tensor(tm[:, k], v[:, :, k, :], sin, ALU.mult)
            link(last)
            for k in HALVES:
                last = dve.tensor_tensor(v[:, :, k, :], v[:, :, k, :], cos, ALU.mult)
            link(last)
            dve.tensor_tensor(v[:, :, 0, :], v[:, :, 0, :], tm[:, 1], ALU.subtract)
            link(dve.tensor_tensor(v[:, :, 1, :], v[:, :, 1, :], tm[:, 0], ALU.add))

        def rotate_tile(t, tmp):
            rotate(q_nat[:, t, :], t, HEADS, tmp)
            rotate(k_nat[:, t, :], t, KV_HEADS, tmp[:, 0:KV])
            dve.sem_inc(s_roped, 1)

        dve.wait_ge(s_par, 16 * 8)
        dve.tensor_scalar(negsink, negsink, -1.0, None, ALU.mult)
        for t in range(TILES):
            if 0 < t < TILES - 1:
                rows_tail(s_axhead, t + 2, s_axtail, t + 1, P)
            dve.wait_ge(s_qkv, t + 1)
            banks = qkv_ps(t)
            for h in HALVES:
                cols = slice(h * BANK, (h + 1) * BANK)
                dve.tensor_tensor(q_nat[:, t, cols], banks[:, h, :], bqkv[:, cols], ALU.add)
            dve.tensor_tensor(k_nat[:, t, :], banks[:, 2, 0:KV], bqkv[:, D:D + KV], ALU.add)
            dve.tensor_tensor(v_nat[:, t, :], banks[:, 2, KV:2 * KV], bqkv[:, D + KV:QKV], ALU.add).then_inc(s_qkv_used, 1)
            dve.wait_ge(s_qkv_used, t + 1)
            if t < TILES - 1:
                rotate_tile(t, score[0].rearrange("p a b -> p (a b)"))

        def wo_tail(k):
            dve.wait_ge(s_wohead, k + 1)
            dve.tensor_tensor(wo[:, 1, k, :], wo_raw[:, k % 3, :], wo[:, 0, k, :].bitcast(F32),
                              ALU.subtract).then_inc(s_wotail, 1)

        def softmax(u):
            n, g = divmod(u, KV_HEADS)
            keys = slice(0 if n else P, 2 * P)
            width = 2 * P if n else P
            dve.wait_ge(s_score, u + 1)
            if u >= 2:
                dve.wait_ge(s_pT, u - 1)
            sc = ps_xT.rearrange("p b (h k) -> p (b h) k", h=2)
            mask = band[:, keys].unsqueeze(1).to_broadcast([P, PER_KV, width])
            buf = score[u % 2][:, :, keys]
            dve.scalar_tensor_tensor(out=buf, in0=sc[:, :, keys], scalar=HEAD ** -0.5, in1=mask,
                                     op0=ALU.mult, op1=ALU.add).then_inc(s_masked, 1)
            dve.wait_ge(s_masked, u + 1)
            link(dve.tensor_reduce(top, buf, AX.X, ALU.max))
            sink = negsink[:, g * PER_KV:(g + 1) * PER_KV]
            link(dve.scalar_tensor_tensor(out=negtop[:, u % 2], in0=top, scalar=-1.0, in1=sink,
                                          op0=ALU.mult, op1=ALU.min))
            dve.tensor_tensor(sink_arg[:, u % 2], negtop[:, u % 2], sink, ALU.subtract).then_inc(s_negtop, 1)

        def previous_out(u):
            if u // KV_HEADS:
                dve.wait_ge(s_pT, u + 1)
                dve.wait_ge(s_pv, u)
                dve.tensor_copy(pT[:, 0], ps_log.rearrange("p (h t) -> p h t", h=PER_KV)).then_inc(s_pT_prev, 1)

        def inverse_total(u):
            dve.wait_ge(s_exp, u + 1)
            link(dve.tensor_tensor(total[:, u % 2], total[:, u % 2], sink_exp[:, u % 2], ALU.add))
            link(dve.reciprocal(inverse[:, u % 2], total[:, u % 2]))

        def divide(u):
            n, g = divmod(u, KV_HEADS)
            dve.wait_ge(s_pv, u + 1)
            dve.tensor_tensor(q_nat[:, n, g * 256:(g + 1) * 256].rearrange("p (h j) -> p h j", h=PER_KV),
                              ps_list[:, 0:256].rearrange("p (h j) -> p h j", h=PER_KV),
                              inverse[:, u % 2].unsqueeze(2).to_broadcast([P, PER_KV, HEAD]),
                              ALU.mult).then_inc(s_o, 1)

        def projection_out(n):
            dve.wait_ge(s_wo, n + 1)
            x = xn[:, n, :].rearrange("p (b n) -> p b n", b=2)
            for h in HALVES:
                last = dve.scalar_tensor_tensor(out=x[:, h], in0=x[:, h], scalar=ALPHA, in1=ps_y[:, h],
                                                op0=ALU.mult, op1=ALU.add)
            last.then_inc(s_wo_used, 1)

        dve.wait_ge(s_band, 16)
        dve.tensor_copy(band, band_raw).then_inc(s_band_copied, 1)
        dve.wait_ge(s_band_copied, 1)
        for i in range(UNITS + 5):
            if projected(i - 1) is not None:
                projection_out(projected(i - 1))
            if 2 <= i < UNITS + 2:
                previous_out(i - 2)
                inverse_total(i - 2)
            if projected(i) is not None:
                rows_tail(s_axhead, TILES + projected(i) + 1, s_axtail, projected(i), P, ps_y)
            if i < UNITS:
                softmax(i)
            if i == 1:
                rotate_tile(TILES - 1, par[:, 0, :])
            if 2 <= i < UNITS + 2:
                divide(i - 2)
            if projected(i - 1) is not None:
                n = projected(i - 1)
                dve.wait_ge(s_wo_used, n + 1)
                link(dve.tensor_tensor(xn[:, n, :], xn[:, n, :], bo, ALU.add))
                norm_stats(n)
            if projected(i - 2) is not None:
                if i == 8:
                    dve.wait_ge(s_par, 16 * 10)
                norm_apply(projected(i - 2))
            if i < 4:
                wo_tail(2 * i)
                wo_tail(2 * i + 1)
            if 9 <= i < 9 + 2 * PIECES:
                matrix_tail(1, (i - 9) // PIECES, (i - 9) % PIECES, i - 8)
            if i == UNITS + 2:
                rows_tail(S[1]["xhead"], 1, S[1]["xtail"], 0, P)
                token_table(1)
        for piece in range(PIECES):
            matrix_tail(1, 2, piece, 2 * PIECES + piece + 1)
        router_tail(1)
        dense_tiles(1)
        route(1)
        experts(1)
        last_norm(1)

    @block.tensor
    def _(pe):
        def product(out_ap, stationary, moving, first, last):
            for k, (a, b) in enumerate(PASSES):
                mm = pe.matmul(out_ap, stationary(a), moving(b), start=first and k == 0,
                               stop=last and k == len(PASSES) - 1)
            return mm

        def transpose_rows(src, m, banks=ps_xT):
            for k in range(CHUNKS):
                mm = pe.transpose(in_chunks(banks, m)[:, k // 4, k % 4, :], src[0:m, k * P:(k + 1) * P], ident[0:m, 0:m])
            return mm

        def first_product(b, m, w1_slot):
            w = split[:, 2 * w1_slot * UNIT:2 * (w1_slot + 2) * UNIT].rearrange(
                "p (m s c n) -> p s c m n", m=2, s=2, c=CHUNKS)
            for k in range(CHUNKS):
                mm = product(ps_h[0:m].rearrange("p (m n) -> p m n", m=2), lambda a: xT[:, b % 2, a, k, 0:m],
                             lambda a: w[:, a, k], k == 0, k == CHUNKS - 1)
            return mm

        def transpose_hidden(m):
            for j in range(FC):
                mm = pe.transpose(ps_hT[:, j * m:(j + 1) * m], h_sb[0:m, j, :], ident[0:m, 0:m])
            return mm

        def second_product(m, slot):
            w = split_slot(slot).rearrange("p s (j n) -> p s j n", j=FC)
            for h in HALVES:
                for j in range(FC):
                    mm = product(ps_y[0:m, h, :], lambda a: hT[:, a, j, 0:m],
                                 lambda a: w[:, a, j, h * BANK:(h + 1) * BANK], j == 0, j == FC - 1)
            return mm

        def rows_transposed(l, t):
            pe.wait_ge(S[l]["xp"], t + 1)
            if t:
                pe.wait_ge(S[l]["xtail"], t)
            transpose_rows(xp, P).then_inc(S[l]["xTready"], 1)

        def dense(l):
            s = S[l]
            for t in range(TILES):
                pe.wait_ge(s["xtail"], t + 1)
                pe.wait_ge(s["tail"], 2 * PIECES)
                first_product(t, P, 0).then_inc(s["m1"], 1)
                pe.wait_ge(s_rw_tail, l + 1)
                for k in range(CHUNKS):
                    mm = product(ps_log[:, t * EXPERTS:(t + 1) * EXPERTS], lambda a: xT[:, t % 2, a, k, :],
                                 lambda a: rw[:, a, k, :], k == 0, k == CHUNKS - 1)
                mm.then_inc(s["logits"], 1)
                pe.wait_ge(s["hidden"], t + 1)
                transpose_hidden(P).then_inc(s["hTready"], 1)
                if t + 1 < TILES:
                    rows_transposed(l, t + 1)
                pe.wait_ge(s["htail"], t + 1)
                pe.wait_ge(s["tail"], 3 * PIECES)
                if t:
                    pe.wait_ge(s["yout"], t)
                second_product(P, 2).then_inc(s["m2"], 1)

        def rank(l):
            s = S[l]
            pe.wait_ge(s_moe_const, 32 * (l + 1))
            pe.wait_ge(s["order"], 2)
            pe.wait_ge(s["chosen"], 1)
            for t in range(TILES):
                for k in range(t + 1):
                    pe.matmul(ps_list[:, t * EXPERTS:(t + 1) * EXPERTS], order[:, 0 if k == t else 1, :],
                              chosen[:, k, :], start=(k == 0), stop=(k == t))
            for k in range(TILES):
                mm = pe.matmul(ps_list[:, 256:256 + EXPERTS], order[:, 1, :], chosen[:, k, :],
                               start=(k == 0), stop=(k == TILES - 1))
            mm.then_inc(s["ranked"], 1)

        def experts(l):
            s = S[l]

            def body(b, valid):
                if valid(-1):
                    n = b.after(-1)
                    pe.wait_ge(s["hidden"], n.times(1, 1))
                    pe.wait_ge(s["htail"], n.times(1))
                    transpose_hidden(CAP).then_inc(s["hTready"], 1)
                if valid(1):
                    n = b.after(1)
                    pe.wait_ge(s_xg[l][n.r % 2], 16 * (2 * (n.q - 1) + n.r // 2 + 1))
                    pe.wait_ge(s["xtail"], n.times(1))
                    transpose_rows(xg[n.r % 2], CAP).then_inc(s["xTready"], 1)
                if valid(2):
                    n = b.after(2)
                    pe.wait_ge(s["oh"], n.times(1, 1 - 4))
                    if not (isinstance(n.q, int) and n.q == 1 and n.r == 0):
                        pe.wait_ge(s["index"], n.times(1, -4))
                    for t in range(TILES):
                        mm = pe.matmul(ps_list[0:CAP, 0:TAB], oh[:, n.r % 2, t, :],
                                       tab[:, t, bass.ds(n.expert, 1), :].rearrange("p e k -> p (e k)"),
                                       start=(t == 0), stop=(t == TILES - 1))
                    mm.then_inc(s["listed"], 1)
                if valid(0):
                    pe.wait_ge(s["xtail"], b.times(1, 1))
                    pe.wait_ge(s["tail"], b.times(3 * PIECES, PIECES * (-12 + 3 + 2)))
                    slot, _ = weight_unit(b, 0)
                    first_product(b.r, CAP, slot).then_inc(s["m1"], 1)
                if valid(-1):
                    n = b.after(-1)
                    pe.wait_ge(s["htail"], n.times(1, 1))
                    pe.wait_ge(s["tail"], n.times(3 * PIECES, PIECES * (-12 + 3 + 3)))
                    pe.wait_ge(s["yout"], n.times(1))
                    slot, _ = weight_unit(n, 2)
                    second_product(CAP, slot).then_inc(s["m2"], 1)

            def one_round(rnd):
                run_steps(pe, rnd, body)
                pe.wait_ge(s["m2"], EXPERTS * (rnd + 1) + 4)

            run_rounds(pe, l, one_round)
            pe.sem_inc(s["pe_idle"], 1)

        pe.wait_ge(s_pool_band, 16)

        def pool_rows(t):
            pe.wait_ge(s_x[t], 16)
            if t:
                pe.wait_ge(s_pooled_sb, t)
            for k in range(CHUNKS):
                g = k * P // GROUP_CH
                dst = ps_xT[:, k // 4, (k % 4) * P:(k % 4 + 1) * P]
                mm = pe.matmul(dst, xn[:, t, k * P:(k + 1) * P], pool_band[:, g, min(t, 1), :],
                               start=True, stop=(t == 0))
                if t:
                    mm = pe.matmul(dst, xn[:, t - 1, k * P:(k + 1) * P], pool_band[:, g, 2, :],
                                   start=False, stop=True)
            mm.then_inc(s_pooled, 1)

        def mix(t):
            pe.wait_ge(s_pooled_sb, t + 1)
            pe.wait_ge(s_pool_scaled, 1)
            if t:
                pe.wait_ge(s_mix_used, t)
            for g in range(len(WINDOWS)):
                dst = ps_y[:, g // 2, (g % 2) * GROUP_CH:(g % 2 + 1) * GROUP_CH]
                for k in range(2):
                    mm = pe.matmul(dst, pooled[:, 2 * g + k, :], pool_w[:, g, k, :], start=(k == 0), stop=(k == 1))
            mm.then_inc(s_mix, 1)

        for t in range(TILES + 1):
            if t < TILES:
                pool_rows(t)
            if t:
                mix(t - 1)
        pe.wait_ge(s_const, 32)
        rows_transposed(0, 0)
        dense(0)
        rank(0)
        experts(0)

        def trunk_transposed(t):
            pe.wait_ge(s_norm, TILES + t + 1)
            if t:
                pe.wait_ge(s_axtail, t)
            transpose_rows(xn[:, t, :], P).then_inc(s_axT, 1)

        trunk_transposed(0)
        for t in range(TILES):
            pe.wait_ge(s_axtail, t + 1)
            if t >= 2:
                pe.wait_ge(s_qkv_used, t - 1)
            for b in range(3):
                if b == 2 and t + 1 < TILES:
                    trunk_transposed(t + 1)
                for k in range(CHUNKS):
                    if t == 0 and b == 0:
                        pe.wait_ge(s_qtail, k + 1)
                    mm = product(qkv_ps(t)[:, b, :], lambda a: xT[:, t % 2, a, k, :],
                                 lambda a: wqkv[:, a, k, b * BANK:(b + 1) * BANK], k == 0, k == CHUNKS - 1)
            mm.then_inc(s_qkv, 1)

        def queries_transposed(u):
            n, g = divmod(u, KV_HEADS)
            pe.wait_ge(s_qkv_used, TILES)
            pe.wait_ge(s_roped, n + 1)
            if u:
                pe.wait_ge(s_qkT_sb, u)
            for h in range(PER_KV):
                pe.transpose(ps_hT[0:HEAD, h * P:(h + 1) * P],
                             q_nat[:, n, (g * PER_KV + h) * HEAD:(g * PER_KV + h + 1) * HEAD], ident[:, :])
            if u >= 3:
                pe.wait_ge(s_o, u - 2)
            pe.transpose(ps_kT, k_nat[:, n, g * HEAD:(g + 1) * HEAD], ident[:, :]).then_inc(s_qkT, 1)

        def scores(u):
            n, g = divmod(u, KV_HEADS)
            pe.wait_ge(s_qkT_sb, u + 1)
            if u:
                pe.wait_ge(s_masked, u)
            for h in range(PER_KV):
                for b in ((1, 0) if n else (1,)):
                    dst = ps_xT[:, h // 2, (h % 2) * 2 * P + b * P:(h % 2) * 2 * P + (b + 1) * P]
                    mm = pe.matmul(dst, qT[u % 2][0:HEAD, h, :], kT[0:HEAD, g, (n - 1 + b) % 2, :], start=True, stop=True)
            mm.then_inc(s_score, 1)

        def weights_transposed(u):
            n = u // KV_HEADS
            pe.wait_ge(s_exp, u + 1)
            if u:
                pe.wait_ge(s_pT_cur, u)
                if prev_count(u):
                    pe.wait_ge(s_pT_prev, prev_count(u))
            for b in ((1, 0) if n else (1,)):
                for h in range(PER_KV):
                    dst = (ps_h if b else ps_log)[:, h * P:(h + 1) * P]
                    mm = pe.transpose(dst, score[u % 2][:, h, b * P:(b + 1) * P], ident[:, :])
            mm.then_inc(s_pT, 1)

        def values(u):
            n, g = divmod(u, KV_HEADS)
            pe.wait_ge(s_pT_cur, u + 1)
            if n:
                pe.wait_ge(s_pT_prev, prev_count(u + 1))
            if u:
                pe.wait_ge(s_o, u)
            blocks = (1, 0) if n else (1,)
            for h in range(PER_KV):
                for b in blocks:
                    mm = pe.matmul(ps_list[:, h * HEAD:(h + 1) * HEAD], pT[:, b, h, :],
                                   v_nat[:, n - 1 + b, g * HEAD:(g + 1) * HEAD],
                                   start=(b == 1), stop=(b == blocks[-1]))
            mm.then_inc(s_pv, 1)

        def project(n):
            pe.wait_ge(s_axtail, TILES + n + 1)
            pe.wait_ge(s_wotail, CHUNKS)
            for b in HALVES:
                for k in range(CHUNKS):
                    mm = product(ps_y[:, b, :], lambda a: xT[:, n % 2, a, k, :],
                                 lambda a: wo[:, a, k, b * BANK:(b + 1) * BANK], k == 0, k == CHUNKS - 1)
            mm.then_inc(s_wo, 1)

        for i in range(UNITS + 3):
            n = projected(i)
            if n is not None:
                pe.wait_ge(s_o, KV_HEADS * (n + 1))
                if n:
                    pe.wait_ge(s_wo_used, n)
                transpose_rows(q_nat[:, n, :], P, ps_y).then_inc(s_axT, 1)
            if i < UNITS:
                queries_transposed(i)
            if 2 <= i < UNITS + 2:
                weights_transposed(i - 2)
            if i < UNITS:
                scores(i)
            if 2 <= i < UNITS + 2:
                values(i - 2)
            if i == UNITS + 2:
                rows_transposed(1, 0)
            if n is not None:
                project(n)
        dense(1)
        rank(1)
        experts(1)

    ctx.close()


def kernel(**inputs):
    import concourse.bacc as bacc
    from concourse.bass_utils import run_bass_kernel_spmd

    names = ("x", "ln_gain", "ln_bias", "pool_w", "pool_scale", "attn_wqkv", "attn_bqkv", "attn_sinks", "attn_wo",
             "attn_bo", "router_w", "router_bias", "expert_w1", "expert_w3", "expert_w2", "shared_w1", "shared_w3",
             "shared_w2")
    nc = bacc.Bacc("TRN2", target_bir_lowering=False, num_devices=1)
    arrays, ins, consts = {}, {}, {}
    for name in names:
        a = np.ascontiguousarray(inputs[name])
        arrays[f"in_{name}"] = a
        ins[name] = nc.dram_tensor(f"in_{name}", a.shape, mybir.dt.from_np(a.dtype), kind="ExternalInput").ap()
    for name, a in shape_constants().items():
        a = np.ascontiguousarray(a)
        arrays[f"const_{name}"] = a
        consts[name] = nc.dram_tensor(f"const_{name}", a.shape, mybir.dt.from_np(a.dtype), kind="ExternalInput").ap()
    out = nc.dram_tensor("out", (1, SEQ, D), F32, kind="ExternalOutput").ap()
    build(nc, ins, consts, out)
    r = run_bass_kernel_spmd(nc, [arrays], core_ids=[0])
    return r.results[0]["out"]
```

```python
from contextlib import ExitStack

import numpy as np

import concourse.bass as bass
from concourse import mybir

F32 = mybir.dt.float32
F32R = mybir.dt.float32r
BF16 = mybir.dt.bfloat16
I32 = mybir.dt.int32
U32 = mybir.dt.uint32
ALU = mybir.AluOpType
ACT = mybir.ActivationFunctionType
AX = mybir.AxisListType

P = 128
SEQ = 512
D = 1024
TILES = SEQ // P
CHUNKS = D // P
LAYERS = 2
WINDOWS = (2, 4, 8, 16)
GROUP_CH = D // len(WINDOWS)
HEAD = 64
HEADS = D // HEAD
KV_HEADS = 4
PER_KV = HEADS // KV_HEADS
KV = KV_HEADS * HEAD
QKV = D + 2 * KV
EXPERTS = 64
TOP_K = 8
EXPERT_GROUPS = 8
PER_GROUP = EXPERTS // EXPERT_GROUPS
TOP_GROUPS = 4
FF = 256
FC = FF // P
ROUTED_SCALE = 2.5
EPS = 1e-5
ALPHA = (2 * LAYERS) ** 0.25
CAP = 88
ROUNDS = -(-SEQ // CAP)
MOVED = (64, 76, CAP)
FAR = -4096.0
LOW = -1.0e30
TAKEN = -3.0e38
FILLER = -2.0e38

UNIT = CHUNKS * FF
SLOTS = 6
PIECES = 2
PIECE = UNIT // PIECES
TAB = 6
BANK = 512


class Block:

    def __init__(self, q, r, expert=None):
        self.q, self.r, self.expert = q + r // 4, r % 4, expert

    def after(self, k):
        return Block(self.q, self.r + k, self.expert + k)

    def times(self, k, plus=0):
        return 4 * k * self.q + (k * self.r + plus)


def shape_constants():
    t = np.arange(P)
    pool = np.zeros((P, len(WINDOWS), 3, P), np.float32)
    for g, w in enumerate(WINDOWS):
        for kind in range(3):
            first = 0 if kind == 0 else P
            dst = first + t[None, :]
            src = t[:, None] + (first if kind < 2 else 0)
            inside = (src <= dst) & (src > dst - w)
            m = np.where(inside, 1.0 / np.minimum(dst + 1, w), 0.0)
            if kind < 2:
                m = m - (src == dst)
            pool[:, g, kind, :] = m
    slots = np.broadcast_to(np.arange(CAP, dtype=np.float32)[None, :], (P, CAP))
    dummy = np.stack([-(SEQ + t), SEQ + t], 1).astype(np.float32)
    inv = (10000.0 ** (-np.arange(0, HEAD, 2, dtype=np.float32) / np.float32(HEAD))).astype(np.float32)
    ang = (np.arange(SEQ, dtype=np.float32)[:, None] * inv[None, :]).astype(np.float32)
    rope = np.stack([np.cos(ang), np.sin(ang)], 1).astype(np.float32)
    rope = rope.reshape(TILES, P, 2, HEAD // 2).transpose(1, 0, 2, 3)
    ki = np.arange(2 * P)[None, :]
    band = np.where((ki > t[:, None]) & (ki <= t[:, None] + P), 0.0, LOW).astype(np.float32)
    return {
        "ident": np.eye(P, dtype=np.float32),
        "pool_band": pool,
        "slots": np.ascontiguousarray(slots),
        "dummy": dummy,
        "rope": np.ascontiguousarray(rope),
        "band": band,
    }


def build(nc, i, c, out):
    ctx = ExitStack()

    def sb(name, shape, dt=F32):
        return ctx.enter_context(nc.sbuf_tensor(name, shape, dt))

    def sem(name):
        return ctx.enter_context(nc.semaphore(name))

    raw = sb("raw", [P, SLOTS * UNIT])
    split = sb("split", [P, 2 * SLOTS * UNIT], F32R)
    xT = sb("xT", [P, 2, 2, CHUNKS, P], F32R)
    xn = sb("xn", [P, TILES, D])
    par = sb("par", [P, 3, D])
    rw = sb("rw", [P, 2, CHUNKS, EXPERTS], F32R)
    hT = sb("hT", [P, 2, FC, P], F32R)
    ident = sb("ident", [P, P])
    work = sb("work", [P, 3360])
    psum = ctx.enter_context(nc.psum_tensor("psum", [P, 8, BANK], F32))
    rows = nc.dram_tensor("rows", [SEQ, D], F32).ap()
    sums = [nc.dram_tensor(f"sums{l}", [SEQ + CAP, D], F32).ap() for l in range(LAYERS)]

    parf = par[:].rearrange("p a d -> p (a d)")

    def at(t, start, *dims, dt=F32):
        n = 1
        for d in dims:
            n *= d
        words = n * (2 if dt == BF16 else 4) // 4
        v = t[:, start:start + words]
        if dt != F32:
            v = v.bitcast(dt)
        if len(dims) == 1:
            return v
        names = "abcd"[:len(dims)]
        return v.rearrange(f"p ({' '.join(names)}) -> p {' '.join(names)}", **dict(zip(names, dims)))

    h_sb = at(work, 0, FC, P)
    oh = at(work, 256, 2, TILES, CAP, dt=BF16)
    tab = at(work, 640, TILES, EXPERTS, TAB, dt=BF16)
    ranks = at(work, 1408, TILES, EXPERTS)
    slots = at(work, 1664, CAP)
    order = at(work, 1760, 2, P, dt=BF16)
    xp = at(work, 1888, D)
    rw_raw = at(work, 0, CHUNKS, EXPERTS)
    k_nat = at(work, 0, TILES, KV)
    v_nat = at(work, 1024, TILES, KV)
    score = [at(work, 2048, PER_KV, 2 * P), at(raw, 7168, PER_KV, 2 * P)]
    router_bias = at(work, 3072, EXPERTS)
    negsink = at(work, 3136, HEADS)
    dummy = at(work, 3152, 2)
    stats = at(work, 3154, 2, 6)
    mean_var = at(work, 3166, 2)
    power = at(work, 3168, 3)
    slot_row = at(work, 3171, 1)
    index = work[:, 3172:3176].bitcast(I32)
    gate = at(work, 3176, 4)
    index_out = work[:, 3180:3184].bitcast(I32)
    most = at(work, 3184, 1)
    most_int = work[:, 3185:3186].bitcast(I32)
    top = at(work, 3188, PER_KV)
    negtop = at(work, 3192, 2, PER_KV)
    sink_arg = at(work, 3200, 2, PER_KV)
    total = at(work, 3208, 2, PER_KV)
    sink_exp = at(work, 3216, 2, PER_KV)
    inverse = at(work, 3224, 2, PER_KV)
    band = at(work, 3232, 2 * P, dt=BF16)
    counts = work[:, 2912:2976].bitcast(I32)
    prob = at(parf, 2048, TILES, EXPERTS)
    sel = at(parf, 2304, TILES, EXPERTS)
    rest = at(parf, 2560, TILES, EXPERTS)
    chosen = at(parf, 2816, TILES, EXPERTS, dt=BF16)
    gsum = at(parf, 2944, TILES)
    group_top = at(work, 256, TILES, EXPERT_GROUPS, 8)
    gext = at(work, 512, TILES, EXPERT_GROUPS + 4)
    gtop = at(work, 560, TILES, 8)
    etop = at(work, 592, TILES, 8)
    xg = [xn[:, b, :] for b in range(2)]
    yo = [xn[:, 2 + b, :] for b in range(2)]
    pool_band = at(raw, 8192, len(WINDOWS), 3, P)
    pool_w = at(raw, 9728, len(WINDOWS), 2, GROUP_CH)
    pooled = [at(work, 1888, CHUNKS, P), at(work, 640, CHUNKS, P)]
    wqkv_raw = at(raw, 0, CHUNKS, QKV)
    wqkv = split[:, :].rearrange("p (s c n) -> p s c n", s=2, c=CHUNKS)
    wo_raw = at(raw, 0, 3, D)
    wo = split[:, 4 * UNIT:4 * UNIT + 2 * CHUNKS * D].rearrange("p (s c n) -> p s c n", s=2, c=CHUNKS)
    band_raw = at(raw, 3072, 2 * P)
    kT = at(raw, 4096, KV_HEADS, 2, P)
    qT = [at(raw, 5120 + 512 * b, PER_KV, P) for b in range(2)]
    pT = at(raw, 6144, 2, PER_KV, P)
    q_nat = at(raw, 8192, TILES, D)
    bqkv = at(parf, 0, QKV)
    rope = at(parf, QKV, TILES, 2, HEAD // 2)
    bo = par[:, 2, :]

    def raw_slot(slot):
        return raw[:, slot * UNIT:(slot + 1) * UNIT]

    def split_slot(slot):
        return split[:, 2 * slot * UNIT:2 * (slot + 1) * UNIT].rearrange("p (s n) -> p s n", s=2)

    ps_xT = psum[:, 0:2, :]
    ps_h = psum[:, 2, :]
    ps_hT = psum[:, 3, :]
    ps_list = psum[:, 4, :]
    ps_y = psum[:, 5:7, :]
    ps_log = psum[:, 7, :]

    def in_chunks(banks, m=P):
        return banks[:, :, 0:4 * m].rearrange("p b (c t) -> p b c t", c=4)

    def qkv_ps(t):
        return psum[:, 5:8, :] if t % 2 == 0 else psum[:, 2:5, :]

    s_const = sem("s_const")
    s_x = [sem(f"s_x{t}") for t in range(TILES)]
    s_pool_band = sem("s_pool_band")
    s_pool_w = sem("s_pool_w")
    s_pool_scale = sem("s_pool_scale")
    s_pool_scaled = sem("s_pool_scaled")
    s_par = sem("s_par")
    s_dve = sem("s_dve")
    s_power = sem("s_power")
    s_pool_waited = sem("s_pool_waited")
    s_sp_waited = sem("s_sp_waited")
    s_dve_waited = sem("s_dve_waited")
    s_pooled = sem("s_pooled")
    s_pooled_sb = sem("s_pooled_sb")
    s_mix = sem("s_mix")
    s_mix_used = sem("s_mix_used")
    s_var = sem("s_var")
    s_vareps = sem("s_vareps")
    s_rstd = sem("s_rstd")
    s_norm = sem("s_norm")
    s_rw_in = sem("s_rw_in")
    s_rw_head = sem("s_rw_head")
    s_rw_tail = sem("s_rw_tail")
    s_moe_const = sem("s_moe_const")
    per_layer = ("xp", "rows_out", "logits", "prob", "order", "chosen", "ranked", "most",
                 "head", "tail", "xTready", "xhead", "xtail", "m1", "silu", "hidden", "hTready", "hhead",
                 "htail", "m2", "yout", "oh", "listed", "slotrow", "index", "idxcopy", "slots",
                 "pe_idle", "split_over")
    S = [{n: sem(f"s_{n}{l}") for n in per_layer} for l in range(LAYERS)]
    s_w = [[sem(f"s_w{l}_{k}") for k in range(SLOTS)] for l in range(LAYERS)]
    s_xg = [[sem(f"s_xg{l}_{b}") for b in range(2)] for l in range(LAYERS)]
    s_scat = [[sem(f"s_scat{l}_{b}") for b in range(2)] for l in range(LAYERS)]
    s_acc_out = [sem(f"s_acc_out{l}") for l in range(LAYERS)]
    s_acc_last = [sem(f"s_acc_last{l}") for l in range(LAYERS)]
    s_acc_in = [[sem(f"s_acc_in{l}_{t}") for t in range(TILES)] for l in range(LAYERS)]
    s_out = sem("s_out")
    s_wqkv = [sem(f"s_wqkv{k}") for k in range(CHUNKS)]
    s_qhead = sem("s_qhead")
    s_qtail = sem("s_qtail")
    s_axT = sem("s_axT")
    s_axhead = sem("s_axhead")
    s_axtail = sem("s_axtail")
    s_qkv = sem("s_qkv")
    s_qkv_used = sem("s_qkv_used")
    s_roped = sem("s_roped")
    s_wo_in = [sem(f"s_wo_in{k}") for k in range(3)]
    s_wohead = sem("s_wohead")
    s_wotail = sem("s_wotail")
    s_qT = sem("s_qT")
    s_qT_sb = sem("s_qT_sb")
    s_kT = sem("s_kT")
    s_kT_sb = sem("s_kT_sb")
    s_score = sem("s_score")
    s_masked = sem("s_masked")
    s_negtop = sem("s_negtop")
    s_exp = sem("s_exp")
    s_pT = sem("s_pT")
    s_pT_cur = sem("s_pT_cur")
    s_pT_prev = sem("s_pT_prev")
    s_pv = sem("s_pv")
    s_o = sem("s_o")
    s_wo = sem("s_wo")
    s_wo_used = sem("s_wo_used")
    s_band = sem("s_band")
    s_band_copied = sem("s_band_copied")

    UNITS = TILES * KV_HEADS
    HALVES = (0, 1)
    WQKV_ORDER = (4, 5, 6, 7, 0, 1, 2, 3)
    PASSES = ((0, 0), (0, 1), (1, 0))

    def projected(i):
        return (i - 6) // KV_HEADS if 6 <= i < UNITS + 6 and i % KV_HEADS == 2 else None

    def prev_count(n):
        return max(0, n - KV_HEADS)

    def run_steps(eng, rnd, body):
        base = EXPERTS // 4 * rnd + 1

        def peeled(s):
            body(Block(base, s, s), lambda k: 0 <= s + k < EXPERTS)

        for s in range(-3, 5):
            peeled(s)
        with eng.Fori(0, 14) as q:
            for r in range(4):
                body(Block(base + 1 + q, 1 + r, 4 * q + (5 + r)), lambda k: True)
        for s in range(61, 66):
            peeled(s)

    def run_rounds(eng, l, one_round):
        if eng is nc.sync:
            one_round(0)
        eng.wait_ge(S[l]["most"], 1)
        most_tokens = eng.value_load(most_int[0:1, 0:1], min_val=0, max_val=SEQ)
        if eng is not nc.sync:
            one_round(0)
        with eng.If(most_tokens > CAP):
            with eng.Fori(1, ROUNDS) as rnd:
                with eng.If(most_tokens > rnd * CAP):
                    one_round(rnd)
                eng.nop()
        eng.nop()

    def first_of_all(b):
        return isinstance(b.q, int) and b.times(1) == 4

    def split_early(b):
        return isinstance(b.q, int) and b.times(1) in (4, 5)

    def weight_unit(b, u):
        k = 3 * (b.r + 1) + u
        return k % SLOTS, 2 * (b.q - 1) + k // SLOTS + 1

    block = ctx.enter_context(nc.Block())

    @block.sync
    def _(sp):
        def load_par(vectors):
            for dst, src in vectors:
                sp.dma_start(dst, src).then_inc(s_par, 16)

        def bc(v):
            return v.partition_broadcast(P)

        def expert_matrix(l, n, u, slot):
            if u < 2:
                w = i["expert_w1" if u == 0 else "expert_w3"]
            else:
                w = i["expert_w2"]
            src = w[l].rearrange("e (p a) f -> p e (a f)", p=P)[:, bass.ds(n, 1), :]
            return sp.dma_start(raw_slot(slot).rearrange("p (e n) -> p e n", e=1), src)

        def shared_matrix(l, u):
            w = i[("shared_w1", "shared_w3", "shared_w2")[u]][l]
            sp.dma_start(raw_slot(u), w.rearrange("(p a) f -> p (a f)", p=P)).then_inc(s_w[l][u], 16)

        def moe_consts(l):
            sp.dma_start(slots, c["slots"]).then_inc(s_moe_const, 16)
            sp.dma_start(router_bias, bc(i["router_bias"][l])).then_inc(s_moe_const, 16)

        def experts(l):
            def one(b, u, e, wait):
                slot, _ = weight_unit(b, u)
                if wait:
                    sp.wait_ge(S[l]["tail"], b.times(3 * PIECES, PIECES * (u - 14)))
                expert_matrix(l, e, u, slot).then_inc(s_w[l][slot], 16)

            def one_round(rnd):
                base = 16 * rnd + 1
                if isinstance(rnd, int):
                    first = 4
                    for n in range(1, first):
                        for u in range(3):
                            one(Block(1, n), u, n, True)
                    with sp.Fori(1, EXPERTS // 4) as q:
                        for r in range(4):
                            for u in range(3):
                                one(Block(base + q, r), u, 4 * q + r, True)
                else:
                    with sp.Fori(0, EXPERTS // 4) as q:
                        for r in range(4):
                            for u in range(3):
                                one(Block(base + q, r), u, 4 * q + r, True)
                sp.wait_ge(S[l]["tail"], 3 * PIECES * EXPERTS * (rnd + 1))
                sp.sem_inc(s_sp_waited, 1)

            run_rounds(sp, l, one_round)

        def load_x(t):
            sp.dma_start(xn[:, t, :], i["x"][0, t * P:(t + 1) * P, :]).then_inc(s_x[t], 16)

        load_x(0)
        sp.dma_start(pool_band, c["pool_band"]).then_inc(s_pool_band, 16)
        sp.dma_start(pool_w, i["pool_w"][0].rearrange("g (k p) n -> p g k n", p=P)).then_inc(s_pool_w, 16)
        sp.dma_start(par[:, 2, :], bc(i["pool_scale"][0])).then_inc(s_pool_scale, 16)
        load_x(1)
        load_par([(par[:, 0, :], bc(i["ln_gain"][0, 0])), (par[:, 1, :], bc(i["ln_bias"][0, 0]))])
        load_x(2)
        sp.dma_start(ident[:], c["ident"]).then_inc(s_const, 16)
        sp.dma_start(dummy, c["dummy"]).then_inc(s_const, 16)
        load_x(3)
        sp.dma_start(rw_raw, i["router_w"][0].rearrange("(p a) e -> p a e", p=P)).then_inc(s_rw_in, 16)
        moe_consts(0)
        for u in range(3):
            shared_matrix(0, u)
        expert_matrix(0, 0, 0, 3).then_inc(s_w[0][3], 16)
        sp.wait_ge(s_norm, 1 * TILES)
        for u in (1, 2):
            expert_matrix(0, 0, u, 3 + u).then_inc(s_w[0][3 + u], 16)
        load_par([(par[:, 0, :], bc(i["ln_gain"][0, 1])), (par[:, 1, :], bc(i["ln_bias"][0, 1]))])
        experts(0)

        for k in WQKV_ORDER:
            if k == 0:
                sp.wait_ge(S[0]["split_over"], 1)
                for t in range(TILES):
                    sp.wait_ge(s_acc_in[0][t], 16)
            sp.dma_start(wqkv_raw[:, k, :], i["attn_wqkv"][0, k * P:(k + 1) * P, :]).then_inc(s_wqkv[k], 16)
        sp.wait_ge(s_norm, 2 * TILES)
        load_par([(bqkv, bc(i["attn_bqkv"][0])), (rope, c["rope"]), (bo, bc(i["attn_bo"][0])),
                  (negsink, bc(i["attn_sinks"][0]))])
        sp.wait_ge(s_qtail, CHUNKS)
        sp.dma_start(band_raw, c["band"]).then_inc(s_band, 16)
        for k in range(CHUNKS):
            if k >= 3:
                sp.wait_ge(s_wotail, k - 2)
            sp.dma_start(wo_raw[:, k % 3, :], i["attn_wo"][0, k * P:(k + 1) * P, :]).then_inc(s_wo_in[k % 3], 16)
        sp.wait_ge(s_roped, TILES)
        load_par([(par[:, 0, :], bc(i["ln_gain"][1, 0])), (par[:, 1, :], bc(i["ln_bias"][1, 0]))])
        sp.wait_ge(s_wotail, CHUNKS)
        sp.wait_ge(s_band_copied, 1)
        for u in range(2):
            shared_matrix(1, u)
        sp.wait_ge(s_o, UNITS)
        sp.wait_ge(s_pv, UNITS)
        shared_matrix(1, 2)
        sp.dma_start(rw_raw, i["router_w"][1].rearrange("(p a) e -> p a e", p=P)).then_inc(s_rw_in, 16)
        moe_consts(1)
        expert_matrix(1, 0, 0, 3).then_inc(s_w[1][3], 16)
        sp.wait_ge(s_axT, 2 * TILES)
        for u in (1, 2):
            expert_matrix(1, 0, u, 3 + u).then_inc(s_w[1][3 + u], 16)
        sp.wait_ge(s_norm, 3 * TILES)
        load_par([(par[:, 0, :], bc(i["ln_gain"][1, 1])), (par[:, 1, :], bc(i["ln_bias"][1, 1]))])
        experts(1)
        for t in range(TILES):
            sp.wait_ge(s_norm, 3 * TILES + t + 1)
            sp.dma_start(out[0, t * P:(t + 1) * P, :], xn[:, t, :]).then_inc(s_out, 16)
        sp.wait_ge(s_out, 16 * TILES)

    @block.gpsimd
    def _(pool):
        pool.memset(power[:, 0:1], -0.5).then_inc(s_power, 1)
        pool.wait_ge(s_power, 1)

        def hold_waits():
            pool.sem_inc(s_pool_waited, 1)

        def rstd(n):
            pool.wait_ge(s_var, n + 1)
            pool.tensor_scalar(power[:, 1:2], mean_var[:, 1:2], EPS, None, ALU.add).then_inc(s_vareps, 1)
            pool.wait_ge(s_vareps, n + 1)
            pool.tensor_tensor(power[:, 2:3], power[:, 1:2], power[:, 0:1], ALU.pow).then_inc(s_rstd, 1)

        def rows_and_sums(l):
            for t in range(TILES):
                if l and t == TILES - 1:
                    store_rows(l, 0)
                rstd(2 * l * TILES + t)
            for t in range(l, TILES):
                store_rows(l, t)

        def store_rows(l, t):
            pool.wait_ge(S[l]["xp"], t + 1)
            pool.dma_start(rows[t * P:(t + 1) * P, :], xp).then_inc(S[l]["rows_out"], 16)

        def order_matrices(l):
            if l:
                pool.wait_ge(s_o, UNITS)
            pool.memset(order, 1.0).then_inc(S[l]["order"], 1)
            pool.wait_ge(S[l]["order"], 1)
            pool.affine_select(out=order[:, 0, :], in_=order[:, 0, :], compare_op=ALU.is_gt, fill=0.0, base=0,
                               pattern=[[1, P]], channel_multiplier=-1).then_inc(S[l]["order"], 1)

        def store_sums(l):
            for t in range(TILES):
                pool.wait_ge(S[l]["yout"], t + 1)
                landed = s_acc_out[l] if t < TILES - 1 else s_acc_last[l]
                pool.dma_start(sums[l][t * P:(t + 1) * P, :], xn[:, t, :]).then_inc(landed, 16)
                if t == 0:
                    pool.dma_start(sums[l][SEQ:SEQ + CAP, :], xn[0:CAP, 0, :]).then_inc(s_acc_out[l], 16)
            pool.wait_ge(S[l]["rows_out"], 16 * TILES)
            pool.wait_ge(s_acc_out[l], 16 * TILES)

        def experts(l):
            s = S[l]

            def rows_moved(n, rnd, move, landed):
                tokens = pool.value_load(counts[0:1, bass.ds(n.expert, 1)], min_val=0, max_val=SEQ)

                def at_least(k):
                    if k == len(MOVED) - 1:
                        move(MOVED[k]).then_inc(landed, 16)
                        return
                    with pool.If(tokens > rnd * CAP + MOVED[k]):
                        at_least(k + 1)
                    with pool.Else():
                        move(MOVED[k]).then_inc(landed, 16)

                at_least(0)

            def body_of(rnd):
                def body(b, valid):
                    if valid(2):
                        n = b.after(2)
                        pool.wait_ge(s["index"], n.times(1, 1 - 4))
                        pool.wait_ge(s["xTready"], n.times(1, -1))
                        hold_waits()

                        def gather(m):
                            return pool.indirect_dma_start(
                                xg[n.r % 2][0:m, :], None, rows[:, :],
                                bass.IndirectOffsetOnAxis(ap=index[0:m, n.r:n.r + 1].bitcast(U32), axis=0),
                                bounds_check=SEQ - 1, oob_is_err=False)

                        rows_moved(n, rnd, gather, s_xg[l][n.r % 2])
                    if valid(0):
                        pool.wait_ge(s["index"], b.times(1, 1 - 4))
                        hold_waits()
                        pool.tensor_copy(index_out[0:CAP, b.r:b.r + 1],
                                         index[0:CAP, b.r:b.r + 1]).then_inc(s["idxcopy"], 1)
                    if valid(-2):
                        n = b.after(-2)
                        pool.wait_ge(s["yout"], n.times(1, 1))
                        pool.wait_ge(s["idxcopy"], n.times(1, 1 - 4))
                        if first_of_all(n):
                            pool.wait_ge(s_acc_last[l], 16)
                        else:
                            before = n.after(-1)
                            pool.wait_ge(s_scat[l][before.r % 2], 16 * (2 * (before.q - 1) + before.r // 2 + 1))
                        hold_waits()

                        def scatter(m):
                            return pool.indirect_dma_start(
                                sums[l][:, :],
                                bass.IndirectOffsetOnAxis(ap=index_out[0:m, n.r:n.r + 1].bitcast(U32), axis=0),
                                yo[n.r % 2][0:m, :], None, compute_op=ALU.add)

                        rows_moved(n, rnd, scatter, s_scat[l][n.r % 2])
                return body

            def one_round(rnd):
                run_steps(pool, rnd, body_of(rnd))
                for b in range(2):
                    pool.wait_ge(s_scat[l][b], 16 * (EXPERTS // 2) * (rnd + 1))
                hold_waits()

            run_rounds(pool, l, one_round)
            pool.wait_ge(s["pe_idle"], 1)
            for t in range(TILES):
                pool.dma_start(xn[:, t, :], sums[l][t * P:(t + 1) * P, :]).then_inc(s_acc_in[l][t], 16)

        for l in range(LAYERS):
            rows_and_sums(l)
            order_matrices(l)
            store_sums(l)
            experts(l)
            for t in range(TILES):
                rstd((2 * l + 1) * TILES + t)

    @block.scalar
    def _(act):
        def matrix_head(l, slot, landed, piece):
            if piece == 0:
                act.wait_ge(s_w[l][slot], 16 * landed)
            cols = slice(piece * PIECE, (piece + 1) * PIECE)
            act.activation(split_slot(slot)[:, 0, cols], raw_slot(slot)[:, cols], ACT.Copy).then_inc(S[l]["head"], 1)

        def rows_head(s, b, m, waits, banks=ps_xT):
            for sm, v in waits:
                act.wait_ge(sm, v)
            act.activation(xT[:, b % 2, 0, :, 0:m].rearrange("p (b c) t -> p b c t", b=2), in_chunks(banks, m),
                           ACT.Copy).then_inc(s, 1)

        def silu(l, b, m):
            act.wait_ge(S[l]["m1"], b.times(1, 1))
            if not (isinstance(b.q, int) and b.times(1) == 0):
                act.wait_ge(S[l]["hTready"], b.times(1))
            act.activation(h_sb[0:m], ps_h[0:m, 0:FF].rearrange("p (a j) -> p j a", j=FC), ACT.Silu).then_inc(S[l]["silu"], 1)

        def hidden_head(l, b, m):
            act.wait_ge(S[l]["hTready"], b.times(1, 1))
            if not (isinstance(b.q, int) and b.times(1) == 0):
                act.wait_ge(S[l]["m2"], b.times(1))
            act.activation(hT[:, 0, :, 0:m], ps_hT[:, 0:FC * m].rearrange("p (j t) -> p j t", j=FC),
                           ACT.Copy).then_inc(S[l]["hhead"], 1)

        def dense(l):
            s = S[l]

            def ordered_rows(t):
                act.wait_ge(s_norm, 2 * l * TILES + t + 1)
                if t:
                    act.wait_ge(s["xTready"], t)
                    act.wait_ge(s["rows_out"], 16 * t)
                elif l == 0:
                    act.wait_ge(s_mix, TILES)
                act.activation(xp.rearrange("p (c a) -> p c a", c=CHUNKS),
                               xn[:, t, :].rearrange("p (a c) -> p c a", c=CHUNKS), ACT.Copy).then_inc(s["xp"], 1)

            def head(t):
                act.wait_ge(s["xTready"], t + 1)
                rows_head(s["xhead"], t, P, [(s["logits"], t - 1)] if t >= 2 else [])

            if l:
                act.wait_ge(s_pv, UNITS)
                act.wait_ge(s_wo, TILES - 1)
            ordered_rows(0)
            head(0)
            if l:
                router_head(1)
                act.wait_ge(s_wo, TILES)
                for piece in range(PIECES):
                    matrix_head(1, 2, 1, piece)
            ordered_rows(1)
            act.wait_ge(s_rw_tail, l + 1)
            def first_expert(u):
                for piece in range(PIECES):
                    matrix_head(l, 3 + u, 1, piece)

            for t in range(TILES - 2):
                silu(l, Block(0, t), P)
                hidden_head(l, Block(0, t), P)
                head(t + 1)
                ordered_rows(t + 2)
                first_expert(t)
            head(TILES - 1)
            first_expert(2)
            silu(l, Block(0, TILES - 2), P)
            hidden_head(l, Block(0, TILES - 2), P)
            act.wait_ge(s["logits"], TILES)
            act.activation(prob, ps_log[:, 0:TILES * EXPERTS].rearrange("p (t e) -> p t e", t=TILES),
                           ACT.Sigmoid).then_inc(s["prob"], 1)
            silu(l, Block(0, TILES - 1), P)
            hidden_head(l, Block(0, TILES - 1), P)
            act.wait_ge(s["m2"], TILES)
            for u in range(3):
                for piece in range(PIECES):
                    matrix_head(l, u, 2, piece)

        def experts(l):
            s = S[l]

            def body(b, valid):
                if valid(-2):
                    n = b.after(-2)
                    act.wait_ge(s["m2"], n.times(1, 1))
                    if first_of_all(n):
                        act.wait_ge(s_acc_last[l], 16)
                    if not (isinstance(n.q, int) and n.q == 1 and n.r < 2):
                        old = n.after(-2)
                        act.wait_ge(s_scat[l][n.r % 2], 16 * (2 * (old.q - 1) + old.r // 2 + 1))
                    act.activation(yo[n.r % 2][0:CAP].rearrange("p (b n) -> p b n", b=2), ps_y[0:CAP], ACT.Copy,
                                   scale=gate[0:CAP, n.r:n.r + 1]).then_inc(s["yout"], 1)
                if valid(-1):
                    hidden_head(l, b.after(-1), CAP)
                if valid(1):
                    n = b.after(1)
                    rows_head(s["xhead"], n.r, CAP, [(s["xTready"], n.times(1, 1)), (s["m1"], n.times(1, -1))])
                if valid(0) and not split_early(b):
                    slot, landed = weight_unit(b, 2)
                    act.wait_ge(s["m2"], b.times(1, -1))
                    for piece in range(PIECES):
                        matrix_head(l, slot, landed, piece)
                if valid(1) and not split_early(b.after(1)):
                    n = b.after(1)
                    act.wait_ge(s["m1"], n.times(1, -1))
                    slot, landed = weight_unit(n, 0)
                    for piece in range(PIECES):
                        matrix_head(l, slot, landed, piece)
                    slot, landed = weight_unit(n, 1)
                    matrix_head(l, slot, landed, 0)
                if valid(0):
                    silu(l, b, CAP)
                if valid(1) and not split_early(b.after(1)):
                    matrix_head(l, slot, landed, 1)

            run_rounds(act, l, lambda rnd: run_steps(act, rnd, body))

        def router_head(l):
            act.wait_ge(s_rw_in, 16 * (l + 1))
            act.activation(rw[:, 0], rw_raw, ACT.Copy).then_inc(s_rw_head, 1)

        for t in range(TILES):
            act.wait_ge(s_pooled, t + 1)
            if t >= 2:
                act.wait_ge(s_mix, t - 1)
            act.activation(pooled[t % 2].rearrange("p (b c) t -> p b (c t)", b=2), ps_xT,
                           ACT.Copy).then_inc(s_pooled_sb, 1)
            if t == 1:
                router_head(0)
            if t == 2:
                for piece in range(PIECES):
                    matrix_head(0, 0, 1, piece)
        for u in (1, 2):
            for piece in range(PIECES):
                matrix_head(0, u, 1, piece)
        dense(0)
        experts(0)

        act.wait_ge(S[0]["pe_idle"], 1)
        for n, k in enumerate(WQKV_ORDER):
            act.wait_ge(s_wqkv[k], 16)
            act.activation(wqkv[:, 0, k, :], wqkv_raw[:, k, :], ACT.Copy).then_inc(s_qhead, 1)
            if n == CHUNKS // 2 - 1:
                rows_head(s_axhead, 0, P, [(s_axT, 1)])
        for t in range(1, TILES):
            waits = [(s_axT, t + 1)]
            if t >= 2:
                waits.append((s_qkv, t - 1))
            rows_head(s_axhead, t, P, waits)

        def wo_head(k):
            act.wait_ge(s_wo_in[k % 3], 16 * (k // 3 + 1))
            act.activation(wo[:, 0, k, :], wo_raw[:, k % 3, :], ACT.Copy).then_inc(s_wohead, 1)

        act.wait_ge(s_qkv, TILES)

        def queries_out(u):
            n, g = divmod(u, KV_HEADS)
            act.wait_ge(s_qT, u + 1)
            if u >= 2:
                act.wait_ge(s_score, u - 1)
            act.activation(qT[u % 2][0:HEAD], ps_hT[0:HEAD, :].rearrange("p (h t) -> p h t", h=PER_KV),
                           ACT.Copy).then_inc(s_qT_sb, 1)
            if g == 0:
                act.wait_ge(s_kT, n + 1)
                act.activation(kT[0:HEAD, :, n % 2, :], ps_list[0:HEAD].rearrange("p (g t) -> p g t", g=KV_HEADS),
                               ACT.Copy).then_inc(s_kT_sb, 1)

        def exponentials(u):
            keys = slice(0 if u // KV_HEADS else P, 2 * P)
            act.wait_ge(s_negtop, u + 1)
            for h in range(PER_KV):
                act.activation(score[u % 2][:, h, keys], score[u % 2][:, h, keys], ACT.Exp,
                               bias=negtop[:, u % 2, h:h + 1], accum_out=total[:, u % 2, h:h + 1])
            act.activation(sink_exp[:, u % 2, :], sink_arg[:, u % 2, :], ACT.Exp).then_inc(s_exp, 1)

        def weights_out(u):
            act.wait_ge(s_pT, u + 1)
            if u:
                act.wait_ge(s_pv, u)
            act.activation(pT[:, 1], ps_h.rearrange("p (h t) -> p h t", h=PER_KV), ACT.Copy).then_inc(s_pT_cur, 1)

        for i in range(UNITS + 3):
            if projected(i) is not None:
                n = projected(i)
                waits = [(s_axT, TILES + n + 1)]
                if n >= 2:
                    waits.append((s_wo, n - 1))
                rows_head(s_axhead, n, P, waits, ps_y)
            if i < UNITS:
                queries_out(i)
            if 2 <= i < UNITS + 2:
                weights_out(i - 2)
            if 1 <= i < UNITS + 1:
                exponentials(i - 1)
            if i < 4:
                wo_head(2 * i)
                wo_head(2 * i + 1)
            if 9 <= i < 9 + 2 * PIECES:
                matrix_head(1, (i - 9) // PIECES, 1, (i - 9) % PIECES)
        dense(1)
        experts(1)

    @block.vector
    def _(dve):
        links = [0]

        def link(ins):
            links[0] += 1
            ins.then_inc(s_dve, 1)
            dve.wait_ge(s_dve, links[0])

        norms = [0]

        def layer_norm(t):
            norm_stats(t)
            norm_apply(t)

        def norm_stats(t):
            x = xn[:, t, :]
            for h in HALVES:
                last = dve.bn_stats(stats[:, h, :], x[:, h * BANK:(h + 1) * BANK])
            link(last)
            dve.bn_aggr(mean_var, stats).then_inc(s_var, 1)
            norms[0] += 1

        def norm_apply(t):
            x = xn[:, t, :]
            dve.wait_ge(s_var, norms[0])
            link(dve.scalar_tensor_tensor(out=x, in0=x, scalar=mean_var[:, 0:1], in1=par[:, 0, :],
                                          op0=ALU.subtract, op1=ALU.mult))
            dve.wait_ge(s_rstd, norms[0])
            dve.scalar_tensor_tensor(out=x, in0=x, scalar=power[:, 2:3], in1=par[:, 1, :],
                                     op0=ALU.mult, op1=ALU.add).then_inc(s_norm, 1)

        def matrix_tail(l, slot, piece, count):
            dve.wait_ge(S[l]["head"], count)
            cols = slice(piece * PIECE, (piece + 1) * PIECE)
            w = split_slot(slot)
            dve.tensor_tensor(w[:, 1, cols], raw_slot(slot)[:, cols], w[:, 0, cols].bitcast(F32),
                              ALU.subtract).then_inc(S[l]["tail"], 1)

        def unit_count(b, u, piece):
            return b.times(3 * PIECES, PIECES * (u - 12 + 3) + piece + 1)

        def rows_tail(head, n, tail, b, m, banks=ps_xT):
            dve.wait_ge(head, n)
            dst = xT[:, b % 2, 1, :, 0:m].rearrange("p (b c) t -> p b c t", b=2)
            hd = xT[:, b % 2, 0, :, 0:m].rearrange("p (b c) t -> p b c t", b=2).bitcast(F32)
            for h in HALVES:
                last = dve.tensor_tensor(dst[:, h], in_chunks(banks, m)[:, h], hd[:, h], ALU.subtract)
            last.then_inc(tail, 1)

        def hidden(l, b, m):
            dve.wait_ge(S[l]["silu"], b.times(1, 1))
            dve.tensor_tensor(h_sb[0:m], h_sb[0:m], ps_h[0:m, FF:2 * FF].rearrange("p (a j) -> p j a", j=FC),
                              ALU.mult).then_inc(S[l]["hidden"], 1)

        def hidden_tail(l, b, m):
            dve.wait_ge(S[l]["hhead"], b.times(1, 1))
            dve.tensor_tensor(hT[:, 1, :, 0:m], ps_hT[:, 0:FC * m].rearrange("p (j t) -> p j t", j=FC),
                              hT[:, 0, :, 0:m].bitcast(F32), ALU.subtract).then_inc(S[l]["htail"], 1)

        def router_tail(l):
            dve.wait_ge(s_rw_head, l + 1)
            dve.tensor_tensor(rw[:, 1], rw_raw, rw[:, 0].bitcast(F32), ALU.subtract).then_inc(s_rw_tail, 1)

        def shared_tile(l, t):
            dve.wait_ge(S[l]["m2"], t + 1)
            dve.wait_ge(S[l]["xp"], t + 1)
            x = xn[:, t, :].rearrange("p (b n) -> p b n", b=2)
            for h in HALVES:
                last = dve.scalar_tensor_tensor(out=x[:, h], in0=x[:, h], scalar=ALPHA, in1=ps_y[:, h],
                                                op0=ALU.mult, op1=ALU.add)
            last.then_inc(S[l]["yout"], 1)

        def first_expert(l, u):
            for piece in range(PIECES):
                matrix_tail(l, 3 + u, piece, unit_count(Block(1, 0), u, piece))

        def route(l):
            s = S[l]
            dve.wait_ge(s["prob"], 1)
            dve.wait_ge(s_moe_const, 32 * (l + 1))
            link(dve.tensor_tensor(sel, prob, router_bias.unsqueeze(1).to_broadcast([P, TILES, EXPERTS]), ALU.add))
            for t in range(TILES):
                for g in range(EXPERT_GROUPS):
                    last = dve.max(group_top[:, t, g, :], sel[:, t, g * PER_GROUP:(g + 1) * PER_GROUP])
            dve.memset(gext[:, :, EXPERT_GROUPS:], FILLER)
            link(last)
            shared_tile(l, TILES - 2)
            link(dve.tensor_tensor(gext[:, :, 0:EXPERT_GROUPS], group_top[:, :, :, 0], group_top[:, :, :, 1], ALU.add))
            for t in range(TILES):
                last = dve.max(gtop[:, t, :], gext[:, t, :])
            link(last)
            link(dve.memset(gtop[:, :, TOP_GROUPS:], FILLER))
            for t in range(TILES):
                last = dve.match_replace(gext[:, t, :], gtop[:, t, :], gext[:, t, :], TAKEN)
            link(last)
            groups = gext[:, :, 0:EXPERT_GROUPS]
            link(dve.tensor_scalar(groups, groups, TAKEN, None, ALU.is_equal))
            wide = groups.unsqueeze(3).to_broadcast([P, TILES, EXPERT_GROUPS, PER_GROUP])
            sel4 = sel.rearrange("p t (g k) -> p t g k", k=PER_GROUP)
            rest4 = rest.rearrange("p t (g k) -> p t g k", k=PER_GROUP)
            link(dve.tensor_tensor(sel4, sel4, wide, ALU.mult))
            link(dve.tensor_scalar(rest4, wide, -LOW, LOW, ALU.mult, ALU.add))
            link(dve.tensor_tensor(sel, sel, rest, ALU.add))
            hidden(l, Block(0, TILES - 1), P)
            for t in range(TILES):
                last = dve.max(etop[:, t, :], sel[:, t, :])
            link(last)
            hidden_tail(l, Block(0, TILES - 1), P)
            for t in range(TILES):
                last = dve.match_replace(rest[:, t, :], etop[:, t, :], sel[:, t, :], TAKEN)
            link(last)
            link(dve.tensor_scalar(rest, rest, TAKEN, None, ALU.is_equal))
            dve.tensor_copy(chosen, rest).then_inc(s["chosen"], 1)
            link(dve.tensor_tensor(prob, prob, rest, ALU.mult))
            link(dve.tensor_reduce(gsum, prob, AX.X, ALU.add))
            link(dve.reciprocal(gsum, gsum))
            link(dve.tensor_tensor(prob, prob, gsum.unsqueeze(2).to_broadcast([P, TILES, EXPERTS]), ALU.mult))
            link(dve.tensor_scalar(prob, prob, ROUTED_SCALE, None, ALU.mult))
            for k in range(3):
                link(dve.tensor_copy(tab[:, :, :, 3 + k], prob))
                if k < 2:
                    link(dve.tensor_tensor(prob, prob, tab[:, :, :, 3 + k], ALU.subtract))
            shared_tile(l, TILES - 1)
            dve.wait_ge(s["ranked"], 1)
            link(dve.tensor_tensor(ranks, ps_list[:, 0:256].rearrange("p (t e) -> p t e", t=TILES), rest, ALU.mult))
            link(dve.tensor_scalar(rest, rest, -FAR, FAR, ALU.mult, ALU.add))
            dve.tensor_reduce(most, ps_list[:, 256:256 + EXPERTS], AX.X, ALU.max)
            link(dve.tensor_tensor(ranks, ranks, rest, ALU.add))
            dve.tensor_copy(counts, ps_list[:, 256:256 + EXPERTS])
            dve.tensor_copy(most_int, most).then_inc(s["most"], 1)

        def experts(l):
            s = S[l]

            def body(b, valid):
                if valid(-1):
                    hidden_tail(l, b.after(-1), CAP)
                if valid(3):
                    n = b.after(3)
                    if not (isinstance(n.q, int) and n.q == 1 and n.r < 2):
                        dve.wait_ge(s["listed"], n.times(1, -1 - 4))
                    dve.tensor_tensor(oh[:, n.r % 2],
                                      ranks[:, :, bass.ds(n.expert, 1)].to_broadcast([P, TILES, CAP]),
                                      slots.unsqueeze(1).to_broadcast([P, TILES, CAP]),
                                      ALU.is_equal).then_inc(s["oh"], 1)
                if valid(2):
                    n = b.after(2)
                    dve.wait_ge(s["listed"], n.times(1, 1 - 4))
                    first = isinstance(n.q, int) and n.q == 1
                    if not first:
                        dve.wait_ge(s["yout"], n.times(1, -3))
                        dve.wait_ge(s["idxcopy"], n.times(1, -3 - 4))
                    dve.tensor_scalar(slot_row[0:CAP], ps_list[0:CAP, 2:3], dummy[0:CAP, 0:1], dummy[0:CAP, 1:2],
                                      ALU.mult, ALU.add).then_inc(s["slotrow"], 1)
                    dve.tensor_reduce(gate[0:CAP, n.r:n.r + 1], ps_list[0:CAP, 3:6], AX.X, ALU.add)
                    dve.wait_ge(s["slotrow"], n.times(1, 1 - 4))
                    dve.tensor_scalar(index[0:CAP, n.r:n.r + 1], slot_row[0:CAP], ps_list[0:CAP, 0:1],
                                      ps_list[0:CAP, 1:2], ALU.add, ALU.add).then_inc(s["index"], 1)
                if valid(1):
                    n = b.after(1)
                    if first_of_all(n):
                        for u in range(2):
                            for piece in range(PIECES):
                                matrix_tail(l, u, piece, unit_count(b.after(2), u, piece))
                    rows_tail(s["xhead"], n.times(1, 1), s["xtail"], n.r, CAP)
                    if first_of_all(n):
                        for piece in range(PIECES):
                            matrix_tail(l, 2, piece, unit_count(b.after(2), 2, piece))
                if valid(0) and not split_early(b):
                    slot, _ = weight_unit(b, 2)
                    for piece in range(PIECES):
                        matrix_tail(l, slot, piece, unit_count(b, 2, piece))
                if valid(1) and not split_early(n):
                    slot, _ = weight_unit(n, 0)
                    for piece in range(PIECES):
                        matrix_tail(l, slot, piece, unit_count(n, 0, piece))
                    slot, _ = weight_unit(n, 1)
                    matrix_tail(l, slot, 0, unit_count(n, 1, 0))
                if valid(0):
                    hidden(l, b, CAP)
                if valid(1) and not split_early(n):
                    matrix_tail(l, slot, 1, unit_count(n, 1, 1))

            def one_round(rnd):
                if not isinstance(rnd, int):
                    dve.tensor_scalar(slots, slots, float(CAP), None, ALU.add).then_inc(s["slots"], 1)
                    dve.wait_ge(s["slots"], rnd)
                run_steps(dve, rnd, body)
                dve.wait_ge(s["tail"], 3 * PIECES * (EXPERTS * (rnd + 1) + 1))
                dve.sem_inc(s_dve_waited, 1)

            run_rounds(dve, l, one_round)
            dve.sem_inc(s["split_over"], 1)

        def shared_tails(l, u):
            for piece in range(PIECES):
                matrix_tail(l, u, piece, PIECES * u + piece + 1)

        def pool_tile(t):
            dve.wait_ge(s_mix, t + 1)
            dve.wait_ge(s_pooled, min(t + 2, TILES))
            x = xn[:, t, :].rearrange("p (b n) -> p b n", b=2)
            for h in HALVES:
                last = dve.scalar_tensor_tensor(out=x[:, h], in0=x[:, h], scalar=ALPHA, in1=ps_y[:, h],
                                                op0=ALU.mult, op1=ALU.add)
            last.then_inc(s_mix_used, 1)
            dve.wait_ge(s_mix_used, t + 1)
            if t == 0:
                dve.wait_ge(s_par, 16 * 2)
            layer_norm(t)

        def last_norm(l):
            dve.wait_ge(s_par, 16 * (4 if l == 0 else 12))
            for t in range(TILES):
                dve.wait_ge(s_acc_in[l][t], 16)
                layer_norm(t)

        dve.wait_ge(s_pool_w, 16)
        dve.wait_ge(s_pool_scale, 16)
        for k in range(2):
            last = dve.tensor_tensor(pool_w[:, :, k, :], pool_w[:, :, k, :],
                                     par[:, 2, :].rearrange("p (g n) -> p g n", g=len(WINDOWS)), ALU.mult)
        last.then_inc(s_pool_scaled, 1)
        for t in range(TILES):
            dve.wait_ge(s_x[t], 16)
            pool_tile(t)
            if t == 1:
                router_tail(0)
            if t == 2:
                shared_tails(0, 0)
        shared_tails(0, 1)
        rows_tail(S[0]["xhead"], 1, S[0]["xtail"], 0, P)
        shared_tails(0, 2)
        dve.wait_ge(s_const, 32)

        def dense_tiles(l):
            for t in range(TILES - 2):
                hidden(l, Block(0, t), P)
                hidden_tail(l, Block(0, t), P)
                rows_tail(S[l]["xhead"], t + 2, S[l]["xtail"], t + 1, P)
                shared_tile(l, t)
                first_expert(l, t)
            rows_tail(S[l]["xhead"], TILES, S[l]["xtail"], TILES - 1, P)
            first_expert(l, 2)
            hidden(l, Block(0, TILES - 2), P)
            hidden_tail(l, Block(0, TILES - 2), P)

        def token_table(l):
            number = dummy[:, 1:2]
            for t in range(TILES):
                dve.memset(tab[:, t, :, 1], float(t * P))
            dve.memset(tab[:, :, :, 2], 1.0)
            dve.memset(tab[:, :, :, 0], 1.0)
            link(dve.tensor_scalar(most, number, -float(SEQ), None, ALU.add))
            link(dve.tensor_scalar(tab[:, :, :, 0], tab[:, :, :, 0], most, None, ALU.mult))

        token_table(0)
        dense_tiles(0)
        route(0)
        experts(0)

        def wqkv_tail(n):
            k = WQKV_ORDER[n]
            dve.wait_ge(s_qhead, n + 1)
            dve.tensor_tensor(wqkv[:, 1, k, :], wqkv_raw[:, k, :], wqkv[:, 0, k, :].bitcast(F32),
                              ALU.subtract).then_inc(s_qtail, 1)

        dve.wait_ge(s_par, 16 * 4)
        for t in range(TILES):
            if t == 0:
                for n in range(CHUNKS // 2):
                    wqkv_tail(n)
            dve.wait_ge(s_acc_in[0][t], 16)
            layer_norm(t)
            if t == 0:
                rows_tail(s_axhead, 1, s_axtail, 0, P)
                for n in range(CHUNKS // 2, CHUNKS):
                    wqkv_tail(n)
            elif t == 1:
                rows_tail(s_axhead, 2, s_axtail, 1, P)

        def rotate(x, t, heads, tmp):
            v = x.rearrange("p (h s j) -> p h s j", s=2, j=HEAD // 2)
            tm = tmp.rearrange("p (s h j) -> p s h j", s=2, h=heads)
            cos = rope[:, t, 0, :].unsqueeze(1).to_broadcast([P, heads, HEAD // 2])
            sin = rope[:, t, 1, :].unsqueeze(1).to_broadcast([P, heads, HEAD // 2])
            for k in HALVES:
                last = dve.tensor_tensor(tm[:, k], v[:, :, k, :], sin, ALU.mult)
            link(last)
            for k in HALVES:
                last = dve.tensor_tensor(v[:, :, k, :], v[:, :, k, :], cos, ALU.mult)
            link(last)
            dve.tensor_tensor(v[:, :, 0, :], v[:, :, 0, :], tm[:, 1], ALU.subtract)
            link(dve.tensor_tensor(v[:, :, 1, :], v[:, :, 1, :], tm[:, 0], ALU.add))

        def rotate_tile(t, tmp):
            rotate(q_nat[:, t, :], t, HEADS, tmp)
            rotate(k_nat[:, t, :], t, KV_HEADS, tmp[:, 0:KV])
            dve.sem_inc(s_roped, 1)

        dve.wait_ge(s_par, 16 * 8)
        dve.tensor_scalar(negsink, negsink, -1.0, None, ALU.mult)
        for t in range(TILES):
            if 0 < t < TILES - 1:
                rows_tail(s_axhead, t + 2, s_axtail, t + 1, P)
            dve.wait_ge(s_qkv, t + 1)
            banks = qkv_ps(t)
            for h in HALVES:
                cols = slice(h * BANK, (h + 1) * BANK)
                dve.tensor_tensor(q_nat[:, t, cols], banks[:, h, :], bqkv[:, cols], ALU.add)
            dve.tensor_tensor(k_nat[:, t, :], banks[:, 2, 0:KV], bqkv[:, D:D + KV], ALU.add)
            dve.tensor_tensor(v_nat[:, t, :], banks[:, 2, KV:2 * KV], bqkv[:, D + KV:QKV], ALU.add).then_inc(s_qkv_used, 1)
            dve.wait_ge(s_qkv_used, t + 1)
            if t < TILES - 1:
                rotate_tile(t, score[0].rearrange("p a b -> p (a b)"))

        def wo_tail(k):
            dve.wait_ge(s_wohead, k + 1)
            dve.tensor_tensor(wo[:, 1, k, :], wo_raw[:, k % 3, :], wo[:, 0, k, :].bitcast(F32),
                              ALU.subtract).then_inc(s_wotail, 1)

        def softmax(u):
            n, g = divmod(u, KV_HEADS)
            keys = slice(0 if n else P, 2 * P)
            width = 2 * P if n else P
            dve.wait_ge(s_score, u + 1)
            if u >= 2:
                dve.wait_ge(s_pT, u - 1)
            sc = ps_xT.rearrange("p b (h k) -> p (b h) k", h=2)
            mask = band[:, keys].unsqueeze(1).to_broadcast([P, PER_KV, width])
            buf = score[u % 2][:, :, keys]
            dve.scalar_tensor_tensor(out=buf, in0=sc[:, :, keys], scalar=HEAD ** -0.5, in1=mask,
                                     op0=ALU.mult, op1=ALU.add).then_inc(s_masked, 1)
            dve.wait_ge(s_masked, u + 1)
            link(dve.tensor_reduce(top, buf, AX.X, ALU.max))
            sink = negsink[:, g * PER_KV:(g + 1) * PER_KV]
            link(dve.scalar_tensor_tensor(out=negtop[:, u % 2], in0=top, scalar=-1.0, in1=sink,
                                          op0=ALU.mult, op1=ALU.min))
            dve.tensor_tensor(sink_arg[:, u % 2], negtop[:, u % 2], sink, ALU.subtract).then_inc(s_negtop, 1)

        def previous_out(u):
            if u // KV_HEADS:
                dve.wait_ge(s_pT, u + 1)
                dve.wait_ge(s_pv, u)
                dve.tensor_copy(pT[:, 0], ps_log.rearrange("p (h t) -> p h t", h=PER_KV)).then_inc(s_pT_prev, 1)

        def inverse_total(u):
            dve.wait_ge(s_exp, u + 1)
            link(dve.tensor_tensor(total[:, u % 2], total[:, u % 2], sink_exp[:, u % 2], ALU.add))
            link(dve.reciprocal(inverse[:, u % 2], total[:, u % 2]))

        def divide(u):
            n, g = divmod(u, KV_HEADS)
            dve.wait_ge(s_pv, u + 1)
            dve.tensor_tensor(q_nat[:, n, g * 256:(g + 1) * 256].rearrange("p (h j) -> p h j", h=PER_KV),
                              ps_list[:, 0:256].rearrange("p (h j) -> p h j", h=PER_KV),
                              inverse[:, u % 2].unsqueeze(2).to_broadcast([P, PER_KV, HEAD]),
                              ALU.mult).then_inc(s_o, 1)

        def projection_out(n):
            dve.wait_ge(s_wo, n + 1)
            x = xn[:, n, :].rearrange("p (b n) -> p b n", b=2)
            for h in HALVES:
                last = dve.scalar_tensor_tensor(out=x[:, h], in0=x[:, h], scalar=ALPHA, in1=ps_y[:, h],
                                                op0=ALU.mult, op1=ALU.add)
            last.then_inc(s_wo_used, 1)

        dve.wait_ge(s_band, 16)
        dve.tensor_copy(band, band_raw).then_inc(s_band_copied, 1)
        dve.wait_ge(s_band_copied, 1)
        for i in range(UNITS + 7):
            if projected(i - 3) is not None:
                projection_out(projected(i - 3))
            if 2 <= i < UNITS + 2:
                previous_out(i - 2)
                inverse_total(i - 2)
            if projected(i) is not None:
                rows_tail(s_axhead, TILES + projected(i) + 1, s_axtail, projected(i), P, ps_y)
            if i < UNITS:
                softmax(i)
            if i == 1:
                rotate_tile(TILES - 1, par[:, 0, :])
            if 2 <= i < UNITS + 2:
                divide(i - 2)
            if projected(i - 3) is not None:
                n = projected(i - 3)
                dve.wait_ge(s_wo_used, n + 1)
                link(dve.tensor_tensor(xn[:, n, :], xn[:, n, :], bo, ALU.add))
                norm_stats(n)
            if projected(i - 4) is not None:
                if projected(i - 4) == 0:
                    dve.wait_ge(s_par, 16 * 10)
                norm_apply(projected(i - 4))
            if i < 4:
                wo_tail(2 * i)
                wo_tail(2 * i + 1)
            if 9 <= i < 9 + 2 * PIECES:
                matrix_tail(1, (i - 9) // PIECES, (i - 9) % PIECES, i - 8)
            if i == UNITS + 2:
                rows_tail(S[1]["xhead"], 1, S[1]["xtail"], 0, P)
                token_table(1)
                router_tail(1)
        shared_tails(1, 2)
        dense_tiles(1)
        route(1)
        experts(1)
        last_norm(1)

    @block.tensor
    def _(pe):
        def product(out_ap, stationary, moving, first, last):
            for k, (a, b) in enumerate(PASSES):
                mm = pe.matmul(out_ap, stationary(a), moving(b), start=first and k == 0,
                               stop=last and k == len(PASSES) - 1)
            return mm

        def transpose_rows(src, m, banks=ps_xT):
            for k in range(CHUNKS):
                mm = pe.transpose(in_chunks(banks, m)[:, k // 4, k % 4, :], src[0:m, k * P:(k + 1) * P], ident[0:m, 0:m])
            return mm

        def first_product(b, m, w1_slot):
            w = split[:, 2 * w1_slot * UNIT:2 * (w1_slot + 2) * UNIT].rearrange(
                "p (m s c n) -> p s c m n", m=2, s=2, c=CHUNKS)
            for k in range(CHUNKS):
                mm = product(ps_h[0:m].rearrange("p (m n) -> p m n", m=2), lambda a: xT[:, b % 2, a, k, 0:m],
                             lambda a: w[:, a, k], k == 0, k == CHUNKS - 1)
            return mm

        def transpose_hidden(m):
            for j in range(FC):
                mm = pe.transpose(ps_hT[:, j * m:(j + 1) * m], h_sb[0:m, j, :], ident[0:m, 0:m])
            return mm

        def second_product(m, slot):
            w = split_slot(slot).rearrange("p s (j n) -> p s j n", j=FC)
            for h in HALVES:
                for j in range(FC):
                    mm = product(ps_y[0:m, h, :], lambda a: hT[:, a, j, 0:m],
                                 lambda a: w[:, a, j, h * BANK:(h + 1) * BANK], j == 0, j == FC - 1)
            return mm

        def rows_transposed(l, t):
            pe.wait_ge(S[l]["xp"], t + 1)
            if t:
                pe.wait_ge(S[l]["xtail"], t)
            transpose_rows(xp, P).then_inc(S[l]["xTready"], 1)

        def dense(l):
            s = S[l]

            def router(t):
                pe.wait_ge(s["xtail"], t + 1)
                pe.wait_ge(s_rw_tail, l + 1)
                for k in range(CHUNKS):
                    mm = product(ps_log[:, t * EXPERTS:(t + 1) * EXPERTS], lambda a: xT[:, t % 2, a, k, :],
                                 lambda a: rw[:, a, k, :], k == 0, k == CHUNKS - 1)
                mm.then_inc(s["logits"], 1)

            def first(t):
                pe.wait_ge(s["xtail"], t + 1)
                pe.wait_ge(s["tail"], 2 * PIECES)
                first_product(t, P, 0).then_inc(s["m1"], 1)

            def hidden_transposed(t):
                pe.wait_ge(s["hidden"], t + 1)
                transpose_hidden(P).then_inc(s["hTready"], 1)

            def second(t):
                pe.wait_ge(s["htail"], t + 1)
                pe.wait_ge(s["tail"], 3 * PIECES)
                if t:
                    pe.wait_ge(s["yout"], t)
                second_product(P, 2).then_inc(s["m2"], 1)

            for t in range(TILES - 2):
                first(t)
                router(t)
                hidden_transposed(t)
                rows_transposed(l, t + 1)
                second(t)
            router(TILES - 2)
            rows_transposed(l, TILES - 1)
            first(TILES - 2)
            router(TILES - 1)
            hidden_transposed(TILES - 2)
            second(TILES - 2)
            first(TILES - 1)
            hidden_transposed(TILES - 1)
            second(TILES - 1)

        def rank(l):
            s = S[l]
            pe.wait_ge(s_moe_const, 32 * (l + 1))
            pe.wait_ge(s["order"], 2)
            pe.wait_ge(s["chosen"], 1)
            for t in range(TILES):
                for k in range(t + 1):
                    pe.matmul(ps_list[:, t * EXPERTS:(t + 1) * EXPERTS], order[:, 0 if k == t else 1, :],
                              chosen[:, k, :], start=(k == 0), stop=(k == t))
            for k in range(TILES):
                mm = pe.matmul(ps_list[:, 256:256 + EXPERTS], order[:, 1, :], chosen[:, k, :],
                               start=(k == 0), stop=(k == TILES - 1))
            mm.then_inc(s["ranked"], 1)

        def experts(l):
            s = S[l]

            def body(b, valid):
                if valid(-1):
                    n = b.after(-1)
                    pe.wait_ge(s["hidden"], n.times(1, 1))
                    pe.wait_ge(s["htail"], n.times(1))
                    transpose_hidden(CAP).then_inc(s["hTready"], 1)
                if valid(2):
                    n = b.after(2)
                    pe.wait_ge(s["oh"], n.times(1, 1 - 4))
                    if not (isinstance(n.q, int) and n.q == 1 and n.r == 0):
                        pe.wait_ge(s["index"], n.times(1, -4))
                    for t in range(TILES):
                        mm = pe.matmul(ps_list[0:CAP, 0:TAB], oh[:, n.r % 2, t, :],
                                       tab[:, t, bass.ds(n.expert, 1), :].rearrange("p e k -> p (e k)"),
                                       start=(t == 0), stop=(t == TILES - 1))
                    mm.then_inc(s["listed"], 1)
                if valid(1):
                    n = b.after(1)
                    pe.wait_ge(s_xg[l][n.r % 2], 16 * (2 * (n.q - 1) + n.r // 2 + 1))
                    pe.wait_ge(s["xtail"], n.times(1))
                    transpose_rows(xg[n.r % 2], CAP).then_inc(s["xTready"], 1)
                if valid(0):
                    pe.wait_ge(s["xtail"], b.times(1, 1))
                    pe.wait_ge(s["tail"], b.times(3 * PIECES, PIECES * (-12 + 3 + 2)))
                    slot, _ = weight_unit(b, 0)
                    first_product(b.r, CAP, slot).then_inc(s["m1"], 1)
                if valid(-1):
                    n = b.after(-1)
                    pe.wait_ge(s["htail"], n.times(1, 1))
                    pe.wait_ge(s["tail"], n.times(3 * PIECES, PIECES * (-12 + 3 + 3)))
                    pe.wait_ge(s["yout"], n.times(1))
                    slot, _ = weight_unit(n, 2)
                    second_product(CAP, slot).then_inc(s["m2"], 1)

            def one_round(rnd):
                run_steps(pe, rnd, body)
                pe.wait_ge(s["m2"], EXPERTS * (rnd + 1) + 4)

            run_rounds(pe, l, one_round)
            pe.sem_inc(s["pe_idle"], 1)

        pe.wait_ge(s_pool_band, 16)

        def pool_rows(t):
            pe.wait_ge(s_x[t], 16)
            if t:
                pe.wait_ge(s_pooled_sb, t)
            for k in range(CHUNKS):
                g = k * P // GROUP_CH
                dst = ps_xT[:, k // 4, (k % 4) * P:(k % 4 + 1) * P]
                mm = pe.matmul(dst, xn[:, t, k * P:(k + 1) * P], pool_band[:, g, min(t, 1), :],
                               start=True, stop=(t == 0))
                if t:
                    mm = pe.matmul(dst, xn[:, t - 1, k * P:(k + 1) * P], pool_band[:, g, 2, :],
                                   start=False, stop=True)
            mm.then_inc(s_pooled, 1)

        def mix(t):
            pe.wait_ge(s_pooled_sb, t + 1)
            pe.wait_ge(s_pool_scaled, 1)
            if t:
                pe.wait_ge(s_mix_used, t)
            for g in range(len(WINDOWS)):
                dst = ps_y[:, g // 2, (g % 2) * GROUP_CH:(g % 2 + 1) * GROUP_CH]
                for k in range(2):
                    mm = pe.matmul(dst, pooled[t % 2][:, 2 * g + k, :], pool_w[:, g, k, :], start=(k == 0), stop=(k == 1))
            mm.then_inc(s_mix, 1)

        for t in range(TILES + 1):
            if t < TILES:
                pool_rows(t)
            if t:
                mix(t - 1)
        pe.wait_ge(s_const, 32)
        rows_transposed(0, 0)
        dense(0)
        rank(0)
        experts(0)

        def trunk_transposed(t):
            pe.wait_ge(s_norm, TILES + t + 1)
            if t:
                pe.wait_ge(s_axtail, t)
            transpose_rows(xn[:, t, :], P).then_inc(s_axT, 1)

        trunk_transposed(0)
        for t in range(TILES):
            pe.wait_ge(s_axtail, t + 1)
            if t >= 2:
                pe.wait_ge(s_qkv_used, t - 1)
            for b in range(3):
                if b == 2 and t + 1 < TILES:
                    trunk_transposed(t + 1)
                for n, k in enumerate(WQKV_ORDER):
                    if t == 0 and b == 0:
                        pe.wait_ge(s_qtail, n + 1)
                    mm = product(qkv_ps(t)[:, b, :], lambda a: xT[:, t % 2, a, k, :],
                                 lambda a: wqkv[:, a, k, b * BANK:(b + 1) * BANK], n == 0, n == CHUNKS - 1)
            mm.then_inc(s_qkv, 1)

        def queries_transposed(u):
            n, g = divmod(u, KV_HEADS)
            pe.wait_ge(s_qkv_used, TILES)
            pe.wait_ge(s_roped, n + 1)
            if u:
                pe.wait_ge(s_qT_sb, u)
            for h in range(PER_KV):
                mm = pe.transpose(ps_hT[0:HEAD, h * P:(h + 1) * P],
                                  q_nat[:, n, (g * PER_KV + h) * HEAD:(g * PER_KV + h + 1) * HEAD], ident[:, :])
            mm.then_inc(s_qT, 1)
            if g == 0:
                if u:
                    pe.wait_ge(s_o, u - 2)
                for h in range(KV_HEADS):
                    mm = pe.transpose(ps_list[0:HEAD, h * P:(h + 1) * P], k_nat[:, n, h * HEAD:(h + 1) * HEAD],
                                      ident[:, :])
                mm.then_inc(s_kT, 1)

        def scores(u):
            n, g = divmod(u, KV_HEADS)
            pe.wait_ge(s_qT_sb, u + 1)
            pe.wait_ge(s_kT_sb, n + 1)
            if u:
                pe.wait_ge(s_masked, u)
            for h in range(PER_KV):
                for b in ((1, 0) if n else (1,)):
                    dst = ps_xT[:, h // 2, (h % 2) * 2 * P + b * P:(h % 2) * 2 * P + (b + 1) * P]
                    mm = pe.matmul(dst, qT[u % 2][0:HEAD, h, :], kT[0:HEAD, g, (n - 1 + b) % 2, :], start=True, stop=True)
            mm.then_inc(s_score, 1)

        def weights_transposed(u):
            n = u // KV_HEADS
            pe.wait_ge(s_exp, u + 1)
            if u:
                pe.wait_ge(s_pT_cur, u)
                if prev_count(u):
                    pe.wait_ge(s_pT_prev, prev_count(u))
            for b in ((1, 0) if n else (1,)):
                for h in range(PER_KV):
                    dst = (ps_h if b else ps_log)[:, h * P:(h + 1) * P]
                    mm = pe.transpose(dst, score[u % 2][:, h, b * P:(b + 1) * P], ident[:, :])
            mm.then_inc(s_pT, 1)

        def values(u):
            n, g = divmod(u, KV_HEADS)
            pe.wait_ge(s_pT_cur, u + 1)
            if n:
                pe.wait_ge(s_pT_prev, prev_count(u + 1))
            if u:
                pe.wait_ge(s_o, u)
            blocks = (1, 0) if n else (1,)
            for h in range(PER_KV):
                for b in blocks:
                    mm = pe.matmul(ps_list[:, h * HEAD:(h + 1) * HEAD], pT[:, b, h, :],
                                   v_nat[:, n - 1 + b, g * HEAD:(g + 1) * HEAD],
                                   start=(b == 1), stop=(b == blocks[-1]))
            mm.then_inc(s_pv, 1)

        pairs = [(b, k) for b in HALVES for k in range(CHUNKS)]
        thirds = (pairs[:5], pairs[5:10], pairs[10:])

        def project(n, third):
            if third == 0:
                pe.wait_ge(s_axtail, TILES + n + 1)
                pe.wait_ge(s_wotail, CHUNKS)
            for b, k in thirds[third]:
                mm = product(ps_y[:, b, :], lambda a: xT[:, n % 2, a, k, :],
                             lambda a: wo[:, a, k, b * BANK:(b + 1) * BANK], k == 0, k == CHUNKS - 1)
            if third == 2:
                mm.then_inc(s_wo, 1)

        for i in range(UNITS + 5):
            n = projected(i)
            if n is not None:
                pe.wait_ge(s_o, KV_HEADS * (n + 1))
                if n:
                    pe.wait_ge(s_wo_used, n)
                transpose_rows(q_nat[:, n, :], P, ps_y).then_inc(s_axT, 1)
            if i < UNITS:
                queries_transposed(i)
            if 2 <= i < UNITS + 2:
                weights_transposed(i - 2)
            if i < UNITS:
                scores(i)
            if 2 <= i < UNITS + 2:
                values(i - 2)
            if i == UNITS + 2:
                rows_transposed(1, 0)
            for third in range(3):
                if projected(i - third) is not None:
                    project(projected(i - third), third)
        dense(1)
        rank(1)
        experts(1)

    ctx.close()


def kernel(**inputs):
    import concourse.bacc as bacc
    from concourse.bass_utils import run_bass_kernel_spmd

    names = ("x", "ln_gain", "ln_bias", "pool_w", "pool_scale", "attn_wqkv", "attn_bqkv", "attn_sinks", "attn_wo",
             "attn_bo", "router_w", "router_bias", "expert_w1", "expert_w3", "expert_w2", "shared_w1", "shared_w3",
             "shared_w2")
    nc = bacc.Bacc("TRN2", target_bir_lowering=False, num_devices=1)
    arrays, ins, consts = {}, {}, {}
    for name in names:
        a = np.ascontiguousarray(inputs[name])
        arrays[f"in_{name}"] = a
        ins[name] = nc.dram_tensor(f"in_{name}", a.shape, mybir.dt.from_np(a.dtype), kind="ExternalInput").ap()
    for name, a in shape_constants().items():
        a = np.ascontiguousarray(a)
        arrays[f"const_{name}"] = a
        consts[name] = nc.dram_tensor(f"const_{name}", a.shape, mybir.dt.from_np(a.dtype), kind="ExternalInput").ap()
    out = nc.dram_tensor("out", (1, SEQ, D), F32, kind="ExternalOutput").ap()
    build(nc, ins, consts, out)
    r = run_bass_kernel_spmd(nc, [arrays], core_ids=[0])
    return r.results[0]["out"]
```
